# Optimizing a Trainium2 kernel written in Bass

```python
import math
import jax, jax.numpy as jnp
from jax import lax
import numpy as np

D_MODEL = 1024
BATCH = 1
SEQ = 2048
DEPTH = 2

M_HEADS = 4
M_DHV = D_MODEL // M_HEADS
M_DHQK = M_DHV // 2
M_QK = M_HEADS * M_DHQK
M_V = M_HEADS * M_DHV
M_PROJ = 2 * M_QK + 2 * M_V + 2 * M_HEADS
CHUNK = 64
CONV_W = 3
N_MLSTM_LAYERS = (DEPTH + 1) // 2
N_CONV_LAYERS = DEPTH // 2
N_EXPERTS = 16
N_GROUPS = 4
EXPERTS_PER_GROUP = N_EXPERTS // N_GROUPS
TOP_K = 2
D_EXPERT = D_MODEL // 2
EPS = 1e-6

kernel_name = "hybrid_mlstm_shortconv_grouped_moe_adaln"

def _rmsnorm(x, g):
    x32 = x.astype(jnp.float32)
    y = x32 * lax.rsqrt(jnp.mean(x32 * x32, axis=-1, keepdims=True) + EPS)
    return (y * g.astype(jnp.float32)).astype(x.dtype)

def _modulate(h, shift, scale):
    return h * (1 + scale[:, None, :]) + shift[:, None, :]

def _mlstm_mixer(u, w_in, b_gates, norm_g, w_out):
    Bn, S, _ = u.shape
    NC = S // CHUNK
    proj = (u @ w_in).astype(jnp.float32)
    q, k, v, og, gi, gf = jnp.split(
        proj, [M_QK, 2 * M_QK, 2 * M_QK + M_V, 2 * M_QK + 2 * M_V, 2 * M_QK + 2 * M_V + M_HEADS], axis=-1)
    bg = b_gates.astype(jnp.float32)
    ig = gi + bg[:M_HEADS]
    lf = jax.nn.log_sigmoid(gf + bg[M_HEADS:])
    q = q * (M_DHQK ** -0.5)

    def chunks(t, d):
        return t.reshape(Bn, NC, CHUNK, M_HEADS, d).transpose(1, 0, 3, 2, 4)

    def gchunks(t):
        return t.reshape(Bn, NC, CHUNK, M_HEADS).transpose(1, 0, 3, 2)

    qc, kc, vc = chunks(q, M_DHQK), chunks(k, M_DHQK), chunks(v, M_DHV)
    igc, lfc = gchunks(ig), gchunks(lf)
    causal = jnp.tril(jnp.ones((CHUNK, CHUNK), dtype=bool))

    def step(carry, xs):
        C, n, m = carry
        qb, kb, vb, ib, fb = xs
        b = jnp.cumsum(fb, axis=-1)
        logD = jnp.where(causal, b[..., :, None] - b[..., None, :] + ib[..., None, :], -jnp.inf)
        inter = b + m[..., None]
        m_t = jnp.maximum(inter, jnp.max(logD, axis=-1))
        Dm = jnp.exp(logD - m_t[..., None])
        w_inter = jnp.exp(inter - m_t)
        s = jnp.einsum('bhtk,bhsk->bhts', qb, kb) * Dm
        num = w_inter[..., None] * jnp.einsum('bhtk,bhkv->bhtv', qb, C) + jnp.einsum('bhts,bhsv->bhtv', s, vb)
        den = w_inter * jnp.einsum('bhtk,bhk->bht', qb, n) + jnp.sum(s, axis=-1)
        h = num / jnp.maximum(jnp.abs(den), jnp.exp(-m_t))[..., None]
        bL = b[..., -1]
        a = bL[..., None] - b + ib
        m_new = jnp.maximum(bL + m, jnp.max(a, axis=-1))
        wk = jnp.exp(a - m_new[..., None])
        decay = jnp.exp(bL + m - m_new)
        C_new = decay[..., None, None] * C + jnp.einsum('bhs,bhsk,bhsv->bhkv', wk, kb, vb)
        n_new = decay[..., None] * n + jnp.einsum('bhs,bhsk->bhk', wk, kb)
        return (C_new, n_new, m_new), h

    init = (jnp.zeros((Bn, M_HEADS, M_DHQK, M_DHV), jnp.float32),
            jnp.zeros((Bn, M_HEADS, M_DHQK), jnp.float32),
            jnp.zeros((Bn, M_HEADS), jnp.float32))
    _, hc = lax.scan(step, init, (qc, kc, vc, igc, lfc))
    h = hc.transpose(1, 0, 3, 2, 4).reshape(Bn, S, M_HEADS, M_DHV)
    h = h * lax.rsqrt(jnp.mean(h * h, axis=-1, keepdims=True) + EPS)
    h = h.reshape(Bn, S, M_V) * norm_g.astype(jnp.float32) * jax.nn.sigmoid(og)
    return h.astype(u.dtype) @ w_out

def _shortconv_mixer(u, w_in, conv_w, conv_b, w_out):
    bg, cg, hx = jnp.split(u @ w_in, 3, axis=-1)
    z = cg * hx
    zc = lax.conv_general_dilated(
        z, conv_w[:, None, :].astype(z.dtype), window_strides=(1,), padding=[(CONV_W - 1, 0)],
        dimension_numbers=('NWC', 'WIO', 'NWC'), feature_group_count=z.shape[-1]) + conv_b
    return (bg * zc) @ w_out

def _moe(h, w_router, b_router, w_gate, w_up, w_down):
    Bn, S, D = h.shape
    T = Bn * S
    ht = h.reshape(T, D)
    probs = jax.nn.softmax((ht @ w_router).astype(jnp.float32), axis=-1)
    sel = probs + b_router.astype(jnp.float32)
    grp_score = lax.top_k(sel.reshape(T, N_GROUPS, EXPERTS_PER_GROUP), 2)[0].sum(-1)
    best = jnp.argmax(grp_score, axis=-1)
    in_grp = (jnp.arange(N_EXPERTS) // EXPERTS_PER_GROUP)[None, :] == best[:, None]
    _, idx = lax.top_k(jnp.where(in_grp, sel, -jnp.inf), TOP_K)
    wts = jnp.take_along_axis(probs, idx, axis=-1)
    wts = wts / jnp.sum(wts, axis=-1, keepdims=True)
    flat_e = idx.reshape(-1)
    flat_t = jnp.repeat(jnp.arange(T), TOP_K)
    order = jnp.argsort(flat_e)
    tok = flat_t[order]
    sizes = jnp.bincount(flat_e, length=N_EXPERTS).astype(jnp.int32)
    xs = ht[tok]
    a = jax.nn.silu(lax.ragged_dot(xs, w_gate, sizes)) * lax.ragged_dot(xs, w_up, sizes)
    out = lax.ragged_dot(a, w_down, sizes) * wts.reshape(-1)[order][:, None].astype(h.dtype)
    y = jax.ops.segment_sum(out, tok, num_segments=T)
    return y.reshape(Bn, S, D)

def setup_inputs(seed: int = 0) -> dict:
    key = jax.random.key(seed)
    ks = jax.random.split(key, 24)
    D = D_MODEL
    f32 = jnp.float32
    nrm = lambda k, shape, s: jax.random.normal(k, shape, f32) * s
    b_gates = jnp.concatenate([
        nrm(ks[7], (N_MLSTM_LAYERS, M_HEADS), 0.1),
        3.0 + nrm(ks[8], (N_MLSTM_LAYERS, M_HEADS), 0.5)], axis=-1)
    return {
        "x": nrm(ks[0], (BATCH, SEQ, D), 1.0),
        "c": nrm(ks[1], (BATCH, D), 1.0),
        "norm1_g": 1.0 + nrm(ks[2], (DEPTH, D), 0.02),
        "norm2_g": 1.0 + nrm(ks[3], (DEPTH, D), 0.02),
        "w_ada": nrm(ks[4], (DEPTH, D, 6 * D), 0.5 * D ** -0.5),
        "b_ada": nrm(ks[5], (DEPTH, 6 * D), 0.02),
        "m_w_in": nrm(ks[6], (N_MLSTM_LAYERS, D, M_PROJ), D ** -0.5),
        "m_b_gates": b_gates,
        "m_norm_g": 1.0 + nrm(ks[9], (N_MLSTM_LAYERS, M_V), 0.02),
        "m_w_out": nrm(ks[10], (N_MLSTM_LAYERS, M_V, D), M_V ** -0.5),
        "c_w_in": nrm(ks[11], (N_CONV_LAYERS, D, 3 * D), D ** -0.5),
        "c_conv_w": nrm(ks[12], (N_CONV_LAYERS, CONV_W, D), CONV_W ** -0.5),
        "c_conv_b": nrm(ks[13], (N_CONV_LAYERS, D), 0.02),
        "c_w_out": nrm(ks[14], (N_CONV_LAYERS, D, D), D ** -0.5),
        "w_router": nrm(ks[15], (D, N_EXPERTS), D ** -0.5),
        "b_router": nrm(ks[16], (N_EXPERTS,), 0.01),
        "e_w_gate": nrm(ks[17], (DEPTH, N_EXPERTS, D, D_EXPERT), D ** -0.5),
        "e_w_up": nrm(ks[18], (DEPTH, N_EXPERTS, D, D_EXPERT), D ** -0.5),
        "e_w_down": nrm(ks[19], (DEPTH, N_EXPERTS, D_EXPERT, D), D_EXPERT ** -0.5),
        "final_g": 1.0 + nrm(ks[20], (D,), 0.02),
    }

def reference(x, c, norm1_g, norm2_g, w_ada, b_ada, m_w_in, m_b_gates, m_norm_g, m_w_out,
              c_w_in, c_conv_w, c_conv_b, c_w_out, w_router, b_router,
              e_w_gate, e_w_up, e_w_down, final_g):
    cond = jax.nn.silu(c)
    for i in range(DEPTH):
        mod = cond @ w_ada[i] + b_ada[i]
        sh1, sc1, g1, sh2, sc2, g2 = jnp.split(mod, 6, axis=-1)
        u = _modulate(_rmsnorm(x, norm1_g[i]), sh1, sc1)
        j = i // 2
        if i % 2 == 0:
            mix = _mlstm_mixer(u, m_w_in[j], m_b_gates[j], m_norm_g[j], m_w_out[j])
        else:
            mix = _shortconv_mixer(u, c_w_in[j], c_conv_w[j], c_conv_b[j], c_w_out[j])
        x = x + g1[:, None, :] * mix
        u = _modulate(_rmsnorm(x, norm2_g[i]), sh2, sc2)
        x = x + g2[:, None, :] * _moe(u, w_router, b_router, e_w_gate[i], e_w_up[i], e_w_down[i])
    return _rmsnorm(x, final_g)


_drawn_inputs = setup_inputs


def setup_inputs(seed=0):
    import zlib

    import numpy as np

    out = dict(_drawn_inputs(seed))
    spreads = {}
    factors = {'m_norm_g': 3.358, 'c_conv_b': 4.148, 'final_g': 2.956}
    for name, (base, spread) in spreads.items():
        noise = np.random.default_rng([zlib.crc32(name.encode()), seed]).standard_normal(out[name].shape)
        drawn = base * np.exp(spread * noise) if base else spread * noise
        out[name] = __import__('jax').numpy.asarray(drawn.astype(out[name].dtype))
    for name, factor in factors.items():
        out[name] = (out[name] * factor).astype(out[name].dtype)
    return out
```

```python
import concourse.bass as bass
from concourse import mybir
from contextlib import ExitStack

F32 = mybir.dt.float32
F32R = mybir.dt.float32r
I32 = mybir.dt.int32
ACT = mybir.ActivationFunctionType
ALU = mybir.AluOpType
AX = mybir.AxisListType

P = 128
D = 1024
T = 2048
KT = D // P
NT = T // P
HALF = 512
NBLK = T // HALF
HEADS = 4
DQK = 128
DV = 256
NCOL = 3 * D
NCHUNK = NCOL // P
E = 16
GROUPS = 4
PER_G = E // GROUPS
DE = 512
FT = DE // P
MAX_TILES = 48
EPS = 1e-6
BIG = 1e30
RING = 2


class Phase:

    def __init__(self, nc, name):
        self.nc, self.name, self.stack, self.sems = nc, name, ExitStack(), []

    def __enter__(self):
        self.stack.__enter__()
        return self

    def __exit__(self, *a):
        self.nc.clear_and_free_semaphores(self.sems)
        self.nc.all_engine_barrier()
        return self.stack.__exit__(*a)

    def sb(self, name, shape, dt=F32):
        return self.stack.enter_context(self.nc.sbuf_tensor(f"{self.name}_{name}", shape, dt))

    def ps(self, name, shape):
        return self.stack.enter_context(self.nc.psum_tensor(f"{self.name}_{name}", shape, F32))

    def sem(self, name):
        self.sems.append(self.nc.alloc_semaphore(f"{self.name}_{name}"))
        return self.sems[-1]

    def block(self):
        return self.nc.Block()


def split_mm(pe, out, lhs, rhs, start, stop):
    pe.matmul(out, lhs[0], rhs[0], start=start, stop=False)
    pe.matmul(out, lhs[0], rhs[1], start=False, stop=False)
    return pe.matmul(out, lhs[1], rhs[0], start=False, stop=stop)


def stand(eng, passed):
    eng.sem_inc(passed, 1)


def cols(ap):
    return ap.rearrange("(k p) -> p k", p=P)


def rowcast(ap):
    return ap.to_broadcast([P, ap.shape[1]])


def adaln(nc, c, w_ada, b_ada, mod_rows, ident):
    with Phase(nc, "ada") as ph:
        ccol = ph.sb("ccol", [P, KT])
        sig = ph.sb("sig", [P, KT])
        cond = ph.sb("cond", [P, KT])
        ones = ph.sb("ones", [P, 1])
        w = ph.sb("w", [P, RING, KT, D])
        bias = ph.sb("bias", [1, RING, D])
        acc = ph.sb("acc", [P, RING, D])
        row = ph.sb("row", [1, RING, D])
        psum = ph.ps("psum", [P, RING, D])
        c_in = ph.sem("c_in")
        w_in = [ph.sem(f"w_in{s}") for s in range(RING)]
        sig_ready = ph.sem("sig_ready")
        cond_ready = ph.sem("cond_ready")
        ones_ready = ph.sem("ones_ready")
        mac = ph.sem("mac")
        w_used = ph.sem("w_used")
        acc_ready = ph.sem("acc_ready")
        sum_ready = ph.sem("sum_ready")
        row_ready = ph.sem("row_ready")
        row_out = [ph.sem(f"row_out{s}") for s in range(RING)]
        id0 = ph.sem("id0")
        GR = 6

        with ph.block() as block:
            @block.sync
            def _(sp):
                with nc.allow_non_contiguous_dma(reason="4 KB vector laid over the partitions"):
                    sp.dma_start(ccol[:, :], cols(c[0, :])).then_inc(c_in, 16)
                for layer in range(2):
                    with sp.Fori(0, GR // RING) as i:
                        for s in range(RING):
                            sp.wait_ge(w_used, RING * i + (layer * GR + s + 1))
                            src = w_ada[layer, :, bass.ds((RING * i + s) * D, D)]
                            sp.dma_start(w[:, s, :, :], src.rearrange("(k p) n -> p k n", p=P)).then_inc(w_in[s], 16)
                            sp.dma_start(bias[0:1, s, :], b_ada[layer:layer + 1, bass.ds((RING * i + s) * D, D)]).then_inc(w_in[s], 16)

            @block.gpsimd
            def _(pool):
                pool.memset(ones[:, :], 1.0).then_inc(ones_ready, 1)
                pool.memset(ident[:, :], 0.0).then_inc(id0, 1)
                pool.wait_ge(id0, 1)
                pool.affine_select(out=ident[:, :], in_=ident[:, :], compare_op=ALU.not_equal, fill=1.0,
                                   base=0, pattern=[[-1, P]], channel_multiplier=1).then_inc(id0, 1)
                pool.wait_ge(id0, 2)

            @block.scalar
            def _(act):
                act.wait_ge(c_in, 16)
                act.activation(sig[:, :], ccol[:, :], ACT.Sigmoid).then_inc(sig_ready, 1)
                for s in range(RING):
                    act.sem_inc(row_out[s], 16)
                for layer in range(2):
                    with act.Fori(0, GR // RING) as i:
                        for s in range(RING):
                            act.wait_ge(row_ready, RING * i + (layer * GR + s + 1))
                            act.dma_start(mod_rows[layer, bass.ds(RING * i + s, 1), :], row[0:1, s, :]).then_inc(row_out[s], 16)
                for s in range(RING):
                    act.wait_ge(row_out[s], 16 * (GR + 1))

            @block.vector
            def _(dve):
                dve.sem_inc(w_used, RING)
                dve.wait_ge(sig_ready, 1)
                dve.tensor_tensor(cond[:, :], ccol[:, :], sig[:, :], ALU.mult).then_inc(cond_ready, 1)
                dve.wait_ge(cond_ready, 1)
                for layer in range(2):
                    with dve.Fori(0, GR // RING) as i:
                        for s in range(RING):
                            dve.wait_ge(w_in[s], 32 * i + 32 * (layer * (GR // RING) + 1))
                            for k in range(KT):
                                if k == 0:
                                    ins = dve.tensor_scalar(acc[:, s, :], w[:, s, k, :], cond[:, k:k + 1], None, ALU.mult)
                                else:
                                    dve.wait_ge(mac, (KT - 1) * (RING * i) + (KT - 1) * (layer * GR + s) + k)
                                    ins = dve.scalar_tensor_tensor(out=acc[:, s, :], in0=w[:, s, k, :], scalar=cond[:, k:k + 1],
                                                                   in1=acc[:, s, :], op0=ALU.mult, op1=ALU.add)
                                if k < KT - 1:
                                    ins.then_inc(mac, 1)
                            ins.then_inc(acc_ready, 1)
                            dve.wait_ge(acc_ready, RING * i + (layer * GR + s + 1))
                            dve.wait_ge(sum_ready, RING * i + (layer * GR + s + 1))
                            dve.wait_ge(row_out[s], 16 * i + 16 * (layer * (GR // RING) + 1))
                            dve.tensor_tensor(row[0:1, s, :], psum[0:1, s, :], bias[0:1, s, :], ALU.add).then_inc(row_ready, 1)
                            dve.wait_ge(row_ready, RING * i + (layer * GR + s + 1))
                            dve.sem_inc(w_used, 1)

            @block.tensor
            def _(pe):
                pe.wait_ge(ones_ready, 1)
                for layer in range(2):
                    with pe.Fori(0, GR // RING) as i:
                        for s in range(RING):
                            pe.wait_ge(acc_ready, RING * i + (layer * GR + s + 1))
                            for h in range(2):
                                last = pe.matmul(psum[0:1, s, h * HALF:(h + 1) * HALF], ones[:, 0:1],
                                                 acc[:, s, h * HALF:(h + 1) * HALF], start=True, stop=True)
                            last.then_inc(sum_ready, 1)


def in_proj(nc, layer, x_src, x_dst, norm_g, mod_rows, w_in, out_t, ident, combine=None, gates=None, conv=None, blank=None):
    with Phase(nc, f"in{layer}") as ph:
        u_hi = ph.sb("u_hi", [P, KT, T], F32R)
        u_lo = ph.sb("u_lo", [P, KT, T], F32R)
        w_raw = ph.sb("w_raw", [P, RING, KT, P])
        w_hi = ph.sb("w_hi", [P, RING, KT, P], F32R)
        w_lo = ph.sb("w_lo", [P, RING, KT, P], F32R)
        work = ph.sb("work", [P, 9 * D])
        view = lambda at, n: work[:, at * D:(at + n) * D]
        xin = view(0, 2).rearrange("p (s d) -> p s d", s=RING)
        row_a = view(2, 2).rearrange("p (s d) -> p s d", s=RING)
        row_b = view(4, 2).rearrange("p (s d) -> p s d", s=RING)
        scale_b, shift_b, gate_b = view(6, 1), view(7, 1), view(8, 1)
        stage = view(0, 4).rearrange("p (s t) -> p s t", s=RING)
        gate_rows = view(4, 2)
        c_rows = view(4, 2)
        z_rows = work[:, 6 * D:6 * D + 2 + T]
        ssq = ph.sb("ssq", [P, RING])
        rstd = ph.sb("rstd", [P, RING])
        mhalf = ph.sb("mhalf", [P, 1])
        idx = ph.sb("idx", [P, RING, 2], I32)
        wts = ph.sb("wts", [P, RING, 2])
        psum_t = ph.ps("psum_t", [P, RING, D])
        psum_o = ph.ps("psum_o", [P, NBLK, HALF])
        mod_in = ph.sem("mod_in")
        mod_ready = ph.sem("mod_ready")
        x_in = [ph.sem(f"x_in{s}") for s in range(RING)]
        ssq_ready = ph.sem("ssq_ready")
        var_ready = ph.sem("var_ready")
        rstd_ready = ph.sem("rstd_ready")
        passed = ph.sem("passed")
        um_ready = ph.sem("um_ready")
        u_ready = ph.sem("u_ready")
        tr_done = ph.sem("tr_done")
        hi_done = ph.sem("hi_done")
        lo_done = ph.sem("lo_done")
        const_ready = ph.sem("const_ready")
        wr_in = [ph.sem(f"wr_in{s}") for s in range(RING)]
        w_hi_ready = ph.sem("w_hi_ready")
        w_lo_ready = ph.sem("w_lo_ready")
        blk_done = ph.sem("blk_done")
        ev_act = ph.sem("ev_act")
        out_done = [ph.sem(f"out_done{s}") for s in range(RING)]
        if combine:
            ys, pos, pair_w, gate_row = combine
            rows_in = [ph.sem(f"rows_in{s}") for s in range(RING)]
            idx_ready = ph.sem("idx_ready")
            wts_ready = ph.sem("wts_ready")
            ra_ready = ph.sem("ra_ready")
            rb_ready = ph.sem("rb_ready")
            mix_ready = ph.sem("mix_ready")
            gate_in = ph.sem("gate_in")
            x2_ready = ph.sem("x2_ready")
            x_out = [ph.sem(f"x_out{s}") for s in range(RING)]
        if blank is not None:
            zero = ph.sb("zero", [P, D])
            zero_ready = ph.sem("zero_ready")
            blank_out = ph.sem("blank_out")
        if gates:
            b_gates, gates_t = gates
            gw_raw = ph.sb("gw_raw", [P, KT, 8])
            gw_hi = ph.sb("gw_hi", [P, KT, 8], F32R)
            gw_lo = ph.sb("gw_lo", [P, KT, 8], F32R)
            gbias = ph.sb("gbias", [8, 1])
            gw_in = ph.sem("gw_in")
            gw_ready = ph.sem("gw_ready")
            gates_ev = ph.sem("gates_ev")
            gates_out = ph.sem("gates_out")
        if conv:
            conv_w, conv_b = conv
            taps = ph.sb("taps", [P, KT, 4])
            tap = ph.sb("tap", [P, RING, 4])
            taps_in = ph.sem("taps_in")
            tap_ready = ph.sem("tap_ready")
            z_ready = ph.sem("z_ready")
            zc_ready = ph.sem("zc_ready")
            y_ready = ph.sem("y_ready")
        m_scale, m_shift = 1, 0
        CH = 6 if conv else 2
        if conv:
            kind_at = (D, 2 * D, 0)
            chunk_col = lambda i, q: kind_at[q % 3] + P * (q // 3) + i * (2 * P)
        else:
            chunk_col = lambda i, q: i * (CH * P) + q * P
        BODIES = NCHUNK // CH

        with ph.block() as block:
            @block.sync
            def _(sp):
                def load_x(n, s):
                    sp.dma_start(xin[:, s, :], x_src[bass.ds(n * P, P), :]).then_inc(x_in[s], 16)

                def load_w(col, s):
                    src = w_in[:, bass.ds(col, P)].rearrange("(k p) n -> p k n", p=P)
                    sp.dma_start(w_raw[:, s, :, :], src).then_inc(wr_in[s], 16)

                load_x(0, 0)
                sp.dma_start(scale_b, rowcast(mod_rows[layer, m_scale:m_scale + 1, :])).then_inc(mod_in, 16)
                sp.dma_start(gate_b if not combine else view(3, 1), rowcast(norm_g[layer:layer + 1, :])).then_inc(mod_in, 16)
                sp.dma_start(shift_b, rowcast(mod_rows[layer, m_shift:m_shift + 1, :])).then_inc(mod_in, 16)
                if combine:
                    sp.dma_start(gate_b, rowcast(gate_row)).then_inc(gate_in, 16)
                load_x(1, 1)
                if gates:
                    with nc.allow_non_contiguous_dma(reason="eight gate columns"):
                        sp.dma_start(gw_raw[:, :, :], w_in[:, NCOL:NCOL + 8].rearrange("(k p) n -> p k n", p=P)).then_inc(gw_in, 16)
                        sp.dma_start(gbias[0:8, 0:1], b_gates[0, :].rearrange("(n a) -> n a", a=1)).then_inc(gw_in, 16)
                if conv:
                    with nc.allow_non_contiguous_dma(reason="a few KB of taps laid over the partitions"):
                        for j in range(3):
                            sp.dma_start(taps[:, :, j], cols(conv_w[0, j, :])).then_inc(taps_in, 16)
                        sp.dma_start(taps[:, :, 3], cols(conv_b[0, :])).then_inc(taps_in, 16)
                for s in range(RING):
                    load_w(chunk_col(0, s), s)

                def a_tail(i, s, more):
                    if combine:
                        sp.wait_ge(x2_ready, RING * i + (s + 1))
                        sp.dma_start(x_dst[bass.ds(i * (RING * P) + s * P, P), :], xin[:, s, :]).then_inc(x_out[s], 16)
                    if more:
                        if combine:
                            sp.wait_ge(x_out[s], 16 * i + 16)
                        sp.wait_ge(um_ready, RING * i + (s + 1))
                        load_x(i * RING + (RING + s), s)

                with sp.Fori(0, NT // RING - 1) as i:
                    for s in range(RING):
                        a_tail(i, s, True)
                for s in range(RING):
                    a_tail(NT // RING - 1, s, False)

                def store(i, q):
                    if conv:
                        if q % 3 == 2:
                            j, s = q // 3, (q // 3) % RING
                            sp.wait_ge(y_ready, i * (2 * NBLK) + NBLK * (j + 2))
                            sp.dma_start(out_t[bass.ds(i * (2 * P) + j * P, P), :], stage[:, s, :]).then_inc(out_done[s], 16)
                    else:
                        sp.wait_ge(ev_act, i * (CH * NBLK) + NBLK * (q + 2))
                        sp.dma_start(out_t[bass.ds(i * (CH * P) + q * P, P), :], stage[:, q % RING, :]).then_inc(out_done[q % RING], 16)

                with sp.Fori(0, BODIES - 1) as i:
                    for q in range(CH):
                        sp.wait_ge(w_lo_ready, i * CH + (q + 1))
                        load_w(chunk_col(i, q + 2), q % RING)
                        store(i, q)
                for q in range(CH):
                    if q + 2 < CH:
                        sp.wait_ge(w_lo_ready, (BODIES - 1) * CH + (q + 1))
                        load_w(chunk_col(BODIES - 1, q + 2), q % RING)
                    store(BODIES - 1, q)
                if gates:
                    sp.wait_ge(gates_ev, NBLK)
                    sp.dma_start(gates_t[:, :], gate_rows[0:8, :]).then_inc(gates_out, 16)
                    sp.wait_ge(gates_out, 16)
                n_out = (KT if conv else NCHUNK) // RING
                for s in range(RING):
                    sp.wait_ge(out_done[s], 16 * (n_out + 1))

            @block.gpsimd
            def _(pool):
                pool.memset(mhalf[:, :], -0.5).then_inc(const_ready, 1)
                pool.wait_ge(const_ready, 1)

                def gather(n, s, count):
                    for j in range(2):
                        pool.tensor_copy(idx[:, s, j:j + 1], pos[:, j, bass.ds(n, 1)]).then_inc(idx_ready, 1)
                    pool.wait_ge(idx_ready, count)
                    stand(pool, passed)
                    for j, dst in enumerate((row_a, row_b)):
                        pool.indirect_dma_start(dst[:, s, :], None, ys, bass.IndirectOffsetOnAxis(ap=idx[:, s, j:j + 1], axis=0)).then_inc(rows_in[s], 16)

                def tile(i, s):
                    n1 = i * RING + (s + 1)
                    if combine:
                        pool.wait_ge(mix_ready, n1)
                        pool.wait_ge(x_in[s], 16 * i + 16)
                        pool.tensor_tensor(xin[:, s, :], xin[:, s, :], row_b[:, s, :], ALU.add).then_inc(x2_ready, 1)
                    pool.wait_ge(ssq_ready, n1)
                    stand(pool, passed)
                    pool.tensor_scalar(rstd[:, s:s + 1], ssq[:, s:s + 1], 1.0 / D, EPS, ALU.mult, ALU.add).then_inc(var_ready, 1)
                    pool.wait_ge(var_ready, n1)
                    pool.tensor_tensor(rstd[:, s:s + 1], rstd[:, s:s + 1], mhalf[:, 0:1], ALU.pow).then_inc(rstd_ready, 1)
                    pool.wait_ge(um_ready, n1)
                    pool.tensor_tensor(row_a[:, s, :], row_a[:, s, :], shift_b, ALU.add).then_inc(u_ready, 1)

                if combine:
                    gather(0, 0, 2)
                    pool.wait_ge(mod_ready, 1)
                    gather(1, 1, 4)
                pool.wait_ge(mod_ready, 1)
                if blank is not None:
                    pool.memset(zero[:, :], 0.0).then_inc(zero_ready, 1)
                with pool.Fori(0, NT // RING - 1) as i:
                    for s in range(RING):
                        tile(i, s)
                        if combine:
                            pool.wait_ge(tr_done, i * RING + (s + 1))
                            gather(i * RING + (RING + s), s, i * (2 * RING) + 2 * (RING + s + 1))
                for s in range(RING):
                    tile(NT // RING - 1, s)
                if blank is not None:
                    pool.wait_ge(zero_ready, 1)
                    for a in range(MAX_TILES):
                        pool.dma_start(blank[a * P:(a + 1) * P, :], zero[:, :]).then_inc(blank_out, 16)
                    pool.wait_ge(blank_out, 16 * MAX_TILES)

            @block.scalar
            def _(act):
                act.sem_inc(hi_done, RING)
                act.sem_inc(ev_act, NBLK)
                for s in range(RING):
                    act.sem_inc(out_done[s], 16)

                def split_w(blocks, loaded, s):
                    act.wait_ge(wr_in[s], loaded)
                    if blocks is not None:
                        act.wait_ge(blk_done, blocks)
                    act.activation(w_hi[:, s, :, :], w_raw[:, s, :, :], ACT.Copy).then_inc(w_hi_ready, 1)

                def tile(i, s):
                    n1 = i * RING + (s + 1)
                    if combine:
                        act.wait_ge(rows_in[s], 32 * i + 32)
                        act.wait_ge(wts_ready, n1)
                        act.activation(row_a[:, s, :], row_a[:, s, :], ACT.Copy, scale=wts[:, s, 0:1]).then_inc(ra_ready, 1)
                        act.wait_ge(x2_ready, n1)
                    else:
                        act.wait_ge(x_in[s], 16 * i + 16)
                    act.activation(row_b[:, s, :], xin[:, s, :], ACT.Square, accum_out=ssq[:, s:s + 1]).then_inc(ssq_ready, 1)
                    act.wait_ge(tr_done, n1)
                    act.activation(u_hi[:, :, bass.ds(i * (RING * P) + s * P, P)],
                                   psum_t[:, s, :].rearrange("p (k t) -> p k t", k=KT), ACT.Copy).then_inc(hi_done, 1)

                with act.Fori(0, NT // RING) as i:
                    for s in range(RING):
                        tile(i, s)
                for s in range(RING):
                    split_w(None, 16, s)
                if gates:
                    act.wait_ge(gw_in, 32)
                    act.activation(gw_hi[:, :, :], gw_raw[:, :, :], ACT.Copy).then_inc(gw_ready, 1)
                if combine:
                    for s in range(RING):
                        act.wait_ge(x_out[s], 16 * (NT // RING))

                def body(i, q, more):
                    if conv:
                        if q % 3 == 0:
                            j = q // 3
                            for b in range(NBLK):
                                act.wait_ge(y_ready, i * (2 * NBLK) + NBLK * j + b + 1)
                                act.wait_ge(blk_done, i * (CH * NBLK) + NBLK * q + b + 1)
                                act.activation(c_rows[:, b * HALF:(b + 1) * HALF], psum_o[:, b, :], ACT.Copy).then_inc(ev_act, 1)
                    else:
                        act.wait_ge(out_done[q % RING], 16 * i + 16)
                        for b in range(NBLK):
                            act.wait_ge(blk_done, i * (CH * NBLK) + NBLK * q + b + 1)
                            act.activation(stage[:, q % RING, b * HALF:(b + 1) * HALF], psum_o[:, b, :], ACT.Copy).then_inc(ev_act, 1)
                    if more:
                        split_w(i * (CH * NBLK) + NBLK * (q + 1), i * (16 * CH // RING) + 16 * (q // RING + 2), q % RING)

                with act.Fori(0, BODIES - 1) as i:
                    for q in range(CH):
                        body(i, q, True)
                for q in range(CH):
                    body(BODIES - 1, q, q + 2 < CH)
                if gates:
                    for b in range(NBLK):
                        act.wait_ge(blk_done, NCHUNK * NBLK + b + 1)
                        act.activation(gate_rows[0:8, b * HALF:(b + 1) * HALF], psum_o[0:8, b, :], ACT.Identity, bias=gbias[0:8, 0:1]).then_inc(gates_ev, 1)

            @block.vector
            def _(dve):
                dve.sem_inc(lo_done, RING)
                dve.wait_ge(mod_in, 48)
                dve.scalar_tensor_tensor(out=scale_b, in0=scale_b, scalar=1.0, in1=gate_b if not combine else view(3, 1),
                                         op0=ALU.add, op1=ALU.mult).then_inc(mod_ready, 1)
                dve.wait_ge(mod_ready, 1)
                if conv:
                    dve.sem_inc(y_ready, NBLK)

                def tile(i, s):
                    n1 = i * RING + (s + 1)
                    if combine:
                        dve.tensor_copy(wts[:, s, :], pair_w[:, :, bass.ds(i * RING + s, 1)].rearrange("p j a -> p (j a)")).then_inc(wts_ready, 1)
                        dve.wait_ge(wts_ready, n1)
                        dve.wait_ge(ra_ready, n1)
                        dve.scalar_tensor_tensor(out=row_b[:, s, :], in0=row_b[:, s, :], scalar=wts[:, s, 1:2], in1=row_a[:, s, :],
                                                 op0=ALU.mult, op1=ALU.add).then_inc(rb_ready, 1)
                        dve.wait_ge(rb_ready, n1)
                        dve.tensor_tensor(row_b[:, s, :], row_b[:, s, :], gate_b, ALU.mult).then_inc(mix_ready, 1)
                    dve.wait_ge(rstd_ready, n1)
                    if not combine:
                        dve.wait_ge(x_in[s], 16 * i + 16)
                    dve.scalar_tensor_tensor(out=row_a[:, s, :], in0=xin[:, s, :], scalar=rstd[:, s:s + 1], in1=scale_b,
                                             op0=ALU.mult, op1=ALU.mult).then_inc(um_ready, 1)
                    dve.wait_ge(hi_done, n1 + RING)
                    dst = bass.ds(i * (RING * P) + s * P, P)
                    dve.tensor_tensor(u_lo[:, :, dst], psum_t[:, s, :].rearrange("p (k t) -> p k t", k=KT),
                                      u_hi[:, :, dst].bitcast(F32), ALU.subtract).then_inc(lo_done, 1)

                if combine:
                    dve.wait_ge(gate_in, 16)
                with dve.Fori(0, NT // RING) as i:
                    for s in range(RING):
                        tile(i, s)

                def split_w(n1, s):
                    dve.wait_ge(w_hi_ready, n1)
                    dve.tensor_tensor(w_lo[:, s, :, :], w_raw[:, s, :, :], w_hi[:, s, :, :].bitcast(F32), ALU.subtract).then_inc(w_lo_ready, 1)

                for s in range(RING):
                    split_w(s + 1, s)
                if gates:
                    dve.wait_ge(gw_ready, 1)
                    dve.tensor_tensor(gw_lo[:, :, :], gw_raw[:, :, :], gw_hi[:, :, :].bitcast(F32), ALU.subtract).then_inc(gw_ready, 1)
                if conv:
                    dve.wait_ge(taps_in, 64)
                    dve.memset(z_rows[:, 0:2], 0.0).then_inc(z_ready, 1)
                    for s in range(RING):
                        dve.wait_ge(x_out[s], 16 * (NT // RING))

                def body(i, q, more):
                    if conv:
                        j, kind = q // 3, q % 3
                        n0 = i * (2 * NBLK) + NBLK * j
                        if kind == 0:
                            dve.tensor_copy(tap[:, j, :], taps[:, bass.ds(i * 2 + j, 1), :].rearrange("p a j -> p (a j)")).then_inc(tap_ready, 1)
                        if kind == 1:
                            for b in range(NBLK):
                                cs, at = c_rows[:, b * HALF:(b + 1) * HALF], b * HALF
                                dve.wait_ge(ev_act, n0 + (NBLK + b + 1))
                                dve.wait_ge(blk_done, i * (CH * NBLK) + NBLK * q + b + 1)
                                dve.tensor_tensor(z_rows[:, 2 + at:2 + at + HALF], cs, psum_o[:, b, :], ALU.mult).then_inc(z_ready, 1)
                            for b in range(NBLK):
                                cs, at = c_rows[:, b * HALF:(b + 1) * HALF], b * HALF
                                if b == 0:
                                    dve.wait_ge(tap_ready, i * 2 + (j + 1))
                                    dve.wait_ge(z_ready, n0 + (NBLK + 1))
                                dve.tensor_scalar(cs, z_rows[:, 2 + at:2 + at + HALF], tap[:, j, 2:3], tap[:, j, 3:4],
                                                  ALU.mult, ALU.add).then_inc(zc_ready, 1)
                                for m, o in ((1, 1), (0, 0)):
                                    dve.wait_ge(zc_ready, i * (2 * NBLK * 3) + 3 * (NBLK * j + b) + 2 - m)
                                    dve.scalar_tensor_tensor(out=cs, in0=z_rows[:, o + at:o + at + HALF], scalar=tap[:, j, m:m + 1],
                                                             in1=cs, op0=ALU.mult, op1=ALU.add).then_inc(zc_ready, 1)
                        if kind == 2:
                            dve.wait_ge(out_done[j], 16 * i + 16)
                            dve.wait_ge(zc_ready, i * (2 * NBLK * 3) + 3 * NBLK * (j + 1))
                            for b in range(NBLK):
                                dve.wait_ge(blk_done, i * (CH * NBLK) + NBLK * q + b + 1)
                                dve.tensor_tensor(stage[:, j, b * HALF:(b + 1) * HALF], c_rows[:, b * HALF:(b + 1) * HALF], psum_o[:, b, :],
                                                  ALU.mult).then_inc(y_ready, 1)
                    if more:
                        split_w(i * CH + (q + 3), q % RING)

                with dve.Fori(0, BODIES - 1) as i:
                    for q in range(CH):
                        body(i, q, True)
                for q in range(CH):
                    body(BODIES - 1, q, q + 2 < CH)

            @block.tensor
            def _(pe):
                with pe.Fori(0, NT // RING) as i:
                    for s in range(RING):
                        n1 = i * RING + (s + 1)
                        pe.wait_ge(u_ready, n1)
                        pe.wait_ge(hi_done, n1)
                        pe.wait_ge(lo_done, n1)
                        for k in range(KT):
                            last = pe.transpose(psum_t[:, s, k * P:(k + 1) * P], row_a[:, s, k * P:(k + 1) * P], ident[:, :])
                        last.then_inc(tr_done, 1)
                pe.wait_ge(hi_done, NT + RING)
                pe.wait_ge(lo_done, NT + RING)

                def block_of(b, rows, wh, wl):
                    ts = slice(b * HALF, (b + 1) * HALF)
                    for k in range(KT):
                        last = split_mm(pe, psum_o[0:rows, b, :], (wh[:, k, :], wl[:, k, :]),
                                        (u_hi[:, k, ts], u_lo[:, k, ts]), k == 0, k == KT - 1)
                    last.then_inc(blk_done, 1)
                    return last

                def body(i, q):
                    pe.wait_ge(w_lo_ready, i * CH + (q + 1))
                    for b in range(NBLK):
                        if conv:
                            n0 = i * (2 * NBLK) + NBLK * (q // 3) + b + 1
                            if q % 3 == 0:
                                pe.wait_ge(y_ready, n0)
                            elif q % 3 == 1:
                                pe.wait_ge(ev_act, n0 + NBLK)
                            else:
                                pe.wait_ge(z_ready, n0 + 1)
                        else:
                            pe.wait_ge(ev_act, i * (CH * NBLK) + NBLK * q + b + 1)
                        block_of(b, P, w_hi[:, q % RING], w_lo[:, q % RING])

                with pe.Fori(0, BODIES) as i:
                    for q in range(CH):
                        body(i, q)
                if gates:
                    pe.wait_ge(gw_ready, 2)
                    for b in range(NBLK):
                        pe.wait_ge(ev_act, NCHUNK * NBLK + b + 1)
                        block_of(b, 8, gw_hi, gw_lo)


def mlstm(nc, proj_t, gates_t, gate_d, norm_g, h_t, ident):
    HC = HEADS * NT
    V1 = DV + 1
    SCALE = float(DQK) ** -0.5
    with Phase(nc, "rec") as ph:
        gi = ph.sb("gi", [HC, P])
        gf = ph.sb("gf", [HC, P])
        tmp = ph.sb("tmp", [HC, P])
        lf = ph.sb("lf", [HC, P])
        b = ph.sb("b", [HC, P])
        g = ph.sb("g", [HC, P])
        zeros = ph.sb("zeros", [HC, P])
        ones = ph.sb("ones", [HC, P])
        m_run = ph.sb("m_run", [HC, P])
        ends = ph.sb("ends", [HC, 2])
        m_start = ph.sb("m_start", [HC, 1])
        neg_last = ph.sb("neg_last", [HC, 1])
        neg_m = ph.sb("neg_m", [HC, 2, P])
        wk = ph.sb("wk", [HC, P])
        enm = ph.sb("enm", [HC, P])
        chain = ph.sb("chain", [HEADS, NT, 2])
        m_seq = ph.sb("m_seq", [HEADS, NT + 1])
        tok = ph.sb("tok", [P, 3, HC])
        decay = ph.sb("decay", [P, HC])
        causal = ph.sb("causal", [P, P])
        causal4 = ph.sb("causal4", [P, HEADS, P])
        ng = ph.sb("ng", [P, KT])
        mhalf = ph.sb("mhalf", [P, HEADS])
        pt = ph.sb("pt", [P, RING, 3 * KT, P])
        bc = ph.sb("bc", [P, RING, HEADS, 2, P])
        kw = ph.sb("kw", [P, RING, HEADS, DQK])
        val = ph.sb("val", [P, RING, HEADS, V1])
        qw = ph.sb("qw", [P, RING, HEADS, P])
        arg = ph.sb("arg", [P, HEADS, P])
        sd = ph.sb("sd", [P, RING, HEADS, P])
        cst = ph.sb("cst", [P, HEADS, V1])
        sgate = ph.sb("sgate", [P, RING, KT, P])
        numer = ph.sb("numer", [P, HEADS, V1])
        junk = ph.sb("junk", [P, DV])
        den = ph.sb("den", [P, HEADS])
        ssq = ph.sb("ssq", [P, HEADS])
        fac = ph.sb("fac", [P, HEADS])
        hout = ph.sb("hout", [P, RING, KT, P])
        tokc = ph.sb("tokc", [P, RING, 3, HEADS])
        decc = ph.sb("decc", [P, RING, HEADS])
        ps_k = ph.ps("ps_k", [P, HEADS, P])
        ps_v = ph.ps("ps_v", [P, KT, P])
        ps_s = ph.ps("ps_s", [P, HEADS, P])
        ps_n = ph.ps("ps_n", [P, RING, HALF])
        ps_c = ph.ps("ps_c", [P, RING, HALF])
        g_in = ph.sem("g_in")
        pre = ph.sem("pre")
        pre_act = ph.sem("pre_act")
        ends_out = ph.sem("ends_out")
        chain_in = ph.sem("chain_in")
        seq_out = ph.sem("seq_out")
        start_in = ph.sem("start_in")
        rows_out = ph.sem("rows_out")
        decay_in = ph.sem("decay_in")
        tok_tr = ph.sem("tok_tr")
        passed = ph.sem("passed")
        tok_ready = ph.sem("tok_ready")
        consts = ph.sem("consts")
        ng_in = ph.sem("ng_in")
        pt_in = [ph.sem(f"pt_in{s}") for s in range(RING)]
        bc_in = [ph.sem(f"bc_in{s}") for s in range(RING)]
        kv_tr = ph.sem("kv_tr")
        s_done = ph.sem("s_done")
        kw_ready = ph.sem("kw_ready")
        val_ready = ph.sem("val_ready")
        qw_ready = ph.sem("qw_ready")
        cols_ready = ph.sem("cols_ready")
        arg_ready = ph.sem("arg_ready")
        masked = ph.sem("masked")
        exp_ready = ph.sem("exp_ready")
        sd_ready = ph.sem("sd_ready")
        num_done = ph.sem("num_done")
        cup_done = ph.sem("cup_done")
        c_ready = ph.sem("c_ready")
        num_ev = ph.sem("num_ev")
        den_ready = ph.sem("den_ready")
        norm_step = ph.sem("norm_step")
        fsq = ph.sem("fsq")
        fss = ph.sem("fss")
        fac_ready = ph.sem("fac_ready")
        hn_ready = ph.sem("hn_ready")
        h_tr = ph.sem("h_tr")
        h_ready = ph.sem("h_ready")
        sig_ready = ph.sem("sig_ready")
        gate_ready = ph.sem("gate_ready")
        h_out = [ph.sem(f"h_out{s}") for s in range(RING)]
        ends_d, seq_d, rows_d, decay_d = gate_d
        NPRE = 3

        with ph.block() as block:
            @block.sync
            def _(sp):
                src = lambda r: gates_t[r:r + HEADS, :].rearrange("h (c t) -> (h c) t", t=P)
                sp.dma_start(gi[:, :], src(0)).then_inc(g_in, 16)
                sp.dma_start(gf[:, :], src(HEADS)).then_inc(g_in, 16)
                with nc.allow_non_contiguous_dma(reason="4 KB vector laid over the partitions"):
                    sp.dma_start(ng[:, :], cols(norm_g[0, :])).then_inc(ng_in, 16)

                def load(c, s):
                    sp.dma_start(pt[:, s, :, :], proj_t[:, bass.ds(c * P, P)].rearrange("(r p) t -> p r t", p=P)).then_inc(pt_in[s], 16)

                def load_bc(c, s):
                    for h in range(HEADS):
                        src = rows_d[bass.ds(c + h * NT, 1), :].to_broadcast([P, 2 * P])
                        sp.dma_start(bc[:, s, h, :, :], src.rearrange("p (a t) -> p a t", a=2)).then_inc(bc_in[s], 16)

                load(0, 0)
                load(1, 1)
                sp.wait_ge(pre, 8)
                sp.dma_start(ends_d[:, :], ends[:, :]).then_inc(ends_out, 16)
                sp.wait_ge(ends_out, 16)
                sp.dma_start(chain[:, :, :], ends_d.rearrange("(h c) a -> h c a", h=HEADS)).then_inc(chain_in, 16)
                sp.wait_ge(pre, 10)
                sp.dma_start(seq_d.rearrange("(h c) a -> h (c a)", h=HEADS), m_seq[:, 0:NT]).then_inc(seq_out, 16)
                sp.wait_ge(seq_out, 16)
                sp.dma_start(m_start[:, :], seq_d).then_inc(start_in, 16)
                sp.wait_ge(pre, 14)
                sp.wait_ge(pre_act, 3)
                sp.dma_start(rows_d, neg_m[:, :, :].rearrange("p a t -> p (a t)")).then_inc(rows_out, 16)
                sp.dma_start(decay_d, neg_m[:, 1, P - 1:P]).then_inc(rows_out, 16)
                sp.wait_ge(rows_out, 32)
                sp.dma_start(decay[:, :], decay_d.rearrange("c a -> a c").to_broadcast([P, HC])).then_inc(decay_in, 16)
                load_bc(0, 0)
                load_bc(1, 1)

                def chunk(i, s, more):
                    n = i * RING + (s + 1)
                    sp.wait_ge(h_ready, n + RING)
                    sp.dma_start(h_t[:, bass.ds(i * (RING * P) + s * P, P)].rearrange("(k p) t -> p k t", p=P), hout[:, s, :, :]).then_inc(h_out[s], 16)
                    if more:
                        sp.wait_ge(sig_ready, n)
                        sp.wait_ge(val_ready, n)
                        sp.wait_ge(kw_ready, n)
                        sp.wait_ge(sd_ready, n)
                        load(i * RING + (RING + s), s)
                        load_bc(i * RING + (RING + s), s)

                with sp.Fori(0, NT // RING - 1) as i:
                    for s in range(RING):
                        chunk(i, s, True)
                for s in range(RING):
                    chunk(NT // RING - 1, s, False)
                for s in range(RING):
                    sp.wait_ge(h_out[s], 16 * (NT // RING + 1))

            @block.gpsimd
            def _(pool):
                pool.memset(zeros[:, :], 0.0).then_inc(consts, 1)
                pool.memset(ones[:, :], 1.0).then_inc(consts, 1)
                pool.memset(mhalf[:, :], -0.5).then_inc(consts, 1)
                pool.memset(causal4[:, :, :], 0.0).then_inc(consts, 1)
                pool.memset(val[:, :, :, DV:V1], 1.0).then_inc(consts, 1)
                pool.memset(cst[:, :, :], 0.0).then_inc(consts, 1)
                pool.wait_ge(consts, 6)
                pool.affine_select(out=causal4[:, :, :], in_=causal4[:, :, :], compare_op=ALU.is_ge, fill=-BIG, base=0,
                                   pattern=[[0, HEADS], [1, P]], channel_multiplier=-1).then_inc(consts, 1)
                pool.wait_ge(consts, 7)
                pool.wait_ge(ng_in, 16)

                def early(i, s):
                    n = i * RING + (s + 1)
                    pool.wait_ge(arg_ready, n)
                    pool.tensor_tensor(arg[:, :, :], arg[:, :, :], causal4[:, :, :], ALU.add).then_inc(masked, 1)

                def late(i, s):
                    n = i * RING + (s + 1)
                    pool.wait_ge(sig_ready, n)
                    pool.tensor_tensor(sgate[:, s, :, :], sgate[:, s, :, :], ng[:, :].unsqueeze(2).to_broadcast([P, KT, P]), ALU.mult).then_inc(gate_ready, 1)
                    pool.wait_ge(norm_step, i * (RING * 3) + (3 * s + 2))
                    pool.tensor_tensor(fac[:, :], fac[:, :], mhalf[:, :], ALU.pow).then_inc(fac_ready, 1)

                early(0, 0)
                with pool.Fori(0, NT // RING - 1) as i:
                    early(i, 1)
                    late(i, 0)
                    early(i + 1, 0)
                    late(i, 1)
                early(NT // RING - 1, 1)
                late(NT // RING - 1, 0)
                late(NT // RING - 1, 1)

            @block.scalar
            def _(act):
                for s in range(RING):
                    act.sem_inc(h_out[s], 16)
                act.sem_inc(num_ev, 2 * RING)
                act.wait_ge(pre, 1)
                act.activation(tmp[:, :], tmp[:, :], ACT.Exp, scale=-1.0).then_inc(pre_act, 1)
                act.wait_ge(pre, 2)
                act.activation(tmp[:, :], tmp[:, :], ACT.Ln).then_inc(pre_act, 1)
                act.wait_ge(pre, 14)
                act.activation(neg_m[:, 1, :], neg_m[:, 0, :], ACT.Exp, bias=m_start[:, 0:1]).then_inc(pre_act, 1)
                act.activation(wk[:, :], g[:, :], ACT.Exp, bias=neg_last[:, 0:1]).then_inc(pre_act, 1)
                act.activation(enm[:, :], tmp[:, :], ACT.Exp, scale=-1.0).then_inc(pre_act, 1)

                def stage1(i, s):
                    n = i * RING + (s + 1)
                    act.wait_ge(kv_tr, n)
                    act.activation(val[:, s, :, 0:DV], ps_v[:, :, :].rearrange("p (h a) d -> p h (a d)", h=HEADS), ACT.Copy).then_inc(val_ready, 1)
                    act.wait_ge(masked, n)
                    act.activation(arg[:, :, :], arg[:, :, :], ACT.Exp).then_inc(exp_ready, 1)
                    act.wait_ge(h_ready, n)
                    act.activation(sgate[:, s, :, :], pt[:, s, 2 * KT:3 * KT, :], ACT.Tanh, scale=0.5)\
                       .then_inc(exp_ready, 1)

                def stage2(i, s):
                    n4 = i * (RING * HEADS) + s * HEADS
                    act.wait_ge(h_tr, i * RING + (s + 1))
                    for h in range(HEADS):
                        act.wait_ge(num_done, n4 + (h + 1))
                        act.wait_ge(num_ev, i * (2 * RING * HEADS) + 2 * (s * HEADS + h) + 3)
                        act.activation(junk[:, :], ps_n[:, h % RING, 0:DV], ACT.Square, accum_out=ssq[:, h:h + 1]).then_inc(num_ev, 1)
                        act.activation(numer[:, h, :], ps_n[:, h % RING, 0:V1], ACT.Copy).then_inc(num_ev, 1)
                    act.wait_ge(cup_done, n4 + HEADS)
                    stand(act, passed)

                act.wait_ge(consts, 7)
                stage1(0, 0)
                with act.Fori(0, NT // RING - 1) as i:
                    stage1(i, 1)
                    stage2(i, 0)
                    stage1(i + 1, 0)
                    stage2(i, 1)
                stage1(NT // RING - 1, 1)
                stage2(NT // RING - 1, 0)
                stage2(NT // RING - 1, 1)

            @block.vector
            def _(dve):
                dve.wait_ge(g_in, 32)
                dve.wait_ge(consts, 7)
                dve.scalar_tensor_tensor(out=tmp[:, :], in0=gf[:, :], scalar=-1.0, in1=gf[:, :], op0=ALU.mult, op1=ALU.max).then_inc(pre, 1)
                dve.wait_ge(pre_act, 1)
                dve.tensor_scalar(tmp[:, :], tmp[:, :], 1.0, None, ALU.add).then_inc(pre, 1)
                dve.wait_ge(pre_act, 2)
                dve.scalar_tensor_tensor(out=lf[:, :], in0=gf[:, :], scalar=0.0, in1=tmp[:, :], op0=ALU.min, op1=ALU.subtract).then_inc(pre, 1)
                dve.wait_ge(pre, 3)
                dve.tensor_tensor_scan(b[:, :], ones[:, :], lf[:, :], 0.0, ALU.mult, ALU.add).then_inc(pre, 1)
                dve.wait_ge(pre, 4)
                dve.tensor_tensor(g[:, :], gi[:, :], b[:, :], ALU.subtract).then_inc(pre, 1)
                dve.tensor_copy(ends[:, 1:2], b[:, P - 1:P]).then_inc(pre, 1)
                dve.wait_ge(pre, 5)
                dve.tensor_tensor_scan(m_run[:, :], zeros[:, :], g[:, :], -BIG, ALU.add, ALU.max).then_inc(pre, 1)
                dve.wait_ge(pre, 7)
                dve.tensor_copy(ends[:, 0:1], m_run[:, P - 1:P]).then_inc(pre, 1)
                dve.memset(m_seq[:, 0:1], 0.0).then_inc(pre, 1)
                dve.wait_ge(chain_in, 16)
                dve.tensor_tensor_scan(m_seq[:, 1:NT + 1], chain[:, :, 0], chain[:, :, 1], 0.0, ALU.max, ALU.add).then_inc(pre, 1)
                dve.wait_ge(start_in, 16)
                dve.tensor_scalar(m_run[:, :], m_run[:, :], m_start[:, 0:1], None, ALU.max).then_inc(pre, 1)
                dve.wait_ge(pre, 11)
                dve.tensor_scalar(neg_m[:, 0, :], m_run[:, :], -1.0, None, ALU.mult).then_inc(pre, 1)
                dve.tensor_scalar(neg_last[:, :], m_run[:, P - 1:P], -1.0, None, ALU.mult).then_inc(pre, 1)
                dve.tensor_tensor(tmp[:, :], b[:, :], m_run[:, :], ALU.add).then_inc(pre, 1)
                dve.wait_ge(tok_tr, 1)
                dve.tensor_copy(tok[:, :, :], ps_s[:, 0:NPRE, 0:HC]).then_inc(tok_ready, 1)
                dve.wait_ge(tok_ready, 1)
                dve.wait_ge(decay_in, 16)
                dve.sem_inc(c_ready, HEADS)
                dve.sem_inc(h_ready, RING)

                def stage1(i, s):
                    n = i * RING + (s + 1)
                    dve.tensor_copy(tokc[:, s, :, :], tok[:, :, :].rearrange("p a (h c) -> p a h c", h=HEADS)[:, :, :, bass.ds(i * RING + s, 1)]
                                    .rearrange("p a h c -> p a (h c)")).then_inc(cols_ready, 1)
                    dve.tensor_copy(decc[:, s, :], decay[:, :].rearrange("p (h c) -> p h c", h=HEADS)[:, :, bass.ds(i * RING + s, 1)]
                                    .rearrange("p h c -> p (h c)")).then_inc(cols_ready, 1)
                    dve.wait_ge(cols_ready, i * (2 * RING) + 2 * (s + 1))
                    dve.wait_ge(bc_in[s], 16 * HEADS * i + 16 * HEADS)
                    dve.tensor_tensor(arg[:, :, :], bc[:, s, :, 0, :], tokc[:, s, 0, :].unsqueeze(2).to_broadcast([P, HEADS, P]), ALU.add).then_inc(arg_ready, 1)
                    dve.wait_ge(pt_in[s], 16 * i + 16)
                    dve.scalar_tensor_tensor(out=qw[:, s, :, :], in0=pt[:, s, 0:HEADS, :], scalar=SCALE, in1=bc[:, s, :, 1, :],
                                             op0=ALU.mult, op1=ALU.mult).then_inc(qw_ready, 1)
                    dve.wait_ge(kv_tr, n)
                    dve.tensor_tensor(kw[:, s, :, :], ps_k[:, :, :], tokc[:, s, 1, :].unsqueeze(2).to_broadcast([P, HEADS, P]), ALU.mult).then_inc(kw_ready, 1)
                    dve.wait_ge(exp_ready, i * (2 * RING) + 2 * s + 1)
                    dve.wait_ge(s_done, n)
                    dve.scalar_tensor_tensor(out=sd[:, s, :, :], in0=ps_s[:, :, :], scalar=SCALE, in1=arg[:, :, :], op0=ALU.mult, op1=ALU.mult).then_inc(sd_ready, 1)
                    dve.wait_ge(exp_ready, i * (2 * RING) + 2 * (s + 1))
                    dve.tensor_scalar(sgate[:, s, :, :], sgate[:, s, :, :], 0.5, 0.5, ALU.mult, ALU.add).then_inc(sig_ready, 1)

                def stage2(i, s):
                    n = i * RING + (s + 1)
                    n4 = i * (RING * HEADS) + s * HEADS
                    n3 = i * (RING * 3) + 3 * s
                    for h in range(HEADS):
                        dve.wait_ge(cup_done, n4 + (h + 1))
                        dve.scalar_tensor_tensor(out=cst[:, h, :], in0=cst[:, h, :], scalar=decc[:, s, h:h + 1], in1=ps_c[:, h % RING, 0:V1],
                                                 op0=ALU.mult, op1=ALU.add).then_inc(c_ready, 1)
                    dve.wait_ge(num_ev, i * (2 * RING * HEADS) + 2 * HEADS * (s + 1) + 2 * RING)
                    dens = numer[:, :, DV:V1].rearrange("p h a -> p (h a)")
                    dve.scalar_tensor_tensor(out=den[:, :], in0=dens, scalar=-1.0, in1=tokc[:, s, 2, :], op0=ALU.mult, op1=ALU.max).then_inc(den_ready, 1)
                    dve.wait_ge(den_ready, i * (2 * RING) + (2 * s + 1))
                    dve.tensor_tensor(den[:, :], den[:, :], dens, ALU.max).then_inc(den_ready, 1)
                    dve.wait_ge(den_ready, i * (2 * RING) + 2 * (s + 1))
                    dve.reciprocal(den[:, :], den[:, :]).then_inc(norm_step, 1)
                    dve.wait_ge(norm_step, n3 + 1)
                    dve.tensor_tensor(fac[:, :], den[:, :], den[:, :], ALU.mult).then_inc(fsq, 1)
                    dve.wait_ge(fsq, n)
                    dve.tensor_tensor(fac[:, :], fac[:, :], ssq[:, :], ALU.mult).then_inc(fss, 1)
                    dve.wait_ge(fss, n)
                    dve.tensor_scalar(fac[:, :], fac[:, :], 1.0 / DV, EPS, ALU.mult, ALU.add).then_inc(norm_step, 1)
                    dve.wait_ge(fac_ready, n)
                    dve.tensor_tensor(fac[:, :], fac[:, :], den[:, :], ALU.mult).then_inc(norm_step, 1)
                    dve.wait_ge(norm_step, n3 + 3)
                    dve.tensor_tensor(numer[:, :, 0:DV], numer[:, :, 0:DV], fac[:, :].unsqueeze(2).to_broadcast([P, HEADS, DV]), ALU.mult).then_inc(hn_ready, 1)
                    dve.wait_ge(h_tr, n + 1)
                    dve.wait_ge(gate_ready, n)
                    dve.wait_ge(h_out[s], 16 * i + 16)
                    dve.tensor_tensor(hout[:, s, :, :], ps_v[:, :, :], sgate[:, s, :, :], ALU.mult).then_inc(h_ready, 1)

                stage1(0, 0)
                with dve.Fori(0, NT // RING - 1) as i:
                    stage1(i, 1)
                    stage2(i, 0)
                    stage1(i + 1, 0)
                    stage2(i, 1)
                stage1(NT // RING - 1, 1)
                stage2(NT // RING - 1, 0)
                stage2(NT // RING - 1, 1)

            @block.tensor
            def _(pe):
                pe.sem_inc(h_tr, 1)
                pe.wait_ge(pre, 14)
                pe.wait_ge(pre_act, 5)
                for a, src in enumerate((g, wk, enm)):
                    last = pe.transpose(ps_s[:, a, 0:HC], src[:, :], ident[0:HC, 0:HC])
                last.then_inc(tok_tr, 1)

                def stage1(i, s, first):
                    n = i * RING + (s + 1)
                    pe.wait_ge(pt_in[s], 16 * i + 16)
                    pe.wait_ge(h_ready, n)
                    if first:
                        pe.wait_ge(tok_ready, 1)
                    else:
                        pe.wait_ge(kw_ready, n - 1)
                        pe.wait_ge(val_ready, n - 1)
                        pe.wait_ge(sd_ready, n - 1)
                    for h in range(HEADS):
                        pe.transpose(ps_k[:, h, :], pt[:, s, HEADS + h, :], ident[:, :])
                    for r in range(KT):
                        last = pe.transpose(ps_v[:, r, :], pt[:, s, KT + r, :], ident[:, :])
                    last.then_inc(kv_tr, 1)
                    for h in range(HEADS):
                        last = pe.matmul(ps_s[:, h, :], pt[:, s, HEADS + h, :], pt[:, s, h, :], start=True, stop=True)
                    last.then_inc(s_done, 1)

                def stage2(i, s, first):
                    n = i * RING + (s + 1)
                    n4 = i * (RING * HEADS) + s * HEADS
                    pe.wait_ge(qw_ready, n)
                    pe.wait_ge(kw_ready, n)
                    pe.wait_ge(val_ready, n)
                    pe.wait_ge(sd_ready, n)
                    for h in range(HEADS):
                        q1 = n4 + (h + 1)
                        pe.wait_ge(c_ready, q1)
                        pe.wait_ge(num_ev, i * (2 * RING * HEADS) + 2 * (s * HEADS + h) + 2)
                        pe.matmul(ps_n[:, h % RING, 0:V1], qw[:, s, h, :], cst[:, h, :], start=True, stop=False)
                        pe.matmul(ps_n[:, h % RING, 0:V1], sd[:, s, h, :], val[:, s, h, :], start=False, stop=True).then_inc(num_done, 1)
                        pe.wait_ge(c_ready, q1 + RING)
                        pe.matmul(ps_c[:, h % RING, 0:V1], kw[:, s, h, :], val[:, s, h, :], start=True, stop=True).then_inc(cup_done, 1)
                    pe.wait_ge(hn_ready, n)
                    if not first:
                        pe.wait_ge(val_ready, n + 1)
                    for r in range(KT):
                        last = pe.transpose(ps_v[:, r, :], numer[:, r // 2, (r % 2) * P:(r % 2 + 1) * P], ident[:, :])
                    last.then_inc(h_tr, 1)

                last_pair = NT // RING - 1
                stage1(0, 0, True)
                with pe.Fori(0, last_pair) as i:
                    stage1(i, 1, False)
                    stage2(i, 0, False)
                    stage1(i + 1, 0, False)
                    stage2(i, 1, False)
                stage1(last_pair, 1, False)
                stage2(last_pair, 0, False)
                stage2(last_pair, 1, True)


def out_proj(nc, layer, h_t, w_out, x_src, x_dst, u_dst, norm_g, mod_rows, w_router, logits, ident):
    with Phase(nc, f"out{layer}") as ph:
        w_raw = ph.sb("w_raw", [P, RING, D])
        w_hi = ph.sb("w_hi", [P, KT, D], F32R)
        w_lo = ph.sb("w_lo", [P, KT, D], F32R)
        wr_raw = ph.sb("wr_raw", [P, KT, E])
        wr_hi = ph.sb("wr_hi", [P, KT, E], F32R)
        wr_lo = ph.sb("wr_lo", [P, KT, E], F32R)
        h_raw = ph.sb("h_raw", [P, RING, KT, P])
        h_hi = ph.sb("h_hi", [P, RING, KT, P], F32R)
        h_lo = ph.sb("h_lo", [P, RING, KT, P], F32R)
        xin = ph.sb("xin", [P, RING, D])
        xo = ph.sb("xo", [P, RING, D])
        u = ph.sb("u", [P, RING, D])
        u_hi = ph.sb("u_hi", [P, KT, P], F32R)
        u_lo = ph.sb("u_lo", [P, KT, P], F32R)
        gate_b = ph.sb("gate_b", [P, D])
        scale_b = ph.sb("scale_b", [P, D])
        shift_b = ph.sb("shift_b", [P, D])
        ng_b = ph.sb("ng_b", [P, D])
        ssq = ph.sb("ssq", [P, RING])
        rstd = ph.sb("rstd", [P, RING])
        mhalf = ph.sb("mhalf", [P, 1])
        psum_o = ph.ps("psum_o", [P, RING, D])
        psum_t = ph.ps("psum_t", [P, D])
        psum_r = ph.ps("psum_r", [P, RING, E])
        mod_in = ph.sem("mod_in")
        mod_ready = ph.sem("mod_ready")
        w_in = [ph.sem(f"w_in{s}") for s in range(RING)]
        wr_in = ph.sem("wr_in")
        w_hi_ready = ph.sem("w_hi_ready")
        w_lo_ready = ph.sem("w_lo_ready")
        h_in = [ph.sem(f"h_in{s}") for s in range(RING)]
        h_hi_ready = ph.sem("h_hi_ready")
        h_lo_ready = ph.sem("h_lo_ready")
        x_in = [ph.sem(f"x_in{s}") for s in range(RING)]
        mm_done = ph.sem("mm_done")
        gated = ph.sem("gated")
        xo_ready = ph.sem("xo_ready")
        x_out = [ph.sem(f"x_out{s}") for s in range(RING)]
        ssq_ready = ph.sem("ssq_ready")
        var_ready = ph.sem("var_ready")
        rstd_ready = ph.sem("rstd_ready")
        passed = ph.sem("passed")
        um_ready = ph.sem("um_ready")
        u_ready = ph.sem("u_ready")
        u_out = [ph.sem(f"u_out{s}") for s in range(RING)]
        tr_done = ph.sem("tr_done")
        u_hi_ready = ph.sem("u_hi_ready")
        u_lo_ready = ph.sem("u_lo_ready")
        r_done = ph.sem("r_done")
        logits_ready = ph.sem("logits_ready")
        const_ready = ph.sem("const_ready")
        LAST = NT // RING - 1

        with ph.block() as block:
            @block.sync
            def _(sp):
                def load(n, s):
                    sp.dma_start(h_raw[:, s, :, :], h_t[:, bass.ds(n * P, P)].rearrange("(k p) t -> p k t", p=P)).then_inc(h_in[s], 16)
                    sp.dma_start(xin[:, s, :], x_src[bass.ds(n * P, P), :]).then_inc(x_in[s], 16)

                load(0, 0)
                for k in range(KT):
                    if k >= RING:
                        sp.wait_ge(w_lo_ready, k - RING + 1)
                    sp.dma_start(w_raw[:, k % RING, :], w_out[k * P:(k + 1) * P, :]).then_inc(w_in[k % RING], 16)
                load(1, 1)
                with nc.allow_non_contiguous_dma(reason="64 KB router"):
                    sp.dma_start(wr_raw[:, :, :], w_router.rearrange("(k p) e -> p k e", p=P)).then_inc(wr_in, 16)
                for g, dst in ((2, gate_b), (3, shift_b), (4, scale_b)):
                    sp.dma_start(dst[:, :], rowcast(mod_rows[layer, g:g + 1, :])).then_inc(mod_in, 16)
                sp.dma_start(ng_b[:, :], rowcast(norm_g[layer:layer + 1, :])).then_inc(mod_in, 16)

                def tile(i, s, more):
                    n = i * RING + (s + 1)
                    if more:
                        sp.wait_ge(h_lo_ready, n)
                        sp.wait_ge(xo_ready, n)
                        load(i * RING + (RING + s), s)
                    else:
                        sp.wait_ge(xo_ready, n)
                    sp.dma_start(x_dst[bass.ds(i * (RING * P) + s * P, P), :], xo[:, s, :]).then_inc(x_out[s], 16)
                    sp.wait_ge(u_ready, n)
                    sp.dma_start(u_dst[bass.ds(i * (RING * P) + s * P, P), :], u[:, s, :]).then_inc(u_out[s], 16)

                with sp.Fori(0, LAST) as i:
                    for s in range(RING):
                        tile(i, s, True)
                for s in range(RING):
                    tile(LAST, s, False)
                for s in range(RING):
                    sp.wait_ge(x_out[s], 16 * (LAST + 2))
                    sp.wait_ge(u_out[s], 16 * (LAST + 2))

            @block.gpsimd
            def _(pool):
                pool.memset(mhalf[:, :], -0.5).then_inc(const_ready, 1)
                pool.wait_ge(const_ready, 1)
                pool.wait_ge(mod_ready, 1)
                with pool.Fori(0, NT // RING) as i:
                    for s in range(RING):
                        n = i * RING + (s + 1)
                        pool.wait_ge(ssq_ready, n)
                        stand(pool, passed)
                        pool.tensor_scalar(rstd[:, s:s + 1], ssq[:, s:s + 1], 1.0 / D, EPS, ALU.mult, ALU.add).then_inc(var_ready, 1)
                        pool.wait_ge(var_ready, n)
                        pool.tensor_tensor(rstd[:, s:s + 1], rstd[:, s:s + 1], mhalf[:, 0:1], ALU.pow).then_inc(rstd_ready, 1)
                        pool.wait_ge(um_ready, n)
                        pool.tensor_tensor(u[:, s, :], u[:, s, :], shift_b[:, :], ALU.add).then_inc(u_ready, 1)

            @block.scalar
            def _(act):
                for s in range(RING):
                    act.sem_inc(x_out[s], 16)
                    act.sem_inc(u_out[s], 16)

                def split_h(n1, i1, s):
                    act.wait_ge(h_in[s], i1)
                    if n1 is not None:
                        act.wait_ge(mm_done, n1)
                    act.activation(h_hi[:, s, :, :], h_raw[:, s, :, :], ACT.Copy).then_inc(h_hi_ready, 1)

                split_h(None, 16, 0)
                for k in range(KT):
                    act.wait_ge(w_in[k % RING], 16 * (k // RING + 1))
                    act.activation(w_hi[:, k, :], w_raw[:, k % RING, :], ACT.Copy).then_inc(w_hi_ready, 1)
                split_h(None, 16, 1)
                act.wait_ge(wr_in, 16)
                act.activation(wr_hi[:, :, :], wr_raw[:, :, :], ACT.Copy).then_inc(w_hi_ready, 1)

                def tile(i, s, more):
                    n = i * RING + (s + 1)
                    act.wait_ge(xo_ready, n)
                    act.wait_ge(u_out[s], 16 * i + 16)
                    act.activation(u[:, s, :], xo[:, s, :], ACT.Square, accum_out=ssq[:, s:s + 1]).then_inc(ssq_ready, 1)
                    if more:
                        split_h(n, 16 * i + 32, s)
                    act.wait_ge(tr_done, n)
                    act.activation(u_hi[:, :, :], psum_t[:, :].rearrange("p (k t) -> p k t", k=KT), ACT.Copy).then_inc(u_hi_ready, 1)
                    act.wait_ge(r_done, n)
                    act.activation(logits[:, bass.ds(i * RING + s, 1), :].rearrange("p a e -> p (a e)"), psum_r[:, s, :], ACT.Copy).then_inc(logits_ready, 1)

                with act.Fori(0, LAST) as i:
                    for s in range(RING):
                        tile(i, s, True)
                for s in range(RING):
                    tile(LAST, s, False)

            @block.vector
            def _(dve):
                def split_h(n1, s):
                    dve.wait_ge(h_hi_ready, n1)
                    dve.tensor_tensor(h_lo[:, s, :, :], h_raw[:, s, :, :], h_hi[:, s, :, :].bitcast(F32), ALU.subtract).then_inc(h_lo_ready, 1)

                split_h(1, 0)
                for k in range(KT):
                    dve.wait_ge(w_hi_ready, k + 1)
                    dve.tensor_tensor(w_lo[:, k, :], w_raw[:, k % RING, :], w_hi[:, k, :].bitcast(F32), ALU.subtract).then_inc(w_lo_ready, 1)
                split_h(2, 1)
                dve.wait_ge(w_hi_ready, KT + 1)
                dve.tensor_tensor(wr_lo[:, :, :], wr_raw[:, :, :], wr_hi[:, :, :].bitcast(F32), ALU.subtract).then_inc(w_lo_ready, 1)
                dve.wait_ge(mod_in, 64)
                dve.scalar_tensor_tensor(out=scale_b[:, :], in0=scale_b[:, :], scalar=1.0, in1=ng_b[:, :],
                                         op0=ALU.add, op1=ALU.mult).then_inc(mod_ready, 1)
                dve.wait_ge(mod_ready, 1)

                def tile(i, s, more):
                    n = i * RING + (s + 1)
                    dve.wait_ge(mm_done, n)
                    dve.wait_ge(x_out[s], 16 * i + 16)
                    dve.tensor_tensor(xo[:, s, :], psum_o[:, s, :], gate_b[:, :], ALU.mult).then_inc(gated, 1)
                    dve.wait_ge(gated, n)
                    dve.wait_ge(x_in[s], 16 * i + 16)
                    dve.tensor_tensor(xo[:, s, :], xo[:, s, :], xin[:, s, :], ALU.add).then_inc(xo_ready, 1)
                    if more:
                        split_h(n + RING, s)
                    dve.wait_ge(rstd_ready, n)
                    dve.scalar_tensor_tensor(out=u[:, s, :], in0=xo[:, s, :], scalar=rstd[:, s:s + 1], in1=scale_b[:, :],
                                             op0=ALU.mult, op1=ALU.mult).then_inc(um_ready, 1)
                    dve.wait_ge(u_hi_ready, n)
                    dve.tensor_tensor(u_lo[:, :, :], psum_t[:, :].rearrange("p (k t) -> p k t", k=KT), u_hi[:, :, :].bitcast(F32), ALU.subtract).then_inc(u_lo_ready, 1)

                with dve.Fori(0, LAST) as i:
                    for s in range(RING):
                        tile(i, s, True)
                for s in range(RING):
                    tile(LAST, s, False)

            @block.tensor
            def _(pe):
                def project(i, s, first):
                    n = i * RING + (s + 1)
                    pe.wait_ge(h_lo_ready, n)
                    if not first:
                        pe.wait_ge(gated, n - RING)
                    for h in range(2):
                        hs = slice(h * HALF, (h + 1) * HALF)
                        for k in range(KT):
                            if first and s == 0 and h == 0:
                                pe.wait_ge(w_lo_ready, k + 1)
                            last = split_mm(pe, psum_o[:, s, hs], (h_hi[:, s, k, :], h_lo[:, s, k, :]),
                                            (w_hi[:, k, hs], w_lo[:, k, hs]), k == 0, k == KT - 1)
                    last.then_inc(mm_done, 1)

                def route(i, s, first):
                    n = i * RING + (s + 1)
                    pe.wait_ge(u_ready, n)
                    if not first:
                        pe.wait_ge(u_lo_ready, n - 1)
                    for k in range(KT):
                        last = pe.transpose(psum_t[:, k * P:(k + 1) * P], u[:, s, k * P:(k + 1) * P], ident[:, :])
                    last.then_inc(tr_done, 1)

                def logit(i, s, first):
                    n = i * RING + (s + 1)
                    pe.wait_ge(u_lo_ready, n)
                    if not first:
                        pe.wait_ge(logits_ready, n - RING)
                    for k in range(KT):
                        last = split_mm(pe, psum_r[:, s, :], (u_hi[:, k, :], u_lo[:, k, :]), (wr_hi[:, k, :], wr_lo[:, k, :]), k == 0, k == KT - 1)
                    last.then_inc(r_done, 1)

                project(0, 0, True)
                project(0, 1, True)
                pe.wait_ge(w_lo_ready, KT + 1)
                route(0, 0, True)
                logit(0, 0, True)
                route(0, 1, False)
                logit(0, 1, True)
                with pe.Fori(1, NT // RING) as i:
                    for s in range(RING):
                        project(i, s, False)
                        route(i, s, False)
                        logit(i, s, False)


def routing(nc, layer, logits, b_router, pos, pair_w, starts, tok_idx):
    with Phase(nc, f"rt{layer}") as ph:
        brb = ph.sb("brb", [P, E])
        iot = ph.sb("iot", [P, 256], I32)
        tid_i = ph.sb("tid_i", [P, NT], I32)
        tid = ph.sb("tid", [P, NT])
        io128 = ph.sb("io128", [P, P])
        rev = ph.sb("rev", [P, E])
        thr = ph.sb("thr", [P, E])
        reset = ph.sb("reset", [P, E, NT])
        ones = ph.sb("ones", [P, P])
        before = ph.sb("before", [P, P])
        probs = ph.sb("probs", [P, NT, E])
        sel = ph.sb("sel", [P, NT, E])
        work = ph.sb("work", [P, NT, E])
        sums = ph.sb("sums", [P, NT * GROUPS, 2])
        maxs = ph.sb("maxs", [P, NT * GROUPS, 2])
        gs = ph.sb("gs", [P, NT, GROUPS])
        ing = ph.sb("ing", [P, NT, GROUPS])
        col = ph.sb("col", [P, NT])
        rec = ph.sb("rec", [P, NT])
        oh = ph.sb("oh", [P, 2, NT, E])
        mask = ph.sb("mask", [P, NT, E])
        tot = ph.sb("tot", [P, E, NT])
        incl = ph.sb("incl", [P, E, NT])
        gt = ph.sb("gt", [P, E, NT])
        tiles = ph.sb("tiles", [P, E])
        ends = ph.sb("ends", [P, E + 1])
        base = ph.sb("base", [P, E])
        posf = ph.sb("posf", [P, 2, NT])
        slot = ph.sb("slot", [P, NT, E])
        ai = ph.sb("ai", [P, 2, NT], I32)
        af = ph.sb("af", [P, 2, NT])
        bf = ph.sb("bf", [P, 2, NT])
        ob = ph.sb("ob", [P, 2 * NT, P])
        oa = ph.sb("oa", [P, 2 * NT, MAX_TILES])
        ps_rank = ph.ps("ps_rank", [P, NT, E])
        ps_tot = ph.ps("ps_tot", [P, NT, E])
        ps_tab = ph.ps("ps_tab", [P, MAX_TILES])
        br_in = ph.sem("br_in")
        iota_ready = ph.sem("iota_ready")
        step = ph.sem("step")
        centred = ph.sem("centred")
        exp_ready = ph.sem("exp_ready")
        mask_ready = ph.sem("mask_ready")
        counted = ph.sem("counted")
        hot_ready = ph.sem("hot_ready")
        tab_done = ph.sem("tab_done")

        with ph.block() as block:
            @block.sync
            def _(sp):
                sp.dma_start(brb[:, :], b_router.rearrange("(a e) -> a e", a=1).to_broadcast([P, E])).then_inc(br_in, 16)

            @block.gpsimd
            def _(pool):
                pool.iota(iot[:, :], pattern=[[1, 256]], base=0, channel_multiplier=0).then_inc(iota_ready, 1)
                pool.iota(tid_i[:, :], pattern=[[P, NT]], base=0, channel_multiplier=1).then_inc(iota_ready, 1)
                pool.memset(ones[:, :], 1.0).then_inc(iota_ready, 1)
                pool.memset(reset[:, :, :], 1.0).then_inc(iota_ready, 1)
                pool.wait_ge(iota_ready, 4)
                pool.affine_select(out=before[:, :], in_=ones[:, :], compare_op=ALU.is_gt, fill=0.0, base=0,
                                   pattern=[[1, P]], channel_multiplier=-1).then_inc(iota_ready, 1)
                pool.memset(reset[:, :, 0:1], 0.0).then_inc(iota_ready, 1)

            @block.scalar
            def _(act):
                act.wait_ge(centred, 1)
                act.activation(work[:, :, :], work[:, :, :], ACT.Exp).then_inc(exp_ready, 1)

            @block.vector
            def _(dve):
                count = [0]

                def link(ins):
                    count[0] += 1
                    ins.then_inc(step, 1)
                    dve.wait_ge(step, count[0])

                def over_e(x):
                    return x.unsqueeze(2).to_broadcast([P, NT, E])

                dve.wait_ge(iota_ready, 6)
                dve.wait_ge(br_in, 16)
                link(dve.tensor_copy(tid[:, :], tid_i[:, :]))
                link(dve.tensor_copy(io128[:, :], iot[:, 0:P]))
                link(dve.tensor_scalar(rev[:, :], io128[:, 0:E], -1.0, float(E), ALU.mult, ALU.add))
                link(dve.tensor_scalar(thr[:, :], io128[:, 0:E], float(P), None, ALU.mult))
                link(dve.tensor_reduce(col[:, :], logits[:, :, :], AX.X, ALU.max))
                dve.tensor_tensor(work[:, :, :], logits[:, :, :], over_e(col[:, :]), ALU.subtract).then_inc(centred, 1)
                dve.wait_ge(exp_ready, 1)
                link(dve.tensor_reduce(col[:, :], work[:, :, :], AX.X, ALU.add))
                link(dve.reciprocal(rec[:, :], col[:, :]))
                link(dve.tensor_tensor(probs[:, :, :], work[:, :, :], over_e(rec[:, :]), ALU.mult))
                link(dve.tensor_tensor(sel[:, :, :], probs[:, :, :], brb[:, :].unsqueeze(1).to_broadcast([P, NT, E]), ALU.add))
                pair = sel[:, :, :].rearrange("p t (g a b) -> p (t g a) b", g=GROUPS, a=2)
                link(dve.tensor_tensor(sums[:, :, :].rearrange("p g a -> p (g a)"), pair[:, :, 0], pair[:, :, 1], ALU.add))
                link(dve.tensor_tensor(maxs[:, :, :].rearrange("p g a -> p (g a)"), pair[:, :, 0], pair[:, :, 1], ALU.max))
                flat = gs[:, :, :].rearrange("p t g -> p (t g)")
                link(dve.tensor_tensor(flat, maxs[:, :, 0], maxs[:, :, 1], ALU.add))
                link(dve.tensor_tensor(flat, flat, sums[:, :, 0], ALU.max))
                link(dve.tensor_tensor(flat, flat, sums[:, :, 1], ALU.max))

                def first_max(out, x, n):
                    wide = lambda c: c.unsqueeze(2).to_broadcast([P, NT, n])
                    link(dve.tensor_reduce(col[:, :], x, AX.X, ALU.max))
                    link(dve.tensor_tensor(out, x, wide(col[:, :]), ALU.is_equal))
                    link(dve.tensor_tensor(out, out, rev[:, 0:n].unsqueeze(1).to_broadcast([P, NT, n]), ALU.mult))
                    link(dve.tensor_reduce(col[:, :], out, AX.X, ALU.max))
                    link(dve.tensor_tensor(out, out, wide(col[:, :]), ALU.is_equal))

                first_max(ing[:, :, :], gs[:, :, :], GROUPS)
                link(dve.tensor_scalar(ing[:, :, :], ing[:, :, :], 1.0, BIG, ALU.subtract, ALU.mult))
                link(dve.tensor_tensor(sel[:, :, :].rearrange("p t (g a) -> p (t g) a", g=GROUPS), sel[:, :, :].rearrange("p t (g a) -> p (t g) a", g=GROUPS),
                                       ing[:, :, :].rearrange("p t g -> p (t g)").unsqueeze(2).to_broadcast([P, NT * GROUPS, PER_G]), ALU.add))
                first_max(oh[:, 0, :, :], sel[:, :, :], E)
                link(dve.scalar_tensor_tensor(out=sel[:, :, :], in0=oh[:, 0, :, :], scalar=-4.0 * BIG, in1=sel[:, :, :], op0=ALU.mult, op1=ALU.add))
                first_max(oh[:, 1, :, :], sel[:, :, :], E)
                dve.tensor_tensor(mask[:, :, :], oh[:, 0, :, :], oh[:, 1, :, :], ALU.add).then_inc(mask_ready, 1)
                for j in range(2):
                    link(dve.tensor_tensor(work[:, :, :], probs[:, :, :], oh[:, j, :, :], ALU.mult))
                    link(dve.tensor_reduce(pair_w[:, j, :], work[:, :, :], AX.X, ALU.add))
                link(dve.tensor_tensor(col[:, :], pair_w[:, 0, :], pair_w[:, 1, :], ALU.add))
                link(dve.reciprocal(rec[:, :], col[:, :]))
                for j in range(2):
                    link(dve.tensor_tensor(pair_w[:, j, :], pair_w[:, j, :], rec[:, :], ALU.mult))
                dve.wait_ge(counted, 1)
                link(dve.tensor_copy(tot[:, :, :], ps_tot[:, :, :].rearrange("p t e -> p e t")))
                et = lambda x: x[:, :, :].rearrange("p e t -> p (e t)")
                link(dve.tensor_tensor_scan(et(incl), et(reset), et(tot), 0.0, ALU.mult, ALU.add))
                link(dve.tensor_tensor(tot[:, :, :], incl[:, :, :], tot[:, :, :], ALU.subtract))
                link(dve.tensor_tensor(gt[:, :, :], incl[:, :, NT - 1:NT].to_broadcast([P, E, NT]), thr[:, :].unsqueeze(1).to_broadcast([P, E, NT]), ALU.is_gt))
                link(dve.tensor_reduce(tiles[:, :], gt[:, :, :], AX.X, ALU.add))
                link(dve.tensor_scalar(tiles[:, :], tiles[:, :], 1.0, None, ALU.max))
                link(dve.memset(ends[:, 0:1], 0.0))
                link(dve.tensor_tensor_scan(ends[:, 1:E + 1], ones[:, 0:E], tiles[:, :], 0.0, ALU.mult, ALU.add))
                link(dve.tensor_copy(starts[0:1, :], ends[0:1, :]))
                link(dve.tensor_scalar(base[:, :], ends[:, 0:E], float(P), None, ALU.mult))
                link(dve.tensor_tensor(slot[:, :, :], ps_rank[:, :, :], tot[:, :, :].rearrange("p e t -> p t e"), ALU.add))
                link(dve.tensor_tensor(slot[:, :, :], slot[:, :, :], base[:, :].unsqueeze(1).to_broadcast([P, NT, E]), ALU.add))
                for j in range(2):
                    link(dve.tensor_tensor(work[:, :, :], slot[:, :, :], oh[:, j, :, :], ALU.mult))
                    link(dve.tensor_reduce(posf[:, j, :], work[:, :, :], AX.X, ALU.add))
                link(dve.tensor_copy(ai[:, :, :], posf[:, :, :]))
                link(dve.tensor_scalar(ai[:, :, :], ai[:, :, :], 7, None, ALU.arith_shift_right))
                link(dve.tensor_copy(af[:, :, :], ai[:, :, :]))
                link(dve.scalar_tensor_tensor(out=bf[:, :, :], in0=af[:, :, :], scalar=-float(P), in1=posf[:, :, :], op0=ALU.mult, op1=ALU.add))
                link(dve.tensor_scalar(pos[:, :, :], posf[:, :, :], float(P), None, ALU.add))
                pairs = lambda x: x[:, :, :].rearrange("p j t -> p (j t)").unsqueeze(2)
                link(dve.tensor_tensor(ob[:, :, :], io128[:, :].unsqueeze(1).to_broadcast([P, 2 * NT, P]), pairs(bf).to_broadcast([P, 2 * NT, P]), ALU.is_equal))
                link(dve.tensor_tensor(oa[:, :, :], io128[:, 0:MAX_TILES].unsqueeze(1).to_broadcast([P, 2 * NT, MAX_TILES]),
                                       pairs(af).to_broadcast([P, 2 * NT, MAX_TILES]), ALU.is_equal))
                for j in range(2):
                    link(dve.tensor_tensor(oa[:, j * NT:(j + 1) * NT, :], oa[:, j * NT:(j + 1) * NT, :], tid[:, :].unsqueeze(2).to_broadcast([P, NT, MAX_TILES]), ALU.mult))
                dve.sem_inc(hot_ready, 1)
                dve.wait_ge(tab_done, 1)
                dve.tensor_copy(tok_idx[:, :], ps_tab[:, :])

            @block.tensor
            def _(pe):
                pe.wait_ge(iota_ready, 6)
                pe.wait_ge(mask_ready, 1)
                flat = mask[:, :, :].rearrange("p t e -> p (t e)")
                pe.matmul(ps_rank[:, :, :].rearrange("p t e -> p (t e)"), before[:, :], flat, start=True, stop=True)
                pe.matmul(ps_tot[:, :, :].rearrange("p t e -> p (t e)"), ones[:, :], flat, start=True, stop=True).then_inc(counted, 1)
                pe.wait_ge(hot_ready, 1)
                for m in range(2 * NT):
                    last = pe.matmul(ps_tab[:, :], ob[:, m, :], oa[:, m, :], start=(m == 0), stop=(m == 2 * NT - 1))
                last.then_inc(tab_done, 1)


def experts(nc, layer, u_src, w_gate, w_up, w_down, starts, tok_idx, ys, ident):
    WG = 4
    WD = 4
    NCH = 2 * WG + WD
    RAW = 6
    with Phase(nc, f"ex{layer}") as ph:
        w_raw = ph.sb("w_raw", [P, RAW, D])
        w_hi = ph.sb("w_hi", [P, NCH, D], F32R)
        w_lo = ph.sb("w_lo", [P, NCH, D], F32R)
        idx = ph.sb("idx", [P, 1], I32)
        rows = ph.sb("rows", [P, D])
        u_hi = ph.sb("u_hi", [P, KT, P], F32R)
        u_lo = ph.sb("u_lo", [P, KT, P], F32R)
        sig = ph.sb("sig", [P, DE])
        a = ph.sb("a", [P, DE])
        a_hi = ph.sb("a_hi", [P, FT, P], F32R)
        a_lo = ph.sb("a_lo", [P, FT, P], F32R)
        out = ph.sb("out", [P, D])
        ps_u = ph.ps("ps_u", [P, D])
        ps_g = ph.ps("ps_g", [P, 2, DE])
        ps_a = ph.ps("ps_a", [P, DE])
        ps_o = ph.ps("ps_o", [P, D])
        raw_in = [ph.sem(f"raw_in{s}") for s in range(RAW)]
        whi_ready = ph.sem("whi_ready")
        wlo_ready = ph.sem("wlo_ready")
        idx_ready = ph.sem("idx_ready")
        rows_in = ph.sem("rows_in")
        passed = ph.sem("passed")
        tr_done = ph.sem("tr_done")
        uhi_ready = ph.sem("uhi_ready")
        ulo_ready = ph.sem("ulo_ready")
        gate_done = ph.sem("gate_done")
        up_done = ph.sem("up_done")
        sig_ready = ph.sem("sig_ready")
        gated = ph.sem("gated")
        a_ready = ph.sem("a_ready")
        at_done = ph.sem("at_done")
        ahi_ready = ph.sem("ahi_ready")
        alo_ready = ph.sem("alo_ready")
        down_done = ph.sem("down_done")
        out_ready = ph.sem("out_ready")
        out_done = ph.sem("out_done")

        def bounds(eng, e):
            return (eng.value_load(starts[0:1, bass.ds(e, 1)], min_val=0, max_val=MAX_TILES - 1),
                    eng.value_load(starts[0:1, bass.ds(e + 1, 1)], min_val=1, max_val=MAX_TILES - 1))

        with ph.block() as block:
            @block.sync
            def _(sp):
                def load(e, c, first):
                    if c < 2 * WG:
                        w = w_gate if c < WG else w_up
                        k = 2 * (c % WG)
                        src = w[layer, bass.ds(e, 1), k * P:(k + 2) * P, :].rearrange("a (k p) n -> p (a k) n", p=P)
                        dst = w_raw[:, c % RAW, :].rearrange("p (k n) -> p k n", k=2)
                    else:
                        f = c - 2 * WG
                        src = w_down[layer, bass.ds(e, 1), f * P:(f + 1) * P, :].rearrange("a p n -> p (a n)")
                        dst = w_raw[:, c % RAW, :]
                    if not first:
                        sp.wait_ge(wlo_ready, e * NCH + (c - RAW + 1))
                    sp.dma_start(dst, src).then_inc(raw_in[c % RAW], 16)

                for c in range(NCH):
                    load(0, c, c < RAW)
                with sp.Fori(1, E) as e:
                    for c in range(NCH):
                        load(e, c, False)

            @block.gpsimd
            def _(pool):
                pool.memset(out[:, :], 0.0).then_inc(idx_ready, 1)

                def fetch(t):
                    pool.tensor_copy(idx[:, :], tok_idx[:, bass.ds(t, 1)]).then_inc(idx_ready, 1)
                    pool.wait_ge(idx_ready, t + 2)
                    stand(pool, passed)
                    pool.indirect_dma_start(rows[:, :], None, u_src, bass.IndirectOffsetOnAxis(ap=idx[:, 0:1], axis=0)).then_inc(rows_in, 16)
                    pool.wait_ge(rows_in, t * 16 + 16)
                    pool.wait_ge(tr_done, t + 1)

                fetch(0)
                with pool.Fori(0, E) as e:
                    first, end = bounds(pool, e)
                    with pool.Fori(first, end) as t:
                        fetch(t + 1)

            @block.scalar
            def _(act):
                act.sem_inc(out_done, 16)

                def split_w(e, c):
                    act.wait_ge(raw_in[c % RAW], e * (16 * NCH // RAW) + 16 * (c // RAW + 1))
                    act.activation(w_hi[:, c, :], w_raw[:, c % RAW, :], ACT.Copy).then_inc(whi_ready, 1)

                def split_u(t):
                    act.wait_ge(tr_done, t + 1)
                    act.activation(u_hi[:, :, :].rearrange("p k t -> p (k t)"), ps_u[:, :], ACT.Copy).then_inc(uhi_ready, 1)

                def store(t):
                    act.wait_ge(down_done, t + 1)
                    act.wait_ge(out_done, t * 16 + 16)
                    act.activation(out[:, :], ps_o[:, :], ACT.Copy).then_inc(out_ready, 1)
                    act.wait_ge(out_ready, t + 1)
                    act.dma_start(ys[bass.ds(t * P, P), :], out[:, :]).then_inc(out_done, 16)

                split_u(0)
                for c in range(NCH):
                    split_w(0, c)

                def tile(t):
                    act.wait_ge(gate_done, t + 1)
                    act.activation(sig[:, :], ps_g[:, 0, :], ACT.Sigmoid).then_inc(sig_ready, 1)
                    store(t)
                    act.wait_ge(at_done, t + 1)
                    act.activation(a_hi[:, :, :].rearrange("p f t -> p (f t)"), ps_a[:, :], ACT.Copy).then_inc(ahi_ready, 1)
                    split_u(t + 1)

                with act.Fori(0, E - 1) as e:
                    first, end = bounds(act, e)
                    with act.Fori(first, end) as t:
                        tile(t)
                    for c in range(NCH):
                        if c == 2 * WG:
                            act.wait_ge(down_done, end + 1)
                        split_w(e + 1, c)
                first, end = bounds(act, E - 1)
                with act.Fori(first, end) as t:
                    tile(t)
                store(end)
                act.wait_ge(out_done, end * 16 + 32)
                stand(act, passed)

            @block.vector
            def _(dve):
                def split_w(e, c):
                    dve.wait_ge(whi_ready, e * NCH + (c + 1))
                    dve.tensor_tensor(w_lo[:, c, :], w_raw[:, c % RAW, :], w_hi[:, c, :].bitcast(F32), ALU.subtract).then_inc(wlo_ready, 1)

                def split_u(t):
                    dve.wait_ge(uhi_ready, t + 1)
                    dve.tensor_tensor(u_lo[:, :, :].rearrange("p k t -> p (k t)"), ps_u[:, :], u_hi[:, :, :].rearrange("p k t -> p (k t)").bitcast(F32),
                                      ALU.subtract).then_inc(ulo_ready, 1)

                split_u(0)
                for c in range(NCH):
                    split_w(0, c)

                def tile(t):
                    dve.wait_ge(sig_ready, t + 1)
                    dve.tensor_tensor(sig[:, :], sig[:, :], ps_g[:, 0, :], ALU.mult).then_inc(gated, 1)
                    dve.wait_ge(gated, t + 1)
                    dve.wait_ge(up_done, t + 1)
                    dve.tensor_tensor(a[:, :], sig[:, :], ps_g[:, 1, :], ALU.mult).then_inc(a_ready, 1)
                    dve.wait_ge(ahi_ready, t + 1)
                    dve.tensor_tensor(a_lo[:, :, :].rearrange("p f t -> p (f t)"), ps_a[:, :], a_hi[:, :, :].rearrange("p f t -> p (f t)").bitcast(F32),
                                      ALU.subtract).then_inc(alo_ready, 1)
                    split_u(t + 1)

                with dve.Fori(0, E - 1) as e:
                    first, end = bounds(dve, e)
                    with dve.Fori(first, end) as t:
                        tile(t)
                    for c in range(NCH):
                        split_w(e + 1, c)
                first, end = bounds(dve, E - 1)
                with dve.Fori(first, end) as t:
                    tile(t)

            @block.tensor
            def _(pe):
                def transpose_rows(t):
                    pe.wait_ge(rows_in, t * 16 + 16)
                    for k in range(KT):
                        last = pe.transpose(ps_u[:, k * P:(k + 1) * P], rows[:, k * P:(k + 1) * P], ident[:, :])
                    last.then_inc(tr_done, 1)

                def up_or_gate(e, which, t):
                    for k in range(KT):
                        c = which * WG + k // 2
                        if k % 2 == 0:
                            pe.wait_ge(wlo_ready, e * NCH + (c + 1))
                        ws = slice((k % 2) * DE, (k % 2 + 1) * DE)
                        last = split_mm(pe, ps_g[:, which, :], (u_hi[:, k, :], u_lo[:, k, :]), (w_hi[:, c, ws], w_lo[:, c, ws]), k == 0, k == KT - 1)
                    return last

                def tile(e, t):
                    pe.wait_ge(ulo_ready, t + 1)
                    up_or_gate(e, 0, t).then_inc(gate_done, 1)
                    up_or_gate(e, 1, t).then_inc(up_done, 1)
                    transpose_rows(t + 1)
                    pe.wait_ge(a_ready, t + 1)
                    for f in range(FT):
                        last = pe.transpose(ps_a[:, f * P:(f + 1) * P], a[:, f * P:(f + 1) * P], ident[:, :])
                    last.then_inc(at_done, 1)
                    pe.wait_ge(alo_ready, t + 1)
                    pe.wait_ge(out_ready, t + 1)
                    for h in range(2):
                        hs = slice(h * HALF, (h + 1) * HALF)
                        for f in range(FT):
                            c = 2 * WG + f
                            if h == 0:
                                pe.wait_ge(wlo_ready, e * NCH + (c + 1))
                            last = split_mm(pe, ps_o[:, hs], (a_hi[:, f, :], a_lo[:, f, :]), (w_hi[:, c, hs], w_lo[:, c, hs]), f == 0, f == FT - 1)
                    last.then_inc(down_done, 1)

                pe.wait_ge(idx_ready, 1)
                for h in range(2):
                    last = pe.matmul(ps_o[:, h * HALF:(h + 1) * HALF], ident[:, :], out[:, h * HALF:(h + 1) * HALF], start=True, stop=True)
                last.then_inc(down_done, 1)
                transpose_rows(0)
                with pe.Fori(0, E) as e:
                    first, end = bounds(pe, e)
                    with pe.Fori(first, end) as t:
                        tile(e, t)


def final(nc, x_src, ys, pos, pair_w, gate_row, final_g, out):
    with Phase(nc, "fin") as ph:
        xin = ph.sb("xin", [P, RING, D])
        row_a = ph.sb("row_a", [P, RING, D])
        row_b = ph.sb("row_b", [P, RING, D])
        yo = ph.sb("yo", [P, RING, D])
        gate_b = ph.sb("gate_b", [P, D])
        fg_b = ph.sb("fg_b", [P, D])
        ssq = ph.sb("ssq", [P, RING])
        rstd = ph.sb("rstd", [P, RING])
        mhalf = ph.sb("mhalf", [P, 1])
        idx = ph.sb("idx", [P, RING, 2], I32)
        wts = ph.sb("wts", [P, RING, 2])
        vec_in = ph.sem("vec_in")
        const_ready = ph.sem("const_ready")
        x_in = [ph.sem(f"x_in{s}") for s in range(RING)]
        rows_in = [ph.sem(f"rows_in{s}") for s in range(RING)]
        idx_ready = ph.sem("idx_ready")
        wts_ready = ph.sem("wts_ready")
        ra_ready = ph.sem("ra_ready")
        rb_ready = ph.sem("rb_ready")
        mix_ready = ph.sem("mix_ready")
        x2_ready = ph.sem("x2_ready")
        ssq_ready = ph.sem("ssq_ready")
        var_ready = ph.sem("var_ready")
        rstd_ready = ph.sem("rstd_ready")
        passed = ph.sem("passed")
        y_ready = ph.sem("y_ready")
        y_out = [ph.sem(f"y_out{s}") for s in range(RING)]
        LAST = NT // RING - 1

        with ph.block() as block:
            @block.sync
            def _(sp):
                def load(n, s):
                    sp.dma_start(xin[:, s, :], x_src[bass.ds(n * P, P), :]).then_inc(x_in[s], 16)

                def tile(i, s, more):
                    n = i * RING + (s + 1)
                    sp.wait_ge(y_ready, n)
                    sp.dma_start(out[0, bass.ds(i * (RING * P) + s * P, P), :], yo[:, s, :]).then_inc(y_out[s], 16)
                    if more:
                        load(i * RING + (RING + s), s)

                for s in range(RING):
                    load(s, s)
                sp.dma_start(gate_b[:, :], rowcast(gate_row)).then_inc(vec_in, 16)
                sp.dma_start(fg_b[:, :], final_g.rearrange("(a d) -> a d", a=1).to_broadcast([P, D])).then_inc(vec_in, 16)
                with sp.Fori(0, LAST) as i:
                    for s in range(RING):
                        tile(i, s, True)
                for s in range(RING):
                    tile(LAST, s, False)
                for s in range(RING):
                    sp.wait_ge(y_out[s], 16 * (LAST + 2))

            @block.gpsimd
            def _(pool):
                pool.memset(mhalf[:, :], -0.5).then_inc(const_ready, 1)
                pool.wait_ge(const_ready, 1)

                def gather(n, s, count):
                    for j in range(2):
                        pool.tensor_copy(idx[:, s, j:j + 1], pos[:, j, bass.ds(n, 1)]).then_inc(idx_ready, 1)
                    pool.wait_ge(idx_ready, count)
                    stand(pool, passed)
                    for j, dst in enumerate((row_a, row_b)):
                        pool.indirect_dma_start(dst[:, s, :], None, ys, bass.IndirectOffsetOnAxis(ap=idx[:, s, j:j + 1], axis=0)).then_inc(rows_in[s], 16)

                def tile(i, s, more):
                    n = i * RING + (s + 1)
                    pool.wait_ge(mix_ready, n)
                    pool.wait_ge(x_in[s], 16 * i + 16)
                    pool.tensor_tensor(xin[:, s, :], xin[:, s, :], row_b[:, s, :], ALU.add).then_inc(x2_ready, 1)
                    pool.wait_ge(ssq_ready, n)
                    if more:
                        gather(i * RING + (RING + s), s, i * (2 * RING) + 2 * (RING + s + 1))
                    stand(pool, passed)
                    pool.tensor_scalar(rstd[:, s:s + 1], ssq[:, s:s + 1], 1.0 / D, EPS, ALU.mult, ALU.add).then_inc(var_ready, 1)
                    pool.wait_ge(var_ready, n)
                    pool.tensor_tensor(rstd[:, s:s + 1], rstd[:, s:s + 1], mhalf[:, 0:1], ALU.pow).then_inc(rstd_ready, 1)

                for s in range(RING):
                    gather(s, s, 2 * (s + 1))
                with pool.Fori(0, LAST) as i:
                    for s in range(RING):
                        tile(i, s, True)
                for s in range(RING):
                    tile(LAST, s, False)

            @block.scalar
            def _(act):
                for s in range(RING):
                    act.sem_inc(y_out[s], 16)
                with act.Fori(0, NT // RING) as i:
                    for s in range(RING):
                        n = i * RING + (s + 1)
                        act.wait_ge(rows_in[s], 32 * i + 32)
                        act.wait_ge(wts_ready, n)
                        act.activation(row_a[:, s, :], row_a[:, s, :], ACT.Copy, scale=wts[:, s, 0:1]).then_inc(ra_ready, 1)
                        act.wait_ge(x2_ready, n)
                        act.wait_ge(y_out[s], 16 * i + 16)
                        act.activation(yo[:, s, :], xin[:, s, :], ACT.Square, accum_out=ssq[:, s:s + 1]).then_inc(ssq_ready, 1)

            @block.vector
            def _(dve):
                dve.wait_ge(vec_in, 32)
                with dve.Fori(0, NT // RING) as i:
                    for s in range(RING):
                        n = i * RING + (s + 1)
                        dve.tensor_copy(wts[:, s, :], pair_w[:, :, bass.ds(i * RING + s, 1)].rearrange("p j a -> p (j a)")).then_inc(wts_ready, 1)
                        dve.wait_ge(wts_ready, n)
                        dve.wait_ge(ra_ready, n)
                        dve.scalar_tensor_tensor(out=row_b[:, s, :], in0=row_b[:, s, :], scalar=wts[:, s, 1:2], in1=row_a[:, s, :],
                                                 op0=ALU.mult, op1=ALU.add).then_inc(rb_ready, 1)
                        dve.wait_ge(rb_ready, n)
                        dve.tensor_tensor(row_b[:, s, :], row_b[:, s, :], gate_b[:, :], ALU.mult).then_inc(mix_ready, 1)
                        dve.wait_ge(rstd_ready, n)
                        dve.scalar_tensor_tensor(out=yo[:, s, :], in0=xin[:, s, :], scalar=rstd[:, s:s + 1], in1=fg_b[:, :],
                                                 op0=ALU.mult, op1=ALU.mult).then_inc(y_ready, 1)


def trunk(nc, x, c, norm1_g, norm2_g, w_ada, b_ada, m_w_in, m_b_gates, m_norm_g, m_w_out,
          c_w_in, c_conv_w, c_conv_b, c_w_out, w_router, b_router, e_w_gate, e_w_up, e_w_down, final_g, out):
    dram = lambda name, shape: nc.dram_tensor(name, shape, F32, kind="Internal").ap()
    mod_rows = dram("mod_rows", (2, 6, D))
    x1 = dram("x1", (T, D))
    x2 = dram("x2", (T, D))
    u2 = dram("u2", (T, D))
    ys = dram("ys", (MAX_TILES * P, D))
    proj_t = dram("proj_t", (NCOL, T))
    gates_t = dram("gates_t", (2 * HEADS, T))
    h_t = dram("h_t", (D, T))
    gate_d = (dram("ends_d", (HEADS * NT, 2)), dram("seq_d", (HEADS * NT, 1)), dram("rows_d", (HEADS * NT, 2 * P)), dram("decay_d", (HEADS * NT, 1)))

    with ExitStack() as ctx:
        sb = lambda name, shape, dt=F32: ctx.enter_context(nc.sbuf_tensor(name, shape, dt))
        ident = sb("ident", [P, P])
        logits = sb("logits", [P, NT, E])
        pos = sb("pos", [P, 2, NT], I32)
        pair_w = sb("pair_w", [P, 2, NT])
        starts = sb("starts", [1, E + 1], I32)
        tok_idx = sb("tok_idx", [P, MAX_TILES], I32)

        adaln(nc, c, w_ada, b_ada, mod_rows, ident)
        for layer in range(2):
            if layer == 0:
                in_proj(nc, 0, x[0, :, :], None, norm1_g, mod_rows, m_w_in[0, :, :], proj_t, ident, gates=(m_b_gates, gates_t), blank=ys)
                mlstm(nc, proj_t, gates_t, gate_d, m_norm_g, h_t, ident)
                out_proj(nc, 0, h_t, m_w_out[0, :, :], x[0, :, :], x1, u2, norm2_g, mod_rows, w_router, logits, ident)
            else:
                in_proj(nc, 1, x1, x2, norm1_g, mod_rows, c_w_in[0, :, :], h_t, ident,
                        combine=(ys, pos, pair_w, mod_rows[0, 5:6, :]), conv=(c_conv_w, c_conv_b))
                out_proj(nc, 1, h_t, c_w_out[0, :, :], x2, x1, u2, norm2_g, mod_rows, w_router, logits, ident)
            routing(nc, layer, logits, b_router, pos, pair_w, starts, tok_idx)
            experts(nc, layer, u2, e_w_gate, e_w_up, e_w_down, starts, tok_idx, ys, ident)
        final(nc, x1, ys, pos, pair_w, mod_rows[1, 5:6, :], final_g, out)


_INS = ["x", "c", "norm1_g", "norm2_g", "w_ada", "b_ada", "m_w_in", "m_b_gates", "m_norm_g", "m_w_out",
        "c_w_in", "c_conv_w", "c_conv_b", "c_w_out", "w_router", "b_router", "e_w_gate", "e_w_up", "e_w_down", "final_g"]


def kernel(**inputs):
    import numpy as _np
    import concourse.bacc as _bacc
    from concourse.bass_utils import run_bass_kernel_spmd as _run

    nc = _bacc.Bacc("TRN2", target_bir_lowering=False, num_devices=1)
    arrays, args = {}, []
    for name in _INS:
        a = _np.ascontiguousarray(inputs[name])
        arrays[f"in_{name}_dram"] = a
        args.append(nc.dram_tensor(f"in_{name}_dram", a.shape, mybir.dt.from_np(a.dtype), kind="ExternalInput").ap())
    args.append(nc.dram_tensor("out_0_dram", (1, T, D), F32, kind="ExternalOutput").ap())
    trunk(nc, *args)
    r = _run(nc, [arrays], core_ids=[0])
    return r.results[0]["out_0_dram"]
```

```python
import concourse.bass as bass
from concourse import mybir
from contextlib import ExitStack

F32 = mybir.dt.float32
F32R = mybir.dt.float32r
I32 = mybir.dt.int32
ACT = mybir.ActivationFunctionType
ALU = mybir.AluOpType
AX = mybir.AxisListType

P = 128
D = 1024
T = 2048
KT = D // P
NT = T // P
HALF = 512
NBLK = T // HALF
HEADS = 4
DQK = 128
DV = 256
NCOL = 3 * D
NCHUNK = NCOL // P
E = 16
GROUPS = 4
PER_G = E // GROUPS
DE = 512
FT = DE // P
MAX_TILES = 48
EPS = 1e-6
BIG = 1e30
RING = 2


class Phase:

    def __init__(self, nc, name):
        self.nc, self.name, self.stack, self.sems = nc, name, ExitStack(), []

    def __enter__(self):
        self.stack.__enter__()
        return self

    def __exit__(self, *a):
        self.nc.clear_and_free_semaphores(self.sems)
        self.nc.all_engine_barrier()
        return self.stack.__exit__(*a)

    def sb(self, name, shape, dt=F32):
        return self.stack.enter_context(self.nc.sbuf_tensor(f"{self.name}_{name}", shape, dt))

    def ps(self, name, shape):
        return self.stack.enter_context(self.nc.psum_tensor(f"{self.name}_{name}", shape, F32))

    def sem(self, name):
        self.sems.append(self.nc.alloc_semaphore(f"{self.name}_{name}"))
        return self.sems[-1]

    def block(self):
        return self.nc.Block()


def split_mm(pe, out, lhs, rhs, start, stop):
    pe.matmul(out, lhs[0], rhs[0], start=start, stop=False)
    pe.matmul(out, lhs[0], rhs[1], start=False, stop=False)
    return pe.matmul(out, lhs[1], rhs[0], start=False, stop=stop)


def stand(eng, passed):
    eng.sem_inc(passed, 1)


def upto(i, s, n=0):
    return i * RING + (s + n + 1)


def slot(s, n=0):
    return (s + n) % RING


def uses(i, s, n=0):
    return i + ((s + n) // RING + 1)


def live(i, s, n=0):
    return not isinstance(i, int) or 0 <= i * RING + s + n < NT


def skewed(eng, step, head=2, behind=2, ahead=1):
    for i in range(head):
        for s in range(RING):
            step(i, s)
    with eng.Fori(head, NT // RING - ahead) as i:
        for s in range(RING):
            step(i, s)
    for i in range(NT // RING - ahead, NT // RING + behind):
        for s in range(RING):
            step(i, s)


def cols(ap):
    return ap.rearrange("(k p) -> p k", p=P)


def rowcast(ap):
    return ap.to_broadcast([P, ap.shape[1]])


def adaln(nc, c, w_ada, b_ada, mod_rows, ident):
    with Phase(nc, "ada") as ph:
        ccol = ph.sb("ccol", [P, KT])
        sig = ph.sb("sig", [P, KT])
        cond = ph.sb("cond", [P, KT])
        ones = ph.sb("ones", [P, 1])
        w = ph.sb("w", [P, RING, KT, D])
        bias = ph.sb("bias", [1, RING, D])
        acc = ph.sb("acc", [P, RING, D])
        row = ph.sb("row", [1, RING, D])
        psum = ph.ps("psum", [P, RING, D])
        c_in = ph.sem("c_in")
        w_in = [ph.sem(f"w_in{s}") for s in range(RING)]
        sig_ready = ph.sem("sig_ready")
        cond_ready = ph.sem("cond_ready")
        ones_ready = ph.sem("ones_ready")
        mac = ph.sem("mac")
        w_used = ph.sem("w_used")
        acc_ready = ph.sem("acc_ready")
        sum_ready = ph.sem("sum_ready")
        row_ready = ph.sem("row_ready")
        row_out = [ph.sem(f"row_out{s}") for s in range(RING)]
        id0 = ph.sem("id0")
        GR = 6

        with ph.block() as block:
            @block.sync
            def _(sp):
                with nc.allow_non_contiguous_dma(reason="4 KB vector laid over the partitions"):
                    sp.dma_start(ccol[:, :], cols(c[0, :])).then_inc(c_in, 16)
                for layer in range(2):
                    with sp.Fori(0, GR // RING) as i:
                        for s in range(RING):
                            sp.wait_ge(w_used, RING * i + (layer * GR + s + 1))
                            src = w_ada[layer, :, bass.ds((RING * i + s) * D, D)]
                            sp.dma_start(w[:, s, :, :], src.rearrange("(k p) n -> p k n", p=P)).then_inc(w_in[s], 16)
                            sp.dma_start(bias[0:1, s, :], b_ada[layer:layer + 1, bass.ds((RING * i + s) * D, D)]).then_inc(w_in[s], 16)

            @block.gpsimd
            def _(pool):
                pool.memset(ones[:, :], 1.0).then_inc(ones_ready, 1)
                pool.memset(ident[:, :], 0.0).then_inc(id0, 1)
                pool.wait_ge(id0, 1)
                pool.affine_select(out=ident[:, :], in_=ident[:, :], compare_op=ALU.not_equal, fill=1.0,
                                   base=0, pattern=[[-1, P]], channel_multiplier=1).then_inc(id0, 1)
                pool.wait_ge(id0, 2)

            @block.scalar
            def _(act):
                act.wait_ge(c_in, 16)
                act.activation(sig[:, :], ccol[:, :], ACT.Sigmoid).then_inc(sig_ready, 1)
                for s in range(RING):
                    act.sem_inc(row_out[s], 16)
                for layer in range(2):
                    with act.Fori(0, GR // RING) as i:
                        for s in range(RING):
                            act.wait_ge(row_ready, RING * i + (layer * GR + s + 1))
                            act.dma_start(mod_rows[layer, bass.ds(RING * i + s, 1), :], row[0:1, s, :]).then_inc(row_out[s], 16)
                for s in range(RING):
                    act.wait_ge(row_out[s], 16 * (GR + 1))

            @block.vector
            def _(dve):
                dve.sem_inc(w_used, RING)
                dve.wait_ge(sig_ready, 1)
                dve.tensor_tensor(cond[:, :], ccol[:, :], sig[:, :], ALU.mult).then_inc(cond_ready, 1)
                dve.wait_ge(cond_ready, 1)
                for layer in range(2):
                    with dve.Fori(0, GR // RING) as i:
                        for s in range(RING):
                            dve.wait_ge(w_in[s], 32 * i + 32 * (layer * (GR // RING) + 1))
                            for k in range(KT):
                                if k == 0:
                                    ins = dve.tensor_scalar(acc[:, s, :], w[:, s, k, :], cond[:, k:k + 1], None, ALU.mult)
                                else:
                                    dve.wait_ge(mac, (KT - 1) * (RING * i) + (KT - 1) * (layer * GR + s) + k)
                                    ins = dve.scalar_tensor_tensor(out=acc[:, s, :], in0=w[:, s, k, :], scalar=cond[:, k:k + 1],
                                                                   in1=acc[:, s, :], op0=ALU.mult, op1=ALU.add)
                                if k < KT - 1:
                                    ins.then_inc(mac, 1)
                            ins.then_inc(acc_ready, 1)
                            dve.wait_ge(acc_ready, RING * i + (layer * GR + s + 1))
                            dve.wait_ge(sum_ready, RING * i + (layer * GR + s + 1))
                            dve.wait_ge(row_out[s], 16 * i + 16 * (layer * (GR // RING) + 1))
                            dve.tensor_tensor(row[0:1, s, :], psum[0:1, s, :], bias[0:1, s, :], ALU.add).then_inc(row_ready, 1)
                            dve.wait_ge(row_ready, RING * i + (layer * GR + s + 1))
                            dve.sem_inc(w_used, 1)

            @block.tensor
            def _(pe):
                pe.wait_ge(ones_ready, 1)
                for layer in range(2):
                    with pe.Fori(0, GR // RING) as i:
                        for s in range(RING):
                            pe.wait_ge(acc_ready, RING * i + (layer * GR + s + 1))
                            for h in range(2):
                                last = pe.matmul(psum[0:1, s, h * HALF:(h + 1) * HALF], ones[:, 0:1],
                                                 acc[:, s, h * HALF:(h + 1) * HALF], start=True, stop=True)
                            last.then_inc(sum_ready, 1)


def in_proj(nc, layer, x_src, x_dst, norm_g, mod_rows, w_in, out_t, ident, combine=None, gates=None, conv=None, blank=None):
    with Phase(nc, f"in{layer}") as ph:
        u_hi = ph.sb("u_hi", [P, KT, T], F32R)
        u_lo = ph.sb("u_lo", [P, KT, T], F32R)
        w_raw = ph.sb("w_raw", [P, RING, KT, P])
        w_hi = ph.sb("w_hi", [P, RING, KT, P], F32R)
        w_lo = ph.sb("w_lo", [P, RING, KT, P], F32R)
        work = ph.sb("work", [P, (11 if combine else 9) * D])
        junk = ph.sb("junk", [P, D])
        view = lambda at, n: work[:, at * D:(at + n) * D]
        xin = view(0, 2).rearrange("p (s d) -> p s d", s=RING)
        row_a = view(2, 2).rearrange("p (s d) -> p s d", s=RING)
        row_b = view(4, 2).rearrange("p (s d) -> p s d", s=RING)
        u = view(9, 2).rearrange("p (s d) -> p s d", s=RING) if combine else row_a
        ng_b = view(10, 1) if combine else view(3, 1)
        scale_b, shift_b, gate_b = view(6, 1), view(7, 1), view(8, 1)
        stage = view(0, 4).rearrange("p (s t) -> p s t", s=RING)
        gate_rows = view(4, 2)
        c_rows = view(4, 2)
        z_rows = work[:, 6 * D:6 * D + 2 + T]
        ssq = ph.sb("ssq", [P, RING])
        rstd = ph.sb("rstd", [P, RING])
        mhalf = ph.sb("mhalf", [P, 1])
        idx = ph.sb("idx", [P, RING, 2], I32)
        wts = ph.sb("wts", [P, RING, 2])
        psum_t = ph.ps("psum_t", [P, RING, D])
        psum_o = ph.ps("psum_o", [P, NBLK, HALF])
        mod_in = ph.sem("mod_in")
        mod_ready = ph.sem("mod_ready")
        x_in = [ph.sem(f"x_in{s}") for s in range(RING)]
        ssq_ready = ph.sem("ssq_ready")
        var_ready = ph.sem("var_ready")
        rstd_ready = ph.sem("rstd_ready")
        passed = ph.sem("passed")
        um_ready = ph.sem("um_ready")
        u_ready = ph.sem("u_ready")
        tr_done = ph.sem("tr_done")
        hi_done = ph.sem("hi_done")
        lo_done = ph.sem("lo_done")
        const_ready = ph.sem("const_ready")
        wr_in = [ph.sem(f"wr_in{s}") for s in range(RING)]
        w_hi_ready = ph.sem("w_hi_ready")
        w_lo_ready = ph.sem("w_lo_ready")
        blk_done = ph.sem("blk_done")
        ev_act = ph.sem("ev_act")
        out_done = [ph.sem(f"out_done{s}") for s in range(RING)]
        if combine:
            ys, pos, pair_w, gate_row = combine
            rows_in = [ph.sem(f"rows_in{s}") for s in range(RING)]
            idx_ready = ph.sem("idx_ready")
            wts_ready = ph.sem("wts_ready")
            ra_ready = ph.sem("ra_ready")
            rb_ready = ph.sem("rb_ready")
            mix_ready = ph.sem("mix_ready")
            gate_in = ph.sem("gate_in")
            x2_ready = ph.sem("x2_ready")
            x_out = [ph.sem(f"x_out{s}") for s in range(RING)]
        if blank is not None:
            zero = ph.sb("zero", [P, D])
            zero_ready = ph.sem("zero_ready")
            blank_out = ph.sem("blank_out")
        if gates:
            b_gates, gates_t = gates
            gw_raw = ph.sb("gw_raw", [P, KT, 8])
            gw_hi = ph.sb("gw_hi", [P, KT, 8], F32R)
            gw_lo = ph.sb("gw_lo", [P, KT, 8], F32R)
            gbias = ph.sb("gbias", [8, 1])
            gw_in = ph.sem("gw_in")
            gw_ready = ph.sem("gw_ready")
            gates_ev = ph.sem("gates_ev")
            gates_out = ph.sem("gates_out")
        if conv:
            conv_w, conv_b = conv
            taps = ph.sb("taps", [P, KT, 4])
            tap = ph.sb("tap", [P, RING, 4])
            taps_in = ph.sem("taps_in")
            tap_ready = ph.sem("tap_ready")
            z_ready = ph.sem("z_ready")
            zc_ready = ph.sem("zc_ready")
            y_ready = ph.sem("y_ready")
        m_scale, m_shift = 1, 0
        CH = 6 if conv else 2
        if conv:
            kind_at = (D, 2 * D, 0)
            chunk_col = lambda i, q: kind_at[q % 3] + P * (q // 3) + i * (2 * P)
        else:
            chunk_col = lambda i, q: i * (CH * P) + q * P
        BODIES = NCHUNK // CH
        UM, HI, LO = (-1, -2, -3) if combine else (0, -1, -1)

        with ph.block() as block:
            @block.sync
            def _(sp):
                def load_x(n, s):
                    sp.dma_start(xin[:, s, :], x_src[bass.ds(n * P, P), :]).then_inc(x_in[s], 16)

                def load_w(col, s):
                    src = w_in[:, bass.ds(col, P)].rearrange("(k p) n -> p k n", p=P)
                    sp.dma_start(w_raw[:, s, :, :], src).then_inc(wr_in[s], 16)

                load_x(0, 0)
                sp.dma_start(scale_b, rowcast(mod_rows[layer, m_scale:m_scale + 1, :])).then_inc(mod_in, 16)
                sp.dma_start(ng_b, rowcast(norm_g[layer:layer + 1, :])).then_inc(mod_in, 16)
                sp.dma_start(shift_b, rowcast(mod_rows[layer, m_shift:m_shift + 1, :])).then_inc(mod_in, 16)
                if combine:
                    sp.dma_start(gate_b, rowcast(gate_row)).then_inc(gate_in, 16)
                load_x(1, 1)
                if gates:
                    with nc.allow_non_contiguous_dma(reason="eight gate columns"):
                        sp.dma_start(gw_raw[:, :, :], w_in[:, NCOL:NCOL + 8].rearrange("(k p) n -> p k n", p=P)).then_inc(gw_in, 16)
                        sp.dma_start(gbias[0:8, 0:1], b_gates[0, :].rearrange("(n a) -> n a", a=1)).then_inc(gw_in, 16)
                if conv:
                    with nc.allow_non_contiguous_dma(reason="a few KB of taps laid over the partitions"):
                        for j in range(3):
                            sp.dma_start(taps[:, :, j], cols(conv_w[0, j, :])).then_inc(taps_in, 16)
                        sp.dma_start(taps[:, :, 3], cols(conv_b[0, :])).then_inc(taps_in, 16)
                for s in range(RING):
                    load_w(chunk_col(0, s), s)

                def step(i, s):
                    if combine:
                        if live(i, s):
                            sp.wait_ge(x2_ready, upto(i, s))
                            sp.dma_start(x_dst[bass.ds((i * RING + s) * P, P), :], xin[:, s, :]).then_inc(x_out[s], 16)
                        if live(i, s, 1) and live(i, s, -1):
                            sp.wait_ge(x_out[slot(s, -1)], 16 * uses(i, s, -1))
                            sp.wait_ge(um_ready, upto(i, s, -1))
                            load_x(i * RING + (s + 1), slot(s, 1))
                    elif live(i, s, RING):
                        sp.wait_ge(um_ready, upto(i, s))
                        load_x(i * RING + (s + RING), s)

                skewed(sp, step, behind=0)

                def store(i, q):
                    if conv:
                        if q % 3 == 2:
                            j, s = q // 3, (q // 3) % RING
                            sp.wait_ge(y_ready, i * (2 * NBLK) + NBLK * (j + 2))
                            sp.dma_start(out_t[bass.ds(i * (2 * P) + j * P, P), :], stage[:, s, :]).then_inc(out_done[s], 16)
                    else:
                        sp.wait_ge(ev_act, i * (CH * NBLK) + NBLK * (q + 2))
                        sp.dma_start(out_t[bass.ds(i * (CH * P) + q * P, P), :], stage[:, q % RING, :]).then_inc(out_done[q % RING], 16)

                with sp.Fori(0, BODIES - 1) as i:
                    for q in range(CH):
                        sp.wait_ge(w_lo_ready, i * CH + (q + 1))
                        load_w(chunk_col(i, q + 2), q % RING)
                        store(i, q)
                for q in range(CH):
                    if q + 2 < CH:
                        sp.wait_ge(w_lo_ready, (BODIES - 1) * CH + (q + 1))
                        load_w(chunk_col(BODIES - 1, q + 2), q % RING)
                    store(BODIES - 1, q)
                if gates:
                    sp.wait_ge(gates_ev, NBLK)
                    sp.dma_start(gates_t[:, :], gate_rows[0:8, :]).then_inc(gates_out, 16)
                    sp.wait_ge(gates_out, 16)
                n_out = (KT if conv else NCHUNK) // RING
                for s in range(RING):
                    sp.wait_ge(out_done[s], 16 * (n_out + 1))

            @block.gpsimd
            def _(pool):
                pool.memset(mhalf[:, :], -0.5).then_inc(const_ready, 1)
                pool.wait_ge(const_ready, 1)

                def gather(n, s, count):
                    pool.tensor_copy(idx[:, s, :], pos[:, :, bass.ds(n, 1)].rearrange("p j a -> p (j a)")).then_inc(idx_ready, 1)
                    pool.wait_ge(idx_ready, count)
                    stand(pool, passed)
                    for j, dst in enumerate((row_a, row_b)):
                        pool.indirect_dma_start(dst[:, s, :], None, ys, bass.IndirectOffsetOnAxis(ap=idx[:, s, j:j + 1], axis=0)).then_inc(rows_in[s], 16)

                def step(i, s):
                    if combine and live(i, s, RING):
                        pool.wait_ge(x2_ready, upto(i, s))
                        gather(i * RING + (s + RING), s, upto(i, s, RING))
                    if live(i, s):
                        pool.wait_ge(ssq_ready, upto(i, s, 1))
                        stand(pool, passed)
                        pool.tensor_scalar(rstd[:, s:s + 1], ssq[:, s:s + 1], 1.0 / D, EPS, ALU.mult, ALU.add).then_inc(var_ready, 1)
                        pool.wait_ge(var_ready, upto(i, s))
                        pool.tensor_tensor(rstd[:, s:s + 1], rstd[:, s:s + 1], mhalf[:, 0:1], ALU.pow).then_inc(rstd_ready, 1)
                    if live(i, s, UM):
                        pool.wait_ge(um_ready, upto(i, s, UM))
                        pool.tensor_tensor(u[:, slot(s, UM), :], u[:, slot(s, UM), :], shift_b, ALU.add).then_inc(u_ready, 1)

                if combine:
                    gather(0, 0, 1)
                    gather(1, 1, 2)
                pool.wait_ge(mod_ready, 1)
                if blank is not None:
                    pool.memset(zero[:, :], 0.0).then_inc(zero_ready, 1)
                skewed(pool, step)
                if blank is not None:
                    pool.wait_ge(zero_ready, 1)
                    for a in range(MAX_TILES):
                        pool.dma_start(blank[a * P:(a + 1) * P, :], zero[:, :]).then_inc(blank_out, 16)
                    pool.wait_ge(blank_out, 16 * MAX_TILES)

            @block.scalar
            def _(act):
                act.sem_inc(hi_done, RING)
                act.sem_inc(ev_act, NBLK)
                act.sem_inc(ssq_ready, 1)
                for s in range(RING):
                    act.sem_inc(out_done[s], 16)

                def split_w(blocks, loaded, s):
                    act.wait_ge(wr_in[s], loaded)
                    if blocks is not None:
                        act.wait_ge(blk_done, blocks)
                    act.activation(w_hi[:, s, :, :], w_raw[:, s, :, :], ACT.Copy).then_inc(w_hi_ready, 1)

                def weigh(i, s, n):
                    act.wait_ge(rows_in[slot(s, n)], 32 * uses(i, s, n))
                    act.wait_ge(wts_ready, upto(i, s, n))
                    act.activation(row_a[:, slot(s, n), :], row_a[:, slot(s, n), :], ACT.Copy, scale=wts[:, slot(s, n), 0:1]).then_inc(ra_ready, 1)

                def step(i, s):
                    if live(i, s):
                        if combine:
                            act.wait_ge(x2_ready, upto(i, s))
                        else:
                            act.wait_ge(x_in[s], 16 * uses(i, s))
                        act.wait_ge(ssq_ready, upto(i, s))
                        act.activation(junk[:, :], xin[:, s, :], ACT.Square, accum_out=ssq[:, s:s + 1]).then_inc(ssq_ready, 1)
                    if live(i, s, HI):
                        act.wait_ge(tr_done, upto(i, s, HI))
                        act.activation(u_hi[:, :, bass.ds((i * RING + (s + HI)) * P, P)],
                                       psum_t[:, slot(s, HI), :].rearrange("p (k t) -> p k t", k=KT), ACT.Copy).then_inc(hi_done, 1)
                    if combine and live(i, s, 1):
                        weigh(i, s, 1)

                if combine:
                    weigh(0, 0, 0)
                for s in range(RING):
                    split_w(None, 16, s)
                if gates:
                    act.wait_ge(gw_in, 32)
                    act.activation(gw_hi[:, :, :], gw_raw[:, :, :], ACT.Copy).then_inc(gw_ready, 1)
                skewed(act, step)
                if combine:
                    for s in range(RING):
                        act.wait_ge(x_out[s], 16 * (NT // RING))

                def body(i, q, more):
                    if conv:
                        if q % 3 == 0:
                            j = q // 3
                            for b in range(NBLK):
                                act.wait_ge(y_ready, i * (2 * NBLK) + NBLK * j + b + 1)
                                act.wait_ge(blk_done, i * (CH * NBLK) + NBLK * q + b + 1)
                                act.activation(c_rows[:, b * HALF:(b + 1) * HALF], psum_o[:, b, :], ACT.Copy).then_inc(ev_act, 1)
                    else:
                        act.wait_ge(out_done[q % RING], 16 * i + 16)
                        for b in range(NBLK):
                            act.wait_ge(blk_done, i * (CH * NBLK) + NBLK * q + b + 1)
                            act.activation(stage[:, q % RING, b * HALF:(b + 1) * HALF], psum_o[:, b, :], ACT.Copy).then_inc(ev_act, 1)
                    if more:
                        split_w(i * (CH * NBLK) + NBLK * (q + 1), i * (16 * CH // RING) + 16 * (q // RING + 2), q % RING)

                with act.Fori(0, BODIES - 1) as i:
                    for q in range(CH):
                        body(i, q, True)
                for q in range(CH):
                    body(BODIES - 1, q, q + 2 < CH)
                if gates:
                    for b in range(NBLK):
                        act.wait_ge(blk_done, NCHUNK * NBLK + b + 1)
                        act.activation(gate_rows[0:8, b * HALF:(b + 1) * HALF], psum_o[0:8, b, :], ACT.Identity, bias=gbias[0:8, 0:1]).then_inc(gates_ev, 1)

            @block.vector
            def _(dve):
                dve.sem_inc(lo_done, RING)
                dve.wait_ge(mod_in, 48)
                dve.scalar_tensor_tensor(out=scale_b, in0=scale_b, scalar=1.0, in1=ng_b,
                                         op0=ALU.add, op1=ALU.mult).then_inc(mod_ready, 1)
                dve.wait_ge(mod_ready, 1)
                if conv:
                    dve.sem_inc(y_ready, NBLK)

                def weights(i, s, n):
                    dve.tensor_copy(wts[:, slot(s, n), :], pair_w[:, :, bass.ds(i * RING + (s + n), 1)].rearrange("p j a -> p (j a)")).then_inc(wts_ready, 1)

                def split_w(n1, s):
                    dve.wait_ge(w_hi_ready, n1)
                    dve.tensor_tensor(w_lo[:, s, :, :], w_raw[:, s, :, :], w_hi[:, s, :, :].bitcast(F32), ALU.subtract).then_inc(w_lo_ready, 1)

                def low(i, s):
                    if live(i, s, LO):
                        dve.wait_ge(hi_done, upto(i, s, LO + RING))
                        dst = bass.ds((i * RING + (s + LO)) * P, P)
                        dve.tensor_tensor(u_lo[:, :, dst], psum_t[:, slot(s, LO), :].rearrange("p (k t) -> p k t", k=KT),
                                          u_hi[:, :, dst].bitcast(F32), ALU.subtract).then_inc(lo_done, 1)

                def step(i, s):
                    if combine and live(i, s):
                        dve.wait_ge(ra_ready, upto(i, s))
                        dve.wait_ge(wts_ready, upto(i, s))
                        dve.scalar_tensor_tensor(out=row_b[:, s, :], in0=row_b[:, s, :], scalar=wts[:, s, 1:2], in1=row_a[:, s, :],
                                                 op0=ALU.mult, op1=ALU.add).then_inc(rb_ready, 1)
                        if live(i, s, 1):
                            weights(i, s, 1)
                    if combine:
                        low(i, s)
                    if combine and live(i, s):
                        dve.wait_ge(rb_ready, upto(i, s))
                        dve.tensor_tensor(row_b[:, s, :], row_b[:, s, :], gate_b, ALU.mult).then_inc(mix_ready, 1)
                        dve.wait_ge(mix_ready, upto(i, s))
                        dve.wait_ge(x_in[s], 16 * uses(i, s))
                        dve.tensor_tensor(xin[:, s, :], xin[:, s, :], row_b[:, s, :], ALU.add).then_inc(x2_ready, 1)
                    if live(i, s, UM):
                        n = slot(s, UM)
                        dve.wait_ge(rstd_ready, upto(i, s, UM))
                        if combine:
                            dve.wait_ge(x2_ready, upto(i, s, UM))
                        else:
                            dve.wait_ge(x_in[n], 16 * uses(i, s, UM))
                        dve.scalar_tensor_tensor(out=u[:, n, :], in0=xin[:, n, :], scalar=rstd[:, n:n + 1], in1=scale_b,
                                                 op0=ALU.mult, op1=ALU.mult).then_inc(um_ready, 1)
                    if not combine:
                        low(i, s)

                if combine:
                    weights(0, 0, 0)
                    dve.wait_ge(gate_in, 16)
                for s in range(RING):
                    split_w(s + 1, s)
                if gates:
                    dve.wait_ge(gw_ready, 1)
                    dve.tensor_tensor(gw_lo[:, :, :], gw_raw[:, :, :], gw_hi[:, :, :].bitcast(F32), ALU.subtract).then_inc(gw_ready, 1)
                skewed(dve, step)
                if conv:
                    dve.wait_ge(taps_in, 64)
                    dve.memset(z_rows[:, 0:2], 0.0).then_inc(z_ready, 1)
                    for s in range(RING):
                        dve.wait_ge(x_out[s], 16 * (NT // RING))

                def body(i, q, more):
                    if conv:
                        j, kind = q // 3, q % 3
                        n0 = i * (2 * NBLK) + NBLK * j
                        if kind == 0:
                            dve.tensor_copy(tap[:, j, :], taps[:, bass.ds(i * 2 + j, 1), :].rearrange("p a j -> p (a j)")).then_inc(tap_ready, 1)
                        if kind == 1:
                            for b in range(NBLK):
                                cs, at = c_rows[:, b * HALF:(b + 1) * HALF], b * HALF
                                dve.wait_ge(ev_act, n0 + (NBLK + b + 1))
                                dve.wait_ge(blk_done, i * (CH * NBLK) + NBLK * q + b + 1)
                                dve.tensor_tensor(z_rows[:, 2 + at:2 + at + HALF], cs, psum_o[:, b, :], ALU.mult).then_inc(z_ready, 1)
                            for b in range(NBLK):
                                cs, at = c_rows[:, b * HALF:(b + 1) * HALF], b * HALF
                                if b == 0:
                                    dve.wait_ge(tap_ready, i * 2 + (j + 1))
                                    dve.wait_ge(z_ready, n0 + (NBLK + 1))
                                dve.tensor_scalar(cs, z_rows[:, 2 + at:2 + at + HALF], tap[:, j, 2:3], tap[:, j, 3:4],
                                                  ALU.mult, ALU.add).then_inc(zc_ready, 1)
                                for m, o in ((1, 1), (0, 0)):
                                    dve.wait_ge(zc_ready, i * (2 * NBLK * 3) + 3 * (NBLK * j + b) + 2 - m)
                                    dve.scalar_tensor_tensor(out=cs, in0=z_rows[:, o + at:o + at + HALF], scalar=tap[:, j, m:m + 1],
                                                             in1=cs, op0=ALU.mult, op1=ALU.add).then_inc(zc_ready, 1)
                        if kind == 2:
                            dve.wait_ge(out_done[j], 16 * i + 16)
                            dve.wait_ge(zc_ready, i * (2 * NBLK * 3) + 3 * NBLK * (j + 1))
                            for b in range(NBLK):
                                dve.wait_ge(blk_done, i * (CH * NBLK) + NBLK * q + b + 1)
                                dve.tensor_tensor(stage[:, j, b * HALF:(b + 1) * HALF], c_rows[:, b * HALF:(b + 1) * HALF], psum_o[:, b, :],
                                                  ALU.mult).then_inc(y_ready, 1)
                    if more:
                        split_w(i * CH + (q + 3), q % RING)

                with dve.Fori(0, BODIES - 1) as i:
                    for q in range(CH):
                        body(i, q, True)
                for q in range(CH):
                    body(BODIES - 1, q, q + 2 < CH)

            @block.tensor
            def _(pe):
                with pe.Fori(0, NT // RING) as i:
                    for s in range(RING):
                        n1 = i * RING + (s + 1)
                        pe.wait_ge(u_ready, n1)
                        pe.wait_ge(hi_done, n1)
                        pe.wait_ge(lo_done, n1)
                        for k in range(KT):
                            last = pe.transpose(psum_t[:, s, k * P:(k + 1) * P], u[:, s, k * P:(k + 1) * P], ident[:, :])
                        last.then_inc(tr_done, 1)
                pe.wait_ge(hi_done, NT + RING)
                pe.wait_ge(lo_done, NT + RING)

                def block_of(b, rows, wh, wl):
                    ts = slice(b * HALF, (b + 1) * HALF)
                    for k in range(KT):
                        last = split_mm(pe, psum_o[0:rows, b, :], (wh[:, k, :], wl[:, k, :]),
                                        (u_hi[:, k, ts], u_lo[:, k, ts]), k == 0, k == KT - 1)
                    last.then_inc(blk_done, 1)
                    return last

                def body(i, q):
                    pe.wait_ge(w_lo_ready, i * CH + (q + 1))
                    for b in range(NBLK):
                        if conv:
                            n0 = i * (2 * NBLK) + NBLK * (q // 3) + b + 1
                            if q % 3 == 0:
                                pe.wait_ge(y_ready, n0)
                            elif q % 3 == 1:
                                pe.wait_ge(ev_act, n0 + NBLK)
                            else:
                                pe.wait_ge(z_ready, n0 + 1)
                        else:
                            pe.wait_ge(ev_act, i * (CH * NBLK) + NBLK * q + b + 1)
                        block_of(b, P, w_hi[:, q % RING], w_lo[:, q % RING])

                with pe.Fori(0, BODIES) as i:
                    for q in range(CH):
                        body(i, q)
                if gates:
                    pe.wait_ge(gw_ready, 2)
                    for b in range(NBLK):
                        pe.wait_ge(ev_act, NCHUNK * NBLK + b + 1)
                        block_of(b, 8, gw_hi, gw_lo)


def mlstm(nc, proj_t, gates_t, gate_d, norm_g, h_t, ident):
    HC = HEADS * NT
    V1 = DV + 1
    SCALE = float(DQK) ** -0.5
    with Phase(nc, "rec") as ph:
        gi = ph.sb("gi", [HC, P])
        gf = ph.sb("gf", [HC, P])
        tmp = ph.sb("tmp", [HC, P])
        lf = ph.sb("lf", [HC, P])
        b = ph.sb("b", [HC, P])
        g = ph.sb("g", [HC, P])
        zeros = ph.sb("zeros", [HC, P])
        ones = ph.sb("ones", [HC, P])
        m_run = ph.sb("m_run", [HC, P])
        ends = ph.sb("ends", [HC, 2])
        m_start = ph.sb("m_start", [HC, 1])
        neg_last = ph.sb("neg_last", [HC, 1])
        neg_m = ph.sb("neg_m", [HC, 2, P])
        wk = ph.sb("wk", [HC, P])
        enm = ph.sb("enm", [HC, P])
        chain = ph.sb("chain", [HEADS, NT, 2])
        m_seq = ph.sb("m_seq", [HEADS, NT + 1])
        tok = ph.sb("tok", [P, 3, HC])
        decay = ph.sb("decay", [P, HC])
        causal = ph.sb("causal", [P, P])
        causal4 = ph.sb("causal4", [P, HEADS, P])
        ng = ph.sb("ng", [P, KT])
        mhalf = ph.sb("mhalf", [P, HEADS])
        pt = ph.sb("pt", [P, RING, 3 * KT, P])
        bc = ph.sb("bc", [P, RING, HEADS, 2, P])
        kw = ph.sb("kw", [P, RING, HEADS, DQK])
        val = ph.sb("val", [P, RING, HEADS, V1])
        qw = ph.sb("qw", [P, RING, HEADS, P])
        arg = ph.sb("arg", [P, HEADS, P])
        sd = ph.sb("sd", [P, RING, HEADS, P])
        cst = ph.sb("cst", [P, HEADS, V1])
        sgate = ph.sb("sgate", [P, RING, KT, P])
        numer = ph.sb("numer", [P, HEADS, V1])
        junk = ph.sb("junk", [P, DV])
        den = ph.sb("den", [P, HEADS])
        ssq = ph.sb("ssq", [P, HEADS])
        fac = ph.sb("fac", [P, HEADS])
        hout = ph.sb("hout", [P, RING, KT, P])
        tokc = ph.sb("tokc", [P, RING, 3, HEADS])
        decc = ph.sb("decc", [P, RING, HEADS])
        ps_k = ph.ps("ps_k", [P, HEADS, P])
        ps_v = ph.ps("ps_v", [P, KT, P])
        ps_s = ph.ps("ps_s", [P, HEADS, P])
        ps_n = ph.ps("ps_n", [P, RING, HALF])
        ps_c = ph.ps("ps_c", [P, RING, HALF])
        g_in = ph.sem("g_in")
        pre = ph.sem("pre")
        pre_act = ph.sem("pre_act")
        ends_out = ph.sem("ends_out")
        chain_in = ph.sem("chain_in")
        seq_out = ph.sem("seq_out")
        start_in = ph.sem("start_in")
        rows_out = ph.sem("rows_out")
        decay_in = ph.sem("decay_in")
        tok_tr = ph.sem("tok_tr")
        passed = ph.sem("passed")
        tok_ready = ph.sem("tok_ready")
        consts = ph.sem("consts")
        ng_in = ph.sem("ng_in")
        pt_in = [ph.sem(f"pt_in{s}") for s in range(RING)]
        bc_in = [ph.sem(f"bc_in{s}") for s in range(RING)]
        kv_tr = ph.sem("kv_tr")
        s_done = ph.sem("s_done")
        kw_ready = ph.sem("kw_ready")
        val_ready = ph.sem("val_ready")
        qw_ready = ph.sem("qw_ready")
        cols_ready = ph.sem("cols_ready")
        arg_ready = ph.sem("arg_ready")
        masked = ph.sem("masked")
        exp_ready = ph.sem("exp_ready")
        sd_ready = ph.sem("sd_ready")
        num_done = ph.sem("num_done")
        cup_done = ph.sem("cup_done")
        c_ready = ph.sem("c_ready")
        num_ev = ph.sem("num_ev")
        den_ready = ph.sem("den_ready")
        norm_step = ph.sem("norm_step")
        fsq = ph.sem("fsq")
        fss = ph.sem("fss")
        fac_ready = ph.sem("fac_ready")
        hn_ready = ph.sem("hn_ready")
        h_tr = ph.sem("h_tr")
        h_ready = ph.sem("h_ready")
        sig_ready = ph.sem("sig_ready")
        gate_ready = ph.sem("gate_ready")
        h_out = [ph.sem(f"h_out{s}") for s in range(RING)]
        ends_d, seq_d, rows_d, decay_d = gate_d
        NPRE = 3

        with ph.block() as block:
            @block.sync
            def _(sp):
                src = lambda r: gates_t[r:r + HEADS, :].rearrange("h (c t) -> (h c) t", t=P)
                sp.dma_start(gi[:, :], src(0)).then_inc(g_in, 16)
                sp.dma_start(gf[:, :], src(HEADS)).then_inc(g_in, 16)
                with nc.allow_non_contiguous_dma(reason="4 KB vector laid over the partitions"):
                    sp.dma_start(ng[:, :], cols(norm_g[0, :])).then_inc(ng_in, 16)

                def load(c, s):
                    sp.dma_start(pt[:, s, :, :], proj_t[:, bass.ds(c * P, P)].rearrange("(r p) t -> p r t", p=P)).then_inc(pt_in[s], 16)

                def load_bc(c, s):
                    for h in range(HEADS):
                        src = rows_d[bass.ds(c + h * NT, 1), :].to_broadcast([P, 2 * P])
                        sp.dma_start(bc[:, s, h, :, :], src.rearrange("p (a t) -> p a t", a=2)).then_inc(bc_in[s], 16)

                load(0, 0)
                load(1, 1)
                sp.wait_ge(pre, 8)
                sp.dma_start(ends_d[:, :], ends[:, :]).then_inc(ends_out, 16)
                sp.wait_ge(ends_out, 16)
                sp.dma_start(chain[:, :, :], ends_d.rearrange("(h c) a -> h c a", h=HEADS)).then_inc(chain_in, 16)
                sp.wait_ge(pre, 10)
                sp.dma_start(seq_d.rearrange("(h c) a -> h (c a)", h=HEADS), m_seq[:, 0:NT]).then_inc(seq_out, 16)
                sp.wait_ge(seq_out, 16)
                sp.dma_start(m_start[:, :], seq_d).then_inc(start_in, 16)
                sp.wait_ge(pre, 14)
                sp.wait_ge(pre_act, 3)
                sp.dma_start(rows_d, neg_m[:, :, :].rearrange("p a t -> p (a t)")).then_inc(rows_out, 16)
                sp.dma_start(decay_d, neg_m[:, 1, P - 1:P]).then_inc(rows_out, 16)
                sp.wait_ge(rows_out, 32)
                sp.dma_start(decay[:, :], decay_d.rearrange("c a -> a c").to_broadcast([P, HC])).then_inc(decay_in, 16)
                load_bc(0, 0)
                load_bc(1, 1)

                def chunk(i, s, more):
                    n = i * RING + (s + 1)
                    sp.wait_ge(h_ready, n + RING)
                    sp.dma_start(h_t[:, bass.ds(i * (RING * P) + s * P, P)].rearrange("(k p) t -> p k t", p=P), hout[:, s, :, :]).then_inc(h_out[s], 16)
                    if more:
                        sp.wait_ge(sig_ready, n)
                        sp.wait_ge(val_ready, n)
                        sp.wait_ge(kw_ready, n)
                        sp.wait_ge(sd_ready, n)
                        load(i * RING + (RING + s), s)
                        load_bc(i * RING + (RING + s), s)

                with sp.Fori(0, NT // RING - 1) as i:
                    for s in range(RING):
                        chunk(i, s, True)
                for s in range(RING):
                    chunk(NT // RING - 1, s, False)
                for s in range(RING):
                    sp.wait_ge(h_out[s], 16 * (NT // RING + 1))

            @block.gpsimd
            def _(pool):
                pool.memset(zeros[:, :], 0.0).then_inc(consts, 1)
                pool.memset(ones[:, :], 1.0).then_inc(consts, 1)
                pool.memset(mhalf[:, :], -0.5).then_inc(consts, 1)
                pool.memset(causal4[:, :, :], 0.0).then_inc(consts, 1)
                pool.memset(val[:, :, :, DV:V1], 1.0).then_inc(consts, 1)
                pool.memset(cst[:, :, :], 0.0).then_inc(consts, 1)
                pool.wait_ge(consts, 6)
                pool.affine_select(out=causal4[:, :, :], in_=causal4[:, :, :], compare_op=ALU.is_ge, fill=-BIG, base=0,
                                   pattern=[[0, HEADS], [1, P]], channel_multiplier=-1).then_inc(consts, 1)
                pool.wait_ge(consts, 7)
                pool.wait_ge(ng_in, 16)

                def early(i, s):
                    n = i * RING + (s + 1)
                    pool.wait_ge(arg_ready, n)
                    pool.tensor_tensor(arg[:, :, :], arg[:, :, :], causal4[:, :, :], ALU.add).then_inc(masked, 1)

                def late(i, s):
                    n = i * RING + (s + 1)
                    pool.wait_ge(sig_ready, n)
                    pool.tensor_tensor(sgate[:, s, :, :], sgate[:, s, :, :], ng[:, :].unsqueeze(2).to_broadcast([P, KT, P]), ALU.mult).then_inc(gate_ready, 1)
                    pool.wait_ge(norm_step, i * (RING * 3) + (3 * s + 2))
                    pool.tensor_tensor(fac[:, :], fac[:, :], mhalf[:, :], ALU.pow).then_inc(fac_ready, 1)

                early(0, 0)
                with pool.Fori(0, NT // RING - 1) as i:
                    early(i, 1)
                    late(i, 0)
                    early(i + 1, 0)
                    late(i, 1)
                early(NT // RING - 1, 1)
                late(NT // RING - 1, 0)
                late(NT // RING - 1, 1)

            @block.scalar
            def _(act):
                for s in range(RING):
                    act.sem_inc(h_out[s], 16)
                act.sem_inc(num_ev, 2 * RING)
                act.wait_ge(pre, 1)
                act.activation(tmp[:, :], tmp[:, :], ACT.Exp, scale=-1.0).then_inc(pre_act, 1)
                act.wait_ge(pre, 2)
                act.activation(tmp[:, :], tmp[:, :], ACT.Ln).then_inc(pre_act, 1)
                act.wait_ge(pre, 14)
                act.activation(neg_m[:, 1, :], neg_m[:, 0, :], ACT.Exp, bias=m_start[:, 0:1]).then_inc(pre_act, 1)
                act.activation(wk[:, :], g[:, :], ACT.Exp, bias=neg_last[:, 0:1]).then_inc(pre_act, 1)
                act.activation(enm[:, :], tmp[:, :], ACT.Exp, scale=-1.0).then_inc(pre_act, 1)

                def stage1(i, s):
                    n = i * RING + (s + 1)
                    act.wait_ge(kv_tr, n)
                    act.activation(val[:, s, :, 0:DV], ps_v[:, :, :].rearrange("p (h a) d -> p h (a d)", h=HEADS), ACT.Copy).then_inc(val_ready, 1)
                    act.wait_ge(masked, n)
                    act.activation(arg[:, :, :], arg[:, :, :], ACT.Exp).then_inc(exp_ready, 1)
                    act.wait_ge(h_ready, n)
                    act.activation(sgate[:, s, :, :], pt[:, s, 2 * KT:3 * KT, :], ACT.Tanh, scale=0.5)\
                       .then_inc(exp_ready, 1)

                def stage2(i, s):
                    n4 = i * (RING * HEADS) + s * HEADS
                    act.wait_ge(h_tr, i * RING + (s + 1))
                    for h in range(HEADS):
                        act.wait_ge(num_done, n4 + (h + 1))
                        act.wait_ge(num_ev, i * (2 * RING * HEADS) + 2 * (s * HEADS + h) + 3)
                        act.activation(junk[:, :], ps_n[:, h % RING, 0:DV], ACT.Square, accum_out=ssq[:, h:h + 1]).then_inc(num_ev, 1)
                        act.activation(numer[:, h, :], ps_n[:, h % RING, 0:V1], ACT.Copy).then_inc(num_ev, 1)
                    act.wait_ge(cup_done, n4 + HEADS)
                    stand(act, passed)

                act.wait_ge(consts, 7)
                stage1(0, 0)
                with act.Fori(0, NT // RING - 1) as i:
                    stage1(i, 1)
                    stage2(i, 0)
                    stage1(i + 1, 0)
                    stage2(i, 1)
                stage1(NT // RING - 1, 1)
                stage2(NT // RING - 1, 0)
                stage2(NT // RING - 1, 1)

            @block.vector
            def _(dve):
                dve.wait_ge(g_in, 32)
                dve.wait_ge(consts, 7)
                dve.scalar_tensor_tensor(out=tmp[:, :], in0=gf[:, :], scalar=-1.0, in1=gf[:, :], op0=ALU.mult, op1=ALU.max).then_inc(pre, 1)
                dve.wait_ge(pre_act, 1)
                dve.tensor_scalar(tmp[:, :], tmp[:, :], 1.0, None, ALU.add).then_inc(pre, 1)
                dve.wait_ge(pre_act, 2)
                dve.scalar_tensor_tensor(out=lf[:, :], in0=gf[:, :], scalar=0.0, in1=tmp[:, :], op0=ALU.min, op1=ALU.subtract).then_inc(pre, 1)
                dve.wait_ge(pre, 3)
                dve.tensor_tensor_scan(b[:, :], ones[:, :], lf[:, :], 0.0, ALU.mult, ALU.add).then_inc(pre, 1)
                dve.wait_ge(pre, 4)
                dve.tensor_tensor(g[:, :], gi[:, :], b[:, :], ALU.subtract).then_inc(pre, 1)
                dve.tensor_copy(ends[:, 1:2], b[:, P - 1:P]).then_inc(pre, 1)
                dve.wait_ge(pre, 5)
                dve.tensor_tensor_scan(m_run[:, :], zeros[:, :], g[:, :], -BIG, ALU.add, ALU.max).then_inc(pre, 1)
                dve.wait_ge(pre, 7)
                dve.tensor_copy(ends[:, 0:1], m_run[:, P - 1:P]).then_inc(pre, 1)
                dve.memset(m_seq[:, 0:1], 0.0).then_inc(pre, 1)
                dve.wait_ge(chain_in, 16)
                dve.tensor_tensor_scan(m_seq[:, 1:NT + 1], chain[:, :, 0], chain[:, :, 1], 0.0, ALU.max, ALU.add).then_inc(pre, 1)
                dve.wait_ge(start_in, 16)
                dve.tensor_scalar(m_run[:, :], m_run[:, :], m_start[:, 0:1], None, ALU.max).then_inc(pre, 1)
                dve.wait_ge(pre, 11)
                dve.tensor_scalar(neg_m[:, 0, :], m_run[:, :], -1.0, None, ALU.mult).then_inc(pre, 1)
                dve.tensor_scalar(neg_last[:, :], m_run[:, P - 1:P], -1.0, None, ALU.mult).then_inc(pre, 1)
                dve.tensor_tensor(tmp[:, :], b[:, :], m_run[:, :], ALU.add).then_inc(pre, 1)
                dve.wait_ge(tok_tr, 1)
                dve.tensor_copy(tok[:, :, :], ps_s[:, 0:NPRE, 0:HC]).then_inc(tok_ready, 1)
                dve.wait_ge(tok_ready, 1)
                dve.wait_ge(decay_in, 16)
                dve.sem_inc(c_ready, HEADS)
                dve.sem_inc(h_ready, RING)

                def stage1(i, s):
                    n = i * RING + (s + 1)
                    dve.tensor_copy(tokc[:, s, :, :], tok[:, :, :].rearrange("p a (h c) -> p a h c", h=HEADS)[:, :, :, bass.ds(i * RING + s, 1)]
                                    .rearrange("p a h c -> p a (h c)")).then_inc(cols_ready, 1)
                    dve.tensor_copy(decc[:, s, :], decay[:, :].rearrange("p (h c) -> p h c", h=HEADS)[:, :, bass.ds(i * RING + s, 1)]
                                    .rearrange("p h c -> p (h c)")).then_inc(cols_ready, 1)
                    dve.wait_ge(cols_ready, i * (2 * RING) + 2 * (s + 1))
                    dve.wait_ge(bc_in[s], 16 * HEADS * i + 16 * HEADS)
                    dve.tensor_tensor(arg[:, :, :], bc[:, s, :, 0, :], tokc[:, s, 0, :].unsqueeze(2).to_broadcast([P, HEADS, P]), ALU.add).then_inc(arg_ready, 1)
                    dve.wait_ge(pt_in[s], 16 * i + 16)
                    dve.scalar_tensor_tensor(out=qw[:, s, :, :], in0=pt[:, s, 0:HEADS, :], scalar=SCALE, in1=bc[:, s, :, 1, :],
                                             op0=ALU.mult, op1=ALU.mult).then_inc(qw_ready, 1)
                    dve.wait_ge(kv_tr, n)
                    dve.tensor_tensor(kw[:, s, :, :], ps_k[:, :, :], tokc[:, s, 1, :].unsqueeze(2).to_broadcast([P, HEADS, P]), ALU.mult).then_inc(kw_ready, 1)
                    dve.wait_ge(exp_ready, i * (2 * RING) + 2 * s + 1)
                    dve.wait_ge(s_done, n)
                    dve.scalar_tensor_tensor(out=sd[:, s, :, :], in0=ps_s[:, :, :], scalar=SCALE, in1=arg[:, :, :], op0=ALU.mult, op1=ALU.mult).then_inc(sd_ready, 1)
                    dve.wait_ge(exp_ready, i * (2 * RING) + 2 * (s + 1))
                    dve.tensor_scalar(sgate[:, s, :, :], sgate[:, s, :, :], 0.5, 0.5, ALU.mult, ALU.add).then_inc(sig_ready, 1)

                def stage2(i, s):
                    n = i * RING + (s + 1)
                    n4 = i * (RING * HEADS) + s * HEADS
                    n3 = i * (RING * 3) + 3 * s
                    for h in range(HEADS):
                        dve.wait_ge(cup_done, n4 + (h + 1))
                        dve.scalar_tensor_tensor(out=cst[:, h, :], in0=cst[:, h, :], scalar=decc[:, s, h:h + 1], in1=ps_c[:, h % RING, 0:V1],
                                                 op0=ALU.mult, op1=ALU.add).then_inc(c_ready, 1)
                    dve.wait_ge(num_ev, i * (2 * RING * HEADS) + 2 * HEADS * (s + 1) + 2 * RING)
                    dens = numer[:, :, DV:V1].rearrange("p h a -> p (h a)")
                    dve.scalar_tensor_tensor(out=den[:, :], in0=dens, scalar=-1.0, in1=tokc[:, s, 2, :], op0=ALU.mult, op1=ALU.max).then_inc(den_ready, 1)
                    dve.wait_ge(den_ready, i * (2 * RING) + (2 * s + 1))
                    dve.tensor_tensor(den[:, :], den[:, :], dens, ALU.max).then_inc(den_ready, 1)
                    dve.wait_ge(den_ready, i * (2 * RING) + 2 * (s + 1))
                    dve.reciprocal(den[:, :], den[:, :]).then_inc(norm_step, 1)
                    dve.wait_ge(norm_step, n3 + 1)
                    dve.tensor_tensor(fac[:, :], den[:, :], den[:, :], ALU.mult).then_inc(fsq, 1)
                    dve.wait_ge(fsq, n)
                    dve.tensor_tensor(fac[:, :], fac[:, :], ssq[:, :], ALU.mult).then_inc(fss, 1)
                    dve.wait_ge(fss, n)
                    dve.tensor_scalar(fac[:, :], fac[:, :], 1.0 / DV, EPS, ALU.mult, ALU.add).then_inc(norm_step, 1)
                    dve.wait_ge(fac_ready, n)
                    dve.tensor_tensor(fac[:, :], fac[:, :], den[:, :], ALU.mult).then_inc(norm_step, 1)
                    dve.wait_ge(norm_step, n3 + 3)
                    dve.tensor_tensor(numer[:, :, 0:DV], numer[:, :, 0:DV], fac[:, :].unsqueeze(2).to_broadcast([P, HEADS, DV]), ALU.mult).then_inc(hn_ready, 1)
                    dve.wait_ge(h_tr, n + 1)
                    dve.wait_ge(gate_ready, n)
                    dve.wait_ge(h_out[s], 16 * i + 16)
                    dve.tensor_tensor(hout[:, s, :, :], ps_v[:, :, :], sgate[:, s, :, :], ALU.mult).then_inc(h_ready, 1)

                stage1(0, 0)
                with dve.Fori(0, NT // RING - 1) as i:
                    stage1(i, 1)
                    stage2(i, 0)
                    stage1(i + 1, 0)
                    stage2(i, 1)
                stage1(NT // RING - 1, 1)
                stage2(NT // RING - 1, 0)
                stage2(NT // RING - 1, 1)

            @block.tensor
            def _(pe):
                pe.sem_inc(h_tr, 1)
                pe.wait_ge(pre, 14)
                pe.wait_ge(pre_act, 5)
                for a, src in enumerate((g, wk, enm)):
                    last = pe.transpose(ps_s[:, a, 0:HC], src[:, :], ident[0:HC, 0:HC])
                last.then_inc(tok_tr, 1)

                def stage1(i, s, first):
                    n = i * RING + (s + 1)
                    pe.wait_ge(pt_in[s], 16 * i + 16)
                    pe.wait_ge(h_ready, n)
                    if first:
                        pe.wait_ge(tok_ready, 1)
                    else:
                        pe.wait_ge(kw_ready, n - 1)
                        pe.wait_ge(val_ready, n - 1)
                        pe.wait_ge(sd_ready, n - 1)
                    for h in range(HEADS):
                        pe.transpose(ps_k[:, h, :], pt[:, s, HEADS + h, :], ident[:, :])
                    for r in range(KT):
                        last = pe.transpose(ps_v[:, r, :], pt[:, s, KT + r, :], ident[:, :])
                    last.then_inc(kv_tr, 1)
                    for h in range(HEADS):
                        last = pe.matmul(ps_s[:, h, :], pt[:, s, HEADS + h, :], pt[:, s, h, :], start=True, stop=True)
                    last.then_inc(s_done, 1)

                def stage2(i, s, first):
                    n = i * RING + (s + 1)
                    n4 = i * (RING * HEADS) + s * HEADS
                    pe.wait_ge(qw_ready, n)
                    pe.wait_ge(kw_ready, n)
                    pe.wait_ge(val_ready, n)
                    pe.wait_ge(sd_ready, n)
                    for h in range(HEADS):
                        q1 = n4 + (h + 1)
                        pe.wait_ge(c_ready, q1)
                        pe.wait_ge(num_ev, i * (2 * RING * HEADS) + 2 * (s * HEADS + h) + 2)
                        pe.matmul(ps_n[:, h % RING, 0:V1], qw[:, s, h, :], cst[:, h, :], start=True, stop=False)
                        pe.matmul(ps_n[:, h % RING, 0:V1], sd[:, s, h, :], val[:, s, h, :], start=False, stop=True).then_inc(num_done, 1)
                        pe.wait_ge(c_ready, q1 + RING)
                        pe.matmul(ps_c[:, h % RING, 0:V1], kw[:, s, h, :], val[:, s, h, :], start=True, stop=True).then_inc(cup_done, 1)
                    pe.wait_ge(hn_ready, n)
                    if not first:
                        pe.wait_ge(val_ready, n + 1)
                    for r in range(KT):
                        last = pe.transpose(ps_v[:, r, :], numer[:, r // 2, (r % 2) * P:(r % 2 + 1) * P], ident[:, :])
                    last.then_inc(h_tr, 1)

                last_pair = NT // RING - 1
                stage1(0, 0, True)
                with pe.Fori(0, last_pair) as i:
                    stage1(i, 1, False)
                    stage2(i, 0, False)
                    stage1(i + 1, 0, False)
                    stage2(i, 1, False)
                stage1(last_pair, 1, False)
                stage2(last_pair, 0, False)
                stage2(last_pair, 1, True)


def out_proj(nc, layer, h_t, w_out, x_src, x_dst, u_dst, norm_g, mod_rows, w_router, logits, ident):
    WS = 4
    with Phase(nc, f"out{layer}") as ph:
        w_raw = ph.sb("w_raw", [P, WS, D])
        w_hi = ph.sb("w_hi", [P, KT, D], F32R)
        w_lo = ph.sb("w_lo", [P, KT, D], F32R)
        wr_raw = ph.sb("wr_raw", [P, KT, E])
        wr_hi = ph.sb("wr_hi", [P, KT, E], F32R)
        wr_lo = ph.sb("wr_lo", [P, KT, E], F32R)
        h_raw = ph.sb("h_raw", [P, RING, KT, P])
        h_hi = ph.sb("h_hi", [P, RING, KT, P], F32R)
        h_lo = ph.sb("h_lo", [P, RING, KT, P], F32R)
        xin = ph.sb("xin", [P, RING, D])
        xo = ph.sb("xo", [P, RING, D])
        u = ph.sb("u", [P, RING, D])
        u_hi = ph.sb("u_hi", [P, KT, P], F32R)
        u_lo = ph.sb("u_lo", [P, KT, P], F32R)
        gate_b = ph.sb("gate_b", [P, D])
        scale_b = ph.sb("scale_b", [P, D])
        shift_b = ph.sb("shift_b", [P, D])
        ng_b = ph.sb("ng_b", [P, D])
        ssq = ph.sb("ssq", [P, RING])
        rstd = ph.sb("rstd", [P, RING])
        mhalf = ph.sb("mhalf", [P, 1])
        psum_o = ph.ps("psum_o", [P, RING, D])
        psum_t = ph.ps("psum_t", [P, D])
        psum_r = ph.ps("psum_r", [P, RING, E])
        mod_in = ph.sem("mod_in")
        mod_ready = ph.sem("mod_ready")
        w_in = [ph.sem(f"w_in{s}") for s in range(WS)]
        wr_in = ph.sem("wr_in")
        w_hi_ready = ph.sem("w_hi_ready")
        w_lo_ready = ph.sem("w_lo_ready")
        h_in = [ph.sem(f"h_in{s}") for s in range(RING)]
        h_hi_ready = ph.sem("h_hi_ready")
        h_lo_ready = ph.sem("h_lo_ready")
        x_in = [ph.sem(f"x_in{s}") for s in range(RING)]
        mm_done = ph.sem("mm_done")
        gated = ph.sem("gated")
        xo_ready = ph.sem("xo_ready")
        x_out = [ph.sem(f"x_out{s}") for s in range(RING)]
        ssq_ready = ph.sem("ssq_ready")
        var_ready = ph.sem("var_ready")
        rstd_ready = ph.sem("rstd_ready")
        passed = ph.sem("passed")
        um_ready = ph.sem("um_ready")
        u_ready = ph.sem("u_ready")
        u_out = [ph.sem(f"u_out{s}") for s in range(RING)]
        tr_done = ph.sem("tr_done")
        u_hi_ready = ph.sem("u_hi_ready")
        u_lo_ready = ph.sem("u_lo_ready")
        r_done = ph.sem("r_done")
        logits_ready = ph.sem("logits_ready")
        const_ready = ph.sem("const_ready")
        LAST = NT // RING - 1
        upto = lambda i, s, n=0: i * RING + (s + n + 1)

        with ph.block() as block:
            @block.sync
            def _(sp):
                def load_h(n, s):
                    sp.dma_start(h_raw[:, s, :, :], h_t[:, bass.ds(n * P, P)].rearrange("(k p) t -> p k t", p=P)).then_inc(h_in[s], 16)

                def load_x(n, s):
                    sp.dma_start(xin[:, s, :], x_src[bass.ds(n * P, P), :]).then_inc(x_in[s], 16)

                load_h(0, 0)
                for k in range(KT):
                    if k >= WS:
                        sp.wait_ge(w_lo_ready, k - WS + 1)
                    sp.dma_start(w_raw[:, k % WS, :], w_out[k * P:(k + 1) * P, :]).then_inc(w_in[k % WS], 16)
                    if k == 0:
                        load_h(1, 1)
                load_x(0, 0)
                for g, dst in ((2, gate_b), (3, shift_b), (4, scale_b)):
                    sp.dma_start(dst[:, :], rowcast(mod_rows[layer, g:g + 1, :])).then_inc(mod_in, 16)
                sp.dma_start(ng_b[:, :], rowcast(norm_g[layer:layer + 1, :])).then_inc(mod_in, 16)
                load_x(1, 1)
                with nc.allow_non_contiguous_dma(reason="64 KB router"):
                    sp.dma_start(wr_raw[:, :, :], w_router.rearrange("(k p) e -> p k e", p=P)).then_inc(wr_in, 16)
                for s in range(RING):
                    sp.wait_ge(h_lo_ready, s + 1)
                    load_h(RING + s, s)

                def step(i, s, more_x, more_h):
                    n = upto(i, s)
                    sp.wait_ge(xo_ready, n)
                    if more_x:
                        load_x(i * RING + (RING + s), s)
                    sp.dma_start(x_dst[bass.ds(i * (RING * P) + s * P, P), :], xo[:, s, :]).then_inc(x_out[s], 16)
                    if more_h:
                        sp.wait_ge(h_lo_ready, upto(i, s, RING))
                        load_h(i * RING + (2 * RING + s), s)
                    sp.wait_ge(u_ready, n)
                    sp.dma_start(u_dst[bass.ds(i * (RING * P) + s * P, P), :], u[:, s, :]).then_inc(u_out[s], 16)

                with sp.Fori(0, LAST - 1) as i:
                    for s in range(RING):
                        step(i, s, True, True)
                for i in (LAST - 1, LAST):
                    for s in range(RING):
                        step(i, s, i < LAST, False)
                for s in range(RING):
                    sp.wait_ge(x_out[s], 16 * (LAST + 2))
                    sp.wait_ge(u_out[s], 16 * (LAST + 2))

            @block.gpsimd
            def _(pool):
                pool.memset(mhalf[:, :], -0.5).then_inc(const_ready, 1)
                pool.wait_ge(const_ready, 1)
                pool.wait_ge(mod_ready, 1)
                with pool.Fori(0, NT // RING) as i:
                    for s in range(RING):
                        n = upto(i, s)
                        pool.wait_ge(ssq_ready, n)
                        stand(pool, passed)
                        pool.tensor_scalar(rstd[:, s:s + 1], ssq[:, s:s + 1], 1.0 / D, EPS, ALU.mult, ALU.add).then_inc(var_ready, 1)
                        pool.wait_ge(var_ready, n)
                        pool.tensor_tensor(rstd[:, s:s + 1], rstd[:, s:s + 1], mhalf[:, 0:1], ALU.pow).then_inc(rstd_ready, 1)
                        pool.wait_ge(um_ready, n)
                        pool.tensor_tensor(u[:, s, :], u[:, s, :], shift_b[:, :], ALU.add).then_inc(u_ready, 1)

            @block.scalar
            def _(act):
                for s in range(RING):
                    act.sem_inc(x_out[s], 16)
                    act.sem_inc(u_out[s], 16)
                act.sem_inc(logits_ready, RING)

                def split_h(products, loaded, s):
                    act.wait_ge(h_in[s], loaded)
                    if products is not None:
                        act.wait_ge(mm_done, products)
                    act.activation(h_hi[:, s, :, :], h_raw[:, s, :, :], ACT.Copy).then_inc(h_hi_ready, 1)

                split_h(None, 16, 0)
                for k in range(KT):
                    act.wait_ge(w_in[k % WS], 16 * (k // WS + 1))
                    act.activation(w_hi[:, k, :], w_raw[:, k % WS, :], ACT.Copy).then_inc(w_hi_ready, 1)
                    if k == 0:
                        split_h(None, 16, 1)
                act.wait_ge(wr_in, 16)
                act.activation(wr_hi[:, :, :], wr_raw[:, :, :], ACT.Copy).then_inc(w_hi_ready, 1)

                def logits_of(i, s, n):
                    act.wait_ge(r_done, upto(i, s, n))
                    act.activation(logits[:, bass.ds(i * RING + (s + n), 1), :].rearrange("p a e -> p (a e)"),
                                   psum_r[:, s, :], ACT.Copy).then_inc(logits_ready, 1)

                def split_u(i, s, n):
                    act.wait_ge(tr_done, upto(i, s, n))
                    act.activation(u_hi[:, :, :], psum_t[:, :].rearrange("p (k t) -> p k t", k=KT), ACT.Copy).then_inc(u_hi_ready, 1)

                def square(i, s):
                    act.wait_ge(xo_ready, upto(i, s))
                    act.wait_ge(u_out[s], 16 * i + 16)
                    act.activation(u[:, s, :], xo[:, s, :], ACT.Square, accum_out=ssq[:, s:s + 1]).then_inc(ssq_ready, 1)

                def step(i, s, more=True):
                    logits_of(i, s, -RING)
                    split_u(i, s, -1)
                    square(i, s)
                    if more:
                        split_h(upto(i, s), 16 * i + 32, s)

                square(0, 0)
                split_h(1, 32, 0)
                split_u(0, 1, -1)
                square(0, 1)
                split_h(2, 32, 1)
                with act.Fori(1, LAST) as i:
                    for s in range(RING):
                        step(i, s)
                for s in range(RING):
                    step(LAST, s, False)
                logits_of(LAST + 1, 0, -RING)
                split_u(LAST + 1, 0, -1)
                logits_of(LAST + 1, 1, -RING)

            @block.vector
            def _(dve):
                def split_h(n1, s):
                    dve.wait_ge(h_hi_ready, n1)
                    dve.tensor_tensor(h_lo[:, s, :, :], h_raw[:, s, :, :], h_hi[:, s, :, :].bitcast(F32), ALU.subtract).then_inc(h_lo_ready, 1)

                split_h(1, 0)
                for k in range(KT):
                    dve.wait_ge(w_hi_ready, k + 1)
                    dve.tensor_tensor(w_lo[:, k, :], w_raw[:, k % WS, :], w_hi[:, k, :].bitcast(F32), ALU.subtract).then_inc(w_lo_ready, 1)
                    if k == 0:
                        split_h(2, 1)
                dve.wait_ge(mod_in, 64)
                dve.scalar_tensor_tensor(out=scale_b[:, :], in0=scale_b[:, :], scalar=1.0, in1=ng_b[:, :],
                                         op0=ALU.add, op1=ALU.mult).then_inc(mod_ready, 1)
                dve.wait_ge(mod_ready, 1)
                dve.wait_ge(w_hi_ready, KT + 1)
                dve.tensor_tensor(wr_lo[:, :, :], wr_raw[:, :, :], wr_hi[:, :, :].bitcast(F32), ALU.subtract).then_inc(w_lo_ready, 1)

                def residual(i, s):
                    n = upto(i, s)
                    dve.wait_ge(mm_done, n)
                    dve.wait_ge(x_out[s], 16 * i + 16)
                    dve.tensor_tensor(xo[:, s, :], psum_o[:, s, :], gate_b[:, :], ALU.mult).then_inc(gated, 1)
                    dve.wait_ge(gated, n)
                    dve.wait_ge(x_in[s], 16 * i + 16)
                    dve.tensor_tensor(xo[:, s, :], xo[:, s, :], xin[:, s, :], ALU.add).then_inc(xo_ready, 1)

                def split_u(i, s, n):
                    dve.wait_ge(u_hi_ready, upto(i, s, n))
                    dve.tensor_tensor(u_lo[:, :, :], psum_t[:, :].rearrange("p (k t) -> p k t", k=KT), u_hi[:, :, :].bitcast(F32), ALU.subtract).then_inc(u_lo_ready, 1)

                def normalise(i, s):
                    dve.wait_ge(rstd_ready, upto(i, s))
                    dve.scalar_tensor_tensor(out=u[:, s, :], in0=xo[:, s, :], scalar=rstd[:, s:s + 1], in1=scale_b[:, :],
                                             op0=ALU.mult, op1=ALU.mult).then_inc(um_ready, 1)

                residual(0, 0)
                split_h(RING + 1, 0)
                normalise(0, 0)
                residual(0, 1)
                split_u(0, 1, -1)
                split_h(RING + 2, 1)
                normalise(0, 1)

                def step(i, s, more=True):
                    residual(i, s)
                    split_u(i, s, -1)
                    if more:
                        split_h(upto(i, s, RING), s)
                    normalise(i, s)

                with dve.Fori(1, LAST) as i:
                    for s in range(RING):
                        step(i, s)
                for s in range(RING):
                    step(LAST, s, False)
                split_u(LAST + 1, 0, -1)

            @block.tensor
            def _(pe):
                def project(i, s, h, first=False):
                    if h == 0:
                        pe.wait_ge(h_lo_ready, upto(i, s))
                        if not first:
                            pe.wait_ge(gated, upto(i, s, -RING))
                    hs = slice(h * HALF, (h + 1) * HALF)
                    for k in range(KT):
                        if first and s == 0 and h == 0:
                            pe.wait_ge(w_lo_ready, k + 1)
                        last = split_mm(pe, psum_o[:, s, hs], (h_hi[:, s, k, :], h_lo[:, s, k, :]),
                                        (w_hi[:, k, hs], w_lo[:, k, hs]), k == 0, k == KT - 1)
                    if h == 1:
                        last.then_inc(mm_done, 1)

                def transpose_u(i, s, n, slot):
                    pe.wait_ge(u_ready, upto(i, s, n))
                    pe.wait_ge(u_lo_ready, upto(i, s, n - 1))
                    for k in range(KT):
                        last = pe.transpose(psum_t[:, k * P:(k + 1) * P], u[:, slot, k * P:(k + 1) * P], ident[:, :])
                    last.then_inc(tr_done, 1)

                def logit(i, s, n):
                    pe.wait_ge(u_lo_ready, upto(i, s, n))
                    pe.wait_ge(logits_ready, upto(i, s, n))
                    for k in range(KT):
                        last = split_mm(pe, psum_r[:, s, :], (u_hi[:, k, :], u_lo[:, k, :]), (wr_hi[:, k, :], wr_lo[:, k, :]), k == 0, k == KT - 1)
                    last.then_inc(r_done, 1)

                project(0, 0, 0, True)
                project(0, 0, 1, True)
                project(0, 1, 0, True)
                project(0, 1, 1, True)
                pe.wait_ge(w_lo_ready, KT + 1)
                pe.wait_ge(u_ready, 1)
                for k in range(KT):
                    last = pe.transpose(psum_t[:, k * P:(k + 1) * P], u[:, 0, k * P:(k + 1) * P], ident[:, :])
                last.then_inc(tr_done, 1)
                with pe.Fori(1, NT // RING) as i:
                    for s in range(RING):
                        project(i, s, 0)
                        logit(i, s, -RING)
                        project(i, s, 1)
                        transpose_u(i, s, -1, 1 - s)
                logit(LAST + 1, 0, -RING)
                transpose_u(LAST + 1, 0, -1, 1)
                logit(LAST + 1, 1, -RING)


def routing(nc, layer, logits, b_router, pos, pair_w, starts, tok_idx):
    with Phase(nc, f"rt{layer}") as ph:
        brb = ph.sb("brb", [P, E])
        iot = ph.sb("iot", [P, 256], I32)
        tid_i = ph.sb("tid_i", [P, NT], I32)
        tid = ph.sb("tid", [P, NT])
        io128 = ph.sb("io128", [P, P])
        rev = ph.sb("rev", [P, E])
        thr = ph.sb("thr", [P, E])
        reset = ph.sb("reset", [P, E, NT])
        ones = ph.sb("ones", [P, P])
        before = ph.sb("before", [P, P])
        probs = ph.sb("probs", [P, NT, E])
        sel = ph.sb("sel", [P, NT, E])
        work = ph.sb("work", [P, NT, E])
        sums = ph.sb("sums", [P, NT * GROUPS, 2])
        maxs = ph.sb("maxs", [P, NT * GROUPS, 2])
        gs = ph.sb("gs", [P, NT, GROUPS])
        ing = ph.sb("ing", [P, NT, GROUPS])
        col = ph.sb("col", [P, NT])
        rec = ph.sb("rec", [P, NT])
        oh = ph.sb("oh", [P, 2, NT, E])
        mask = ph.sb("mask", [P, NT, E])
        tot = ph.sb("tot", [P, E, NT])
        incl = ph.sb("incl", [P, E, NT])
        gt = ph.sb("gt", [P, E, NT])
        tiles = ph.sb("tiles", [P, E])
        ends = ph.sb("ends", [P, E + 1])
        base = ph.sb("base", [P, E])
        posf = ph.sb("posf", [P, 2, NT])
        slot = ph.sb("slot", [P, NT, E])
        ai = ph.sb("ai", [P, 2, NT], I32)
        af = ph.sb("af", [P, 2, NT])
        bf = ph.sb("bf", [P, 2, NT])
        ob = ph.sb("ob", [P, 2 * NT, P])
        oa = ph.sb("oa", [P, 2 * NT, MAX_TILES])
        ps_rank = ph.ps("ps_rank", [P, NT, E])
        ps_tot = ph.ps("ps_tot", [P, NT, E])
        ps_tab = ph.ps("ps_tab", [P, MAX_TILES])
        br_in = ph.sem("br_in")
        iota_ready = ph.sem("iota_ready")
        step = ph.sem("step")
        centred = ph.sem("centred")
        exp_ready = ph.sem("exp_ready")
        mask_ready = ph.sem("mask_ready")
        counted = ph.sem("counted")
        hot_ready = ph.sem("hot_ready")
        tab_done = ph.sem("tab_done")

        with ph.block() as block:
            @block.sync
            def _(sp):
                sp.dma_start(brb[:, :], b_router.rearrange("(a e) -> a e", a=1).to_broadcast([P, E])).then_inc(br_in, 16)

            @block.gpsimd
            def _(pool):
                pool.iota(iot[:, :], pattern=[[1, 256]], base=0, channel_multiplier=0).then_inc(iota_ready, 1)
                pool.iota(tid_i[:, :], pattern=[[P, NT]], base=0, channel_multiplier=1).then_inc(iota_ready, 1)
                pool.memset(ones[:, :], 1.0).then_inc(iota_ready, 1)
                pool.memset(reset[:, :, :], 1.0).then_inc(iota_ready, 1)
                pool.wait_ge(iota_ready, 4)
                pool.affine_select(out=before[:, :], in_=ones[:, :], compare_op=ALU.is_gt, fill=0.0, base=0,
                                   pattern=[[1, P]], channel_multiplier=-1).then_inc(iota_ready, 1)
                pool.memset(reset[:, :, 0:1], 0.0).then_inc(iota_ready, 1)

            @block.scalar
            def _(act):
                act.wait_ge(centred, 1)
                act.activation(work[:, :, :], work[:, :, :], ACT.Exp).then_inc(exp_ready, 1)

            @block.vector
            def _(dve):
                count = [0]

                def link(ins):
                    count[0] += 1
                    ins.then_inc(step, 1)
                    dve.wait_ge(step, count[0])

                def over_e(x):
                    return x.unsqueeze(2).to_broadcast([P, NT, E])

                dve.wait_ge(iota_ready, 6)
                dve.wait_ge(br_in, 16)
                link(dve.tensor_copy(tid[:, :], tid_i[:, :]))
                link(dve.tensor_copy(io128[:, :], iot[:, 0:P]))
                link(dve.tensor_scalar(rev[:, :], io128[:, 0:E], -1.0, float(E), ALU.mult, ALU.add))
                link(dve.tensor_scalar(thr[:, :], io128[:, 0:E], float(P), None, ALU.mult))
                link(dve.tensor_reduce(col[:, :], logits[:, :, :], AX.X, ALU.max))
                dve.tensor_tensor(work[:, :, :], logits[:, :, :], over_e(col[:, :]), ALU.subtract).then_inc(centred, 1)
                dve.wait_ge(exp_ready, 1)
                link(dve.tensor_reduce(col[:, :], work[:, :, :], AX.X, ALU.add))
                link(dve.reciprocal(rec[:, :], col[:, :]))
                link(dve.tensor_tensor(probs[:, :, :], work[:, :, :], over_e(rec[:, :]), ALU.mult))
                link(dve.tensor_tensor(sel[:, :, :], probs[:, :, :], brb[:, :].unsqueeze(1).to_broadcast([P, NT, E]), ALU.add))
                pair = sel[:, :, :].rearrange("p t (g a b) -> p (t g a) b", g=GROUPS, a=2)
                link(dve.tensor_tensor(sums[:, :, :].rearrange("p g a -> p (g a)"), pair[:, :, 0], pair[:, :, 1], ALU.add))
                link(dve.tensor_tensor(maxs[:, :, :].rearrange("p g a -> p (g a)"), pair[:, :, 0], pair[:, :, 1], ALU.max))
                flat = gs[:, :, :].rearrange("p t g -> p (t g)")
                link(dve.tensor_tensor(flat, maxs[:, :, 0], maxs[:, :, 1], ALU.add))
                link(dve.tensor_tensor(flat, flat, sums[:, :, 0], ALU.max))
                link(dve.tensor_tensor(flat, flat, sums[:, :, 1], ALU.max))

                def first_max(out, x, n):
                    wide = lambda c: c.unsqueeze(2).to_broadcast([P, NT, n])
                    link(dve.tensor_reduce(col[:, :], x, AX.X, ALU.max))
                    link(dve.tensor_tensor(out, x, wide(col[:, :]), ALU.is_equal))
                    link(dve.tensor_tensor(out, out, rev[:, 0:n].unsqueeze(1).to_broadcast([P, NT, n]), ALU.mult))
                    link(dve.tensor_reduce(col[:, :], out, AX.X, ALU.max))
                    link(dve.tensor_tensor(out, out, wide(col[:, :]), ALU.is_equal))

                first_max(ing[:, :, :], gs[:, :, :], GROUPS)
                link(dve.tensor_scalar(ing[:, :, :], ing[:, :, :], 1.0, BIG, ALU.subtract, ALU.mult))
                link(dve.tensor_tensor(sel[:, :, :].rearrange("p t (g a) -> p (t g) a", g=GROUPS), sel[:, :, :].rearrange("p t (g a) -> p (t g) a", g=GROUPS),
                                       ing[:, :, :].rearrange("p t g -> p (t g)").unsqueeze(2).to_broadcast([P, NT * GROUPS, PER_G]), ALU.add))
                first_max(oh[:, 0, :, :], sel[:, :, :], E)
                link(dve.scalar_tensor_tensor(out=sel[:, :, :], in0=oh[:, 0, :, :], scalar=-4.0 * BIG, in1=sel[:, :, :], op0=ALU.mult, op1=ALU.add))
                first_max(oh[:, 1, :, :], sel[:, :, :], E)
                dve.tensor_tensor(mask[:, :, :], oh[:, 0, :, :], oh[:, 1, :, :], ALU.add).then_inc(mask_ready, 1)
                for j in range(2):
                    link(dve.tensor_tensor(work[:, :, :], probs[:, :, :], oh[:, j, :, :], ALU.mult))
                    link(dve.tensor_reduce(pair_w[:, j, :], work[:, :, :], AX.X, ALU.add))
                link(dve.tensor_tensor(col[:, :], pair_w[:, 0, :], pair_w[:, 1, :], ALU.add))
                link(dve.reciprocal(rec[:, :], col[:, :]))
                for j in range(2):
                    link(dve.tensor_tensor(pair_w[:, j, :], pair_w[:, j, :], rec[:, :], ALU.mult))
                dve.wait_ge(counted, 1)
                link(dve.tensor_copy(tot[:, :, :], ps_tot[:, :, :].rearrange("p t e -> p e t")))
                et = lambda x: x[:, :, :].rearrange("p e t -> p (e t)")
                link(dve.tensor_tensor_scan(et(incl), et(reset), et(tot), 0.0, ALU.mult, ALU.add))
                link(dve.tensor_tensor(tot[:, :, :], incl[:, :, :], tot[:, :, :], ALU.subtract))
                link(dve.tensor_tensor(gt[:, :, :], incl[:, :, NT - 1:NT].to_broadcast([P, E, NT]), thr[:, :].unsqueeze(1).to_broadcast([P, E, NT]), ALU.is_gt))
                link(dve.tensor_reduce(tiles[:, :], gt[:, :, :], AX.X, ALU.add))
                link(dve.tensor_scalar(tiles[:, :], tiles[:, :], 1.0, None, ALU.max))
                link(dve.memset(ends[:, 0:1], 0.0))
                link(dve.tensor_tensor_scan(ends[:, 1:E + 1], ones[:, 0:E], tiles[:, :], 0.0, ALU.mult, ALU.add))
                link(dve.tensor_copy(starts[0:1, :], ends[0:1, :]))
                link(dve.tensor_scalar(base[:, :], ends[:, 0:E], float(P), None, ALU.mult))
                link(dve.tensor_tensor(slot[:, :, :], ps_rank[:, :, :], tot[:, :, :].rearrange("p e t -> p t e"), ALU.add))
                link(dve.tensor_tensor(slot[:, :, :], slot[:, :, :], base[:, :].unsqueeze(1).to_broadcast([P, NT, E]), ALU.add))
                for j in range(2):
                    link(dve.tensor_tensor(work[:, :, :], slot[:, :, :], oh[:, j, :, :], ALU.mult))
                    link(dve.tensor_reduce(posf[:, j, :], work[:, :, :], AX.X, ALU.add))
                link(dve.tensor_copy(ai[:, :, :], posf[:, :, :]))
                link(dve.tensor_scalar(ai[:, :, :], ai[:, :, :], 7, None, ALU.arith_shift_right))
                link(dve.tensor_copy(af[:, :, :], ai[:, :, :]))
                link(dve.scalar_tensor_tensor(out=bf[:, :, :], in0=af[:, :, :], scalar=-float(P), in1=posf[:, :, :], op0=ALU.mult, op1=ALU.add))
                link(dve.tensor_scalar(pos[:, :, :], posf[:, :, :], float(P), None, ALU.add))
                pairs = lambda x: x[:, :, :].rearrange("p j t -> p (j t)").unsqueeze(2)
                link(dve.tensor_tensor(ob[:, :, :], io128[:, :].unsqueeze(1).to_broadcast([P, 2 * NT, P]), pairs(bf).to_broadcast([P, 2 * NT, P]), ALU.is_equal))
                link(dve.tensor_tensor(oa[:, :, :], io128[:, 0:MAX_TILES].unsqueeze(1).to_broadcast([P, 2 * NT, MAX_TILES]),
                                       pairs(af).to_broadcast([P, 2 * NT, MAX_TILES]), ALU.is_equal))
                for j in range(2):
                    link(dve.tensor_tensor(oa[:, j * NT:(j + 1) * NT, :], oa[:, j * NT:(j + 1) * NT, :], tid[:, :].unsqueeze(2).to_broadcast([P, NT, MAX_TILES]), ALU.mult))
                dve.sem_inc(hot_ready, 1)
                dve.wait_ge(tab_done, 1)
                dve.tensor_copy(tok_idx[:, :], ps_tab[:, :])

            @block.tensor
            def _(pe):
                pe.wait_ge(iota_ready, 6)
                pe.wait_ge(mask_ready, 1)
                flat = mask[:, :, :].rearrange("p t e -> p (t e)")
                pe.matmul(ps_rank[:, :, :].rearrange("p t e -> p (t e)"), before[:, :], flat, start=True, stop=True)
                pe.matmul(ps_tot[:, :, :].rearrange("p t e -> p (t e)"), ones[:, :], flat, start=True, stop=True).then_inc(counted, 1)
                pe.wait_ge(hot_ready, 1)
                for m in range(2 * NT):
                    last = pe.matmul(ps_tab[:, :], ob[:, m, :], oa[:, m, :], start=(m == 0), stop=(m == 2 * NT - 1))
                last.then_inc(tab_done, 1)


def experts(nc, layer, u_src, w_gate, w_up, w_down, starts, tok_idx, ys, ident):
    WG = 4
    WD = 4
    NCH = 2 * WG + WD
    RAW = 6
    with Phase(nc, f"ex{layer}") as ph:
        w_raw = ph.sb("w_raw", [P, RAW, D])
        w_hi = ph.sb("w_hi", [P, NCH, D], F32R)
        w_lo = ph.sb("w_lo", [P, NCH, D], F32R)
        idx = ph.sb("idx", [P, 1], I32)
        rows = ph.sb("rows", [P, D])
        u_hi = ph.sb("u_hi", [P, KT, P], F32R)
        u_lo = ph.sb("u_lo", [P, KT, P], F32R)
        sig = ph.sb("sig", [P, DE])
        a = ph.sb("a", [P, DE])
        a_hi = ph.sb("a_hi", [P, FT, P], F32R)
        a_lo = ph.sb("a_lo", [P, FT, P], F32R)
        out = ph.sb("out", [P, D])
        ps_u = ph.ps("ps_u", [P, D])
        ps_g = ph.ps("ps_g", [P, 2, DE])
        ps_a = ph.ps("ps_a", [P, DE])
        ps_o = ph.ps("ps_o", [P, D])
        raw_in = [ph.sem(f"raw_in{s}") for s in range(RAW)]
        whi_ready = ph.sem("whi_ready")
        wlo_ready = ph.sem("wlo_ready")
        idx_ready = ph.sem("idx_ready")
        rows_in = ph.sem("rows_in")
        passed = ph.sem("passed")
        tr_done = ph.sem("tr_done")
        uhi_ready = ph.sem("uhi_ready")
        ulo_ready = ph.sem("ulo_ready")
        gate_done = ph.sem("gate_done")
        up_done = ph.sem("up_done")
        sig_ready = ph.sem("sig_ready")
        gated = ph.sem("gated")
        a_ready = ph.sem("a_ready")
        at_done = ph.sem("at_done")
        ahi_ready = ph.sem("ahi_ready")
        alo_ready = ph.sem("alo_ready")
        down_done = ph.sem("down_done")
        out_ready = ph.sem("out_ready")
        out_done = ph.sem("out_done")

        def bounds(eng, e):
            return (eng.value_load(starts[0:1, bass.ds(e, 1)], min_val=0, max_val=MAX_TILES - 1),
                    eng.value_load(starts[0:1, bass.ds(e + 1, 1)], min_val=1, max_val=MAX_TILES - 1))

        with ph.block() as block:
            @block.sync
            def _(sp):
                def load(e, c, first):
                    if c < 2 * WG:
                        w = w_gate if c < WG else w_up
                        k = 2 * (c % WG)
                        src = w[layer, bass.ds(e, 1), k * P:(k + 2) * P, :].rearrange("a (k p) n -> p (a k) n", p=P)
                        dst = w_raw[:, c % RAW, :].rearrange("p (k n) -> p k n", k=2)
                    else:
                        f = c - 2 * WG
                        src = w_down[layer, bass.ds(e, 1), f * P:(f + 1) * P, :].rearrange("a p n -> p (a n)")
                        dst = w_raw[:, c % RAW, :]
                    if not first:
                        sp.wait_ge(wlo_ready, e * NCH + (c - RAW + 1))
                    sp.dma_start(dst, src).then_inc(raw_in[c % RAW], 16)

                for c in range(NCH):
                    load(0, c, c < RAW)
                with sp.Fori(1, E) as e:
                    for c in range(NCH):
                        load(e, c, False)

            @block.gpsimd
            def _(pool):
                pool.memset(out[:, :], 0.0).then_inc(idx_ready, 1)

                def fetch(t):
                    pool.tensor_copy(idx[:, :], tok_idx[:, bass.ds(t, 1)]).then_inc(idx_ready, 1)
                    pool.wait_ge(idx_ready, t + 2)
                    stand(pool, passed)
                    pool.indirect_dma_start(rows[:, :], None, u_src, bass.IndirectOffsetOnAxis(ap=idx[:, 0:1], axis=0)).then_inc(rows_in, 16)
                    pool.wait_ge(rows_in, t * 16 + 16)
                    pool.wait_ge(tr_done, t + 1)

                fetch(0)
                with pool.Fori(0, E) as e:
                    first, end = bounds(pool, e)
                    with pool.Fori(first, end) as t:
                        fetch(t + 1)

            @block.scalar
            def _(act):
                act.sem_inc(out_done, 16)

                def split_w(e, c):
                    act.wait_ge(raw_in[c % RAW], e * (16 * NCH // RAW) + 16 * (c // RAW + 1))
                    act.activation(w_hi[:, c, :], w_raw[:, c % RAW, :], ACT.Copy).then_inc(whi_ready, 1)

                def split_u(t):
                    act.wait_ge(tr_done, t + 1)
                    act.activation(u_hi[:, :, :].rearrange("p k t -> p (k t)"), ps_u[:, :], ACT.Copy).then_inc(uhi_ready, 1)

                def store(t):
                    act.wait_ge(down_done, t + 1)
                    act.wait_ge(out_done, t * 16 + 16)
                    act.activation(out[:, :], ps_o[:, :], ACT.Copy).then_inc(out_ready, 1)
                    act.wait_ge(out_ready, t + 1)
                    act.dma_start(ys[bass.ds(t * P, P), :], out[:, :]).then_inc(out_done, 16)

                split_u(0)
                for c in range(NCH):
                    split_w(0, c)

                def tile(t):
                    act.wait_ge(gate_done, t + 1)
                    act.activation(sig[:, :], ps_g[:, 0, :], ACT.Sigmoid).then_inc(sig_ready, 1)
                    store(t)
                    act.wait_ge(at_done, t + 1)
                    act.activation(a_hi[:, :, :].rearrange("p f t -> p (f t)"), ps_a[:, :], ACT.Copy).then_inc(ahi_ready, 1)
                    split_u(t + 1)

                with act.Fori(0, E - 1) as e:
                    first, end = bounds(act, e)
                    with act.Fori(first, end) as t:
                        tile(t)
                    for c in range(NCH):
                        if c == 2 * WG:
                            act.wait_ge(down_done, end + 1)
                        split_w(e + 1, c)
                first, end = bounds(act, E - 1)
                with act.Fori(first, end) as t:
                    tile(t)
                store(end)
                act.wait_ge(out_done, end * 16 + 32)
                stand(act, passed)

            @block.vector
            def _(dve):
                def split_w(e, c):
                    dve.wait_ge(whi_ready, e * NCH + (c + 1))
                    dve.tensor_tensor(w_lo[:, c, :], w_raw[:, c % RAW, :], w_hi[:, c, :].bitcast(F32), ALU.subtract).then_inc(wlo_ready, 1)

                def split_u(t):
                    dve.wait_ge(uhi_ready, t + 1)
                    dve.tensor_tensor(u_lo[:, :, :].rearrange("p k t -> p (k t)"), ps_u[:, :], u_hi[:, :, :].rearrange("p k t -> p (k t)").bitcast(F32),
                                      ALU.subtract).then_inc(ulo_ready, 1)

                split_u(0)
                for c in range(NCH):
                    split_w(0, c)

                def tile(t):
                    dve.wait_ge(sig_ready, t + 1)
                    dve.tensor_tensor(sig[:, :], sig[:, :], ps_g[:, 0, :], ALU.mult).then_inc(gated, 1)
                    dve.wait_ge(gated, t + 1)
                    dve.wait_ge(up_done, t + 1)
                    dve.tensor_tensor(a[:, :], sig[:, :], ps_g[:, 1, :], ALU.mult).then_inc(a_ready, 1)
                    dve.wait_ge(ahi_ready, t + 1)
                    dve.tensor_tensor(a_lo[:, :, :].rearrange("p f t -> p (f t)"), ps_a[:, :], a_hi[:, :, :].rearrange("p f t -> p (f t)").bitcast(F32),
                                      ALU.subtract).then_inc(alo_ready, 1)
                    split_u(t + 1)

                with dve.Fori(0, E - 1) as e:
                    first, end = bounds(dve, e)
                    with dve.Fori(first, end) as t:
                        tile(t)
                    for c in range(NCH):
                        split_w(e + 1, c)
                first, end = bounds(dve, E - 1)
                with dve.Fori(first, end) as t:
                    tile(t)

            @block.tensor
            def _(pe):
                def transpose_rows(t):
                    pe.wait_ge(rows_in, t * 16 + 16)
                    for k in range(KT):
                        last = pe.transpose(ps_u[:, k * P:(k + 1) * P], rows[:, k * P:(k + 1) * P], ident[:, :])
                    last.then_inc(tr_done, 1)

                def up_or_gate(e, which, t):
                    for k in range(KT):
                        c = which * WG + k // 2
                        if k % 2 == 0:
                            pe.wait_ge(wlo_ready, e * NCH + (c + 1))
                        ws = slice((k % 2) * DE, (k % 2 + 1) * DE)
                        last = split_mm(pe, ps_g[:, which, :], (u_hi[:, k, :], u_lo[:, k, :]), (w_hi[:, c, ws], w_lo[:, c, ws]), k == 0, k == KT - 1)
                    return last

                def tile(e, t):
                    pe.wait_ge(ulo_ready, t + 1)
                    up_or_gate(e, 0, t).then_inc(gate_done, 1)
                    up_or_gate(e, 1, t).then_inc(up_done, 1)
                    transpose_rows(t + 1)
                    pe.wait_ge(a_ready, t + 1)
                    for f in range(FT):
                        last = pe.transpose(ps_a[:, f * P:(f + 1) * P], a[:, f * P:(f + 1) * P], ident[:, :])
                    last.then_inc(at_done, 1)
                    pe.wait_ge(alo_ready, t + 1)
                    pe.wait_ge(out_ready, t + 1)
                    for h in range(2):
                        hs = slice(h * HALF, (h + 1) * HALF)
                        for f in range(FT):
                            c = 2 * WG + f
                            if h == 0:
                                pe.wait_ge(wlo_ready, e * NCH + (c + 1))
                            last = split_mm(pe, ps_o[:, hs], (a_hi[:, f, :], a_lo[:, f, :]), (w_hi[:, c, hs], w_lo[:, c, hs]), f == 0, f == FT - 1)
                    last.then_inc(down_done, 1)

                pe.wait_ge(idx_ready, 1)
                for h in range(2):
                    last = pe.matmul(ps_o[:, h * HALF:(h + 1) * HALF], ident[:, :], out[:, h * HALF:(h + 1) * HALF], start=True, stop=True)
                last.then_inc(down_done, 1)
                transpose_rows(0)
                with pe.Fori(0, E) as e:
                    first, end = bounds(pe, e)
                    with pe.Fori(first, end) as t:
                        tile(e, t)


def final(nc, x_src, ys, pos, pair_w, gate_row, final_g, out):
    with Phase(nc, "fin") as ph:
        xin = ph.sb("xin", [P, RING, D])
        row_a = ph.sb("row_a", [P, RING, D])
        row_b = ph.sb("row_b", [P, RING, D])
        yo = ph.sb("yo", [P, RING, D])
        gate_b = ph.sb("gate_b", [P, D])
        fg_b = ph.sb("fg_b", [P, D])
        ssq = ph.sb("ssq", [P, RING])
        rstd = ph.sb("rstd", [P, RING])
        mhalf = ph.sb("mhalf", [P, 1])
        junk = ph.sb("junk", [P, D])
        idx = ph.sb("idx", [P, RING, 2], I32)
        wts = ph.sb("wts", [P, RING, 2])
        vec_in = ph.sem("vec_in")
        const_ready = ph.sem("const_ready")
        x_in = [ph.sem(f"x_in{s}") for s in range(RING)]
        rows_in = [ph.sem(f"rows_in{s}") for s in range(RING)]
        idx_ready = ph.sem("idx_ready")
        wts_ready = ph.sem("wts_ready")
        ra_ready = ph.sem("ra_ready")
        rb_ready = ph.sem("rb_ready")
        mix_ready = ph.sem("mix_ready")
        x2_ready = ph.sem("x2_ready")
        ssq_ready = ph.sem("ssq_ready")
        var_ready = ph.sem("var_ready")
        rstd_ready = ph.sem("rstd_ready")
        passed = ph.sem("passed")
        y_ready = ph.sem("y_ready")
        y_out = [ph.sem(f"y_out{s}") for s in range(RING)]
        UM = -1

        with ph.block() as block:
            @block.sync
            def _(sp):
                def load(n, s):
                    sp.dma_start(xin[:, s, :], x_src[bass.ds(n * P, P), :]).then_inc(x_in[s], 16)

                def step(i, s):
                    if live(i, s, UM):
                        q = slot(s, UM)
                        sp.wait_ge(y_ready, upto(i, s, UM))
                        if live(i, s, UM + RING):
                            load(i * RING + (s + UM + RING), q)
                        sp.dma_start(out[0, bass.ds((i * RING + (s + UM)) * P, P), :], yo[:, q, :]).then_inc(y_out[q], 16)

                for s in range(RING):
                    load(s, s)
                sp.dma_start(gate_b[:, :], rowcast(gate_row)).then_inc(vec_in, 16)
                sp.dma_start(fg_b[:, :], final_g.rearrange("(a d) -> a d", a=1).to_broadcast([P, D])).then_inc(vec_in, 16)
                skewed(sp, step)
                for s in range(RING):
                    sp.wait_ge(y_out[s], 16 * (NT // RING + 1))

            @block.gpsimd
            def _(pool):
                pool.memset(mhalf[:, :], -0.5).then_inc(const_ready, 1)
                pool.wait_ge(const_ready, 1)

                def gather(n, s, count):
                    pool.tensor_copy(idx[:, s, :], pos[:, :, bass.ds(n, 1)].rearrange("p j a -> p (j a)")).then_inc(idx_ready, 1)
                    pool.wait_ge(idx_ready, count)
                    stand(pool, passed)
                    for j, dst in enumerate((row_a, row_b)):
                        pool.indirect_dma_start(dst[:, s, :], None, ys, bass.IndirectOffsetOnAxis(ap=idx[:, s, j:j + 1], axis=0)).then_inc(rows_in[s], 16)

                def step(i, s):
                    if live(i, s, RING):
                        pool.wait_ge(x2_ready, upto(i, s))
                        gather(i * RING + (s + RING), s, upto(i, s, RING))
                    if live(i, s):
                        pool.wait_ge(ssq_ready, upto(i, s, 1))
                        stand(pool, passed)
                        pool.tensor_scalar(rstd[:, s:s + 1], ssq[:, s:s + 1], 1.0 / D, EPS, ALU.mult, ALU.add).then_inc(var_ready, 1)
                        pool.wait_ge(var_ready, upto(i, s))
                        pool.tensor_tensor(rstd[:, s:s + 1], rstd[:, s:s + 1], mhalf[:, 0:1], ALU.pow).then_inc(rstd_ready, 1)

                for s in range(RING):
                    gather(s, s, s + 1)
                skewed(pool, step)

            @block.scalar
            def _(act):
                for s in range(RING):
                    act.sem_inc(y_out[s], 16)
                act.sem_inc(ssq_ready, 1)

                def weigh(i, s, n):
                    act.wait_ge(rows_in[slot(s, n)], 32 * uses(i, s, n))
                    act.wait_ge(wts_ready, upto(i, s, n))
                    act.activation(row_a[:, slot(s, n), :], row_a[:, slot(s, n), :], ACT.Copy, scale=wts[:, slot(s, n), 0:1]).then_inc(ra_ready, 1)

                def step(i, s):
                    if live(i, s):
                        act.wait_ge(x2_ready, upto(i, s))
                        act.wait_ge(ssq_ready, upto(i, s))
                        act.activation(junk[:, :], xin[:, s, :], ACT.Square, accum_out=ssq[:, s:s + 1]).then_inc(ssq_ready, 1)
                    if live(i, s, 1):
                        weigh(i, s, 1)

                weigh(0, 0, 0)
                skewed(act, step)

            @block.vector
            def _(dve):
                def weights(i, s, n):
                    dve.tensor_copy(wts[:, slot(s, n), :], pair_w[:, :, bass.ds(i * RING + (s + n), 1)].rearrange("p j a -> p (j a)")).then_inc(wts_ready, 1)

                def step(i, s):
                    if live(i, s):
                        dve.wait_ge(ra_ready, upto(i, s))
                        dve.wait_ge(wts_ready, upto(i, s))
                        dve.scalar_tensor_tensor(out=row_b[:, s, :], in0=row_b[:, s, :], scalar=wts[:, s, 1:2], in1=row_a[:, s, :],
                                                 op0=ALU.mult, op1=ALU.add).then_inc(rb_ready, 1)
                        if live(i, s, 1):
                            weights(i, s, 1)
                        dve.wait_ge(rb_ready, upto(i, s))
                        dve.tensor_tensor(row_b[:, s, :], row_b[:, s, :], gate_b[:, :], ALU.mult).then_inc(mix_ready, 1)
                        dve.wait_ge(mix_ready, upto(i, s))
                        dve.wait_ge(x_in[s], 16 * uses(i, s))
                        dve.tensor_tensor(xin[:, s, :], xin[:, s, :], row_b[:, s, :], ALU.add).then_inc(x2_ready, 1)
                    if live(i, s, UM):
                        q = slot(s, UM)
                        dve.wait_ge(rstd_ready, upto(i, s, UM))
                        dve.wait_ge(x2_ready, upto(i, s, UM))
                        dve.wait_ge(y_out[q], 16 * uses(i, s, UM))
                        dve.scalar_tensor_tensor(out=yo[:, q, :], in0=xin[:, q, :], scalar=rstd[:, q:q + 1], in1=fg_b[:, :],
                                                 op0=ALU.mult, op1=ALU.mult).then_inc(y_ready, 1)

                weights(0, 0, 0)
                dve.wait_ge(vec_in, 32)
                skewed(dve, step)


def trunk(nc, x, c, norm1_g, norm2_g, w_ada, b_ada, m_w_in, m_b_gates, m_norm_g, m_w_out,
          c_w_in, c_conv_w, c_conv_b, c_w_out, w_router, b_router, e_w_gate, e_w_up, e_w_down, final_g, out):
    dram = lambda name, shape: nc.dram_tensor(name, shape, F32, kind="Internal").ap()
    mod_rows = dram("mod_rows", (2, 6, D))
    x1 = dram("x1", (T, D))
    x2 = dram("x2", (T, D))
    u2 = dram("u2", (T, D))
    ys = dram("ys", (MAX_TILES * P, D))
    proj_t = dram("proj_t", (NCOL, T))
    gates_t = dram("gates_t", (2 * HEADS, T))
    h_t = dram("h_t", (D, T))
    gate_d = (dram("ends_d", (HEADS * NT, 2)), dram("seq_d", (HEADS * NT, 1)), dram("rows_d", (HEADS * NT, 2 * P)), dram("decay_d", (HEADS * NT, 1)))

    with ExitStack() as ctx:
        sb = lambda name, shape, dt=F32: ctx.enter_context(nc.sbuf_tensor(name, shape, dt))
        ident = sb("ident", [P, P])
        logits = sb("logits", [P, NT, E])
        pos = sb("pos", [P, 2, NT], I32)
        pair_w = sb("pair_w", [P, 2, NT])
        starts = sb("starts", [1, E + 1], I32)
        tok_idx = sb("tok_idx", [P, MAX_TILES], I32)

        adaln(nc, c, w_ada, b_ada, mod_rows, ident)
        for layer in range(2):
            if layer == 0:
                in_proj(nc, 0, x[0, :, :], None, norm1_g, mod_rows, m_w_in[0, :, :], proj_t, ident, gates=(m_b_gates, gates_t), blank=ys)
                mlstm(nc, proj_t, gates_t, gate_d, m_norm_g, h_t, ident)
                out_proj(nc, 0, h_t, m_w_out[0, :, :], x[0, :, :], x1, u2, norm2_g, mod_rows, w_router, logits, ident)
            else:
                in_proj(nc, 1, x1, x2, norm1_g, mod_rows, c_w_in[0, :, :], h_t, ident,
                        combine=(ys, pos, pair_w, mod_rows[0, 5:6, :]), conv=(c_conv_w, c_conv_b))
                out_proj(nc, 1, h_t, c_w_out[0, :, :], x2, x1, u2, norm2_g, mod_rows, w_router, logits, ident)
            routing(nc, layer, logits, b_router, pos, pair_w, starts, tok_idx)
            experts(nc, layer, u2, e_w_gate, e_w_up, e_w_down, starts, tok_idx, ys, ident)
        final(nc, x1, ys, pos, pair_w, mod_rows[1, 5:6, :], final_g, out)


_INS = ["x", "c", "norm1_g", "norm2_g", "w_ada", "b_ada", "m_w_in", "m_b_gates", "m_norm_g", "m_w_out",
        "c_w_in", "c_conv_w", "c_conv_b", "c_w_out", "w_router", "b_router", "e_w_gate", "e_w_up", "e_w_down", "final_g"]


def kernel(**inputs):
    import numpy as _np
    import concourse.bacc as _bacc
    from concourse.bass_utils import run_bass_kernel_spmd as _run

    nc = _bacc.Bacc("TRN2", target_bir_lowering=False, num_devices=1)
    arrays, args = {}, []
    for name in _INS:
        a = _np.ascontiguousarray(inputs[name])
        arrays[f"in_{name}_dram"] = a
        args.append(nc.dram_tensor(f"in_{name}_dram", a.shape, mybir.dt.from_np(a.dtype), kind="ExternalInput").ap())
    args.append(nc.dram_tensor("out_0_dram", (1, T, D), F32, kind="ExternalOutput").ap())
    trunk(nc, *args)
    r = _run(nc, [arrays], core_ids=[0])
    return r.results[0]["out_0_dram"]
```

```python
import concourse.bass as bass
from concourse import mybir
from contextlib import ExitStack

F32 = mybir.dt.float32
F32R = mybir.dt.float32r
I32 = mybir.dt.int32
ACT = mybir.ActivationFunctionType
ALU = mybir.AluOpType
AX = mybir.AxisListType

P = 128
D = 1024
T = 2048
KT = D // P
NT = T // P
HALF = 512
NBLK = T // HALF
HEADS = 4
DQK = 128
DV = 256
NCOL = 3 * D
NCHUNK = NCOL // P
E = 16
GROUPS = 4
PER_G = E // GROUPS
DE = 512
FT = DE // P
MAX_TILES = 48
EPS = 1e-6
BIG = 1e30
RING = 2
MOD_L = 6
MOD_ROWS = 2 * MOD_L
ADA_FIRST = 2


class Phase:

    def __init__(self, nc, name):
        self.nc, self.name, self.stack, self.sems = nc, name, ExitStack(), []

    def __enter__(self):
        self.stack.__enter__()
        return self

    def __exit__(self, *a):
        self.nc.clear_and_free_semaphores(self.sems)
        self.nc.all_engine_barrier()
        return self.stack.__exit__(*a)

    def sb(self, name, shape, dt=F32):
        return self.stack.enter_context(self.nc.sbuf_tensor(f"{self.name}_{name}", shape, dt))

    def ps(self, name, shape):
        return self.stack.enter_context(self.nc.psum_tensor(f"{self.name}_{name}", shape, F32))

    def sem(self, name):
        self.sems.append(self.nc.alloc_semaphore(f"{self.name}_{name}"))
        return self.sems[-1]

    def block(self):
        return self.nc.Block()


def split_mm(pe, out, lhs, rhs, start, stop):
    pe.matmul(out, lhs[0], rhs[0], start=start, stop=False)
    pe.matmul(out, lhs[0], rhs[1], start=False, stop=False)
    return pe.matmul(out, lhs[1], rhs[0], start=False, stop=stop)


def stand(eng, passed):
    eng.sem_inc(passed, 1)


def upto(i, s, n=0):
    return i * RING + (s + n + 1)


def slot(s, n=0):
    return (s + n) % RING


def uses(i, s, n=0):
    return i + ((s + n) // RING + 1)


def live(i, s, n=0):
    return not isinstance(i, int) or 0 <= i * RING + s + n < NT


def skewed(eng, step, head=2, behind=2, ahead=1, between=None):
    for i in range(head):
        for s in range(RING):
            step(i, s)
    if between:
        between()
    with eng.Fori(head, NT // RING - ahead) as i:
        for s in range(RING):
            step(i, s)
    for i in range(NT // RING - ahead, NT // RING + behind):
        for s in range(RING):
            step(i, s)


def cols(ap):
    return ap.rearrange("(k p) -> p k", p=P)


def rowcast(ap):
    return ap.to_broadcast([P, ap.shape[1]])


def adaln(nc, c, w_ada, b_ada, mod_rows, cond, ones, ident):
    with Phase(nc, "ada") as ph:
        ccol = ph.sb("ccol", [P, KT])
        sig = ph.sb("sig", [P, KT])
        w = ph.sb("w", [P, ADA_FIRST, KT, D])
        acc = ph.sb("acc", [P, ADA_FIRST, D])
        row = ph.sb("row", [1, ADA_FIRST, D])
        psum = ph.ps("psum", [P, ADA_FIRST, D])
        c_in = ph.sem("c_in")
        b_in = ph.sem("b_in")
        w_in = [[ph.sem(f"w_in{g}_{k}") for k in range(KT)] for g in range(ADA_FIRST)]
        sig_ready = ph.sem("sig_ready")
        cond_ready = ph.sem("cond_ready")
        ones_ready = ph.sem("ones_ready")
        mac = ph.sem("mac")
        sum_ready = ph.sem("sum_ready")
        row_ready = ph.sem("row_ready")
        row_out = ph.sem("row_out")
        id0 = ph.sem("id0")

        with ph.block() as block:
            @block.sync
            def _(sp):
                with nc.allow_non_contiguous_dma(reason="4 KB vector laid over the partitions"):
                    sp.dma_start(ccol[:, :], cols(c[0, :])).then_inc(c_in, 16)
                for g in range(ADA_FIRST):
                    for k in range(KT):
                        sp.dma_start(w[:, g, k, :], w_ada[0, k * P:(k + 1) * P, g * D:(g + 1) * D]).then_inc(w_in[g][k], 16)
                    sp.dma_start(row[0:1, g, :], b_ada[0:1, g * D:(g + 1) * D]).then_inc(b_in, 16)
                for g in range(ADA_FIRST):
                    sp.wait_ge(row_ready, g + 1)
                    sp.dma_start(mod_rows[g:g + 1, :], row[0:1, g, :]).then_inc(row_out, 16)
                sp.wait_ge(row_out, 16 * ADA_FIRST)

            @block.gpsimd
            def _(pool):
                pool.memset(ones[:, :], 1.0).then_inc(ones_ready, 1)
                pool.memset(ident[:, :], 0.0).then_inc(id0, 1)
                pool.wait_ge(id0, 1)
                pool.affine_select(out=ident[:, :], in_=ident[:, :], compare_op=ALU.not_equal, fill=1.0,
                                   base=0, pattern=[[-1, P]], channel_multiplier=1).then_inc(id0, 1)
                pool.wait_ge(id0, 2)

            @block.scalar
            def _(act):
                act.wait_ge(c_in, 16)
                act.activation(sig[:, :], ccol[:, :], ACT.Sigmoid).then_inc(sig_ready, 1)

            @block.vector
            def _(dve):
                dve.wait_ge(sig_ready, 1)
                dve.tensor_tensor(cond[:, :], ccol[:, :], sig[:, :], ALU.mult).then_inc(cond_ready, 1)
                dve.wait_ge(cond_ready, 1)
                for g in range(ADA_FIRST):
                    for k in range(KT):
                        dve.wait_ge(w_in[g][k], 16)
                        if k == 0:
                            dve.tensor_scalar(acc[:, g, :], w[:, g, k, :], cond[:, k:k + 1], None, ALU.mult).then_inc(mac, 1)
                        else:
                            dve.wait_ge(mac, g * KT + k)
                            dve.scalar_tensor_tensor(out=acc[:, g, :], in0=w[:, g, k, :], scalar=cond[:, k:k + 1],
                                                     in1=acc[:, g, :], op0=ALU.mult, op1=ALU.add).then_inc(mac, 1)
                dve.wait_ge(b_in, 16 * ADA_FIRST)
                for g in range(ADA_FIRST):
                    dve.wait_ge(sum_ready, g + 1)
                    dve.tensor_tensor(row[0:1, g, :], psum[0:1, g, :], row[0:1, g, :], ALU.add).then_inc(row_ready, 1)

            @block.tensor
            def _(pe):
                pe.wait_ge(ones_ready, 1)
                for g in range(ADA_FIRST):
                    pe.wait_ge(mac, (g + 1) * KT)
                    for h in range(2):
                        last = pe.matmul(psum[0:1, g, h * HALF:(h + 1) * HALF], ones[:, 0:1],
                                         acc[:, g, h * HALF:(h + 1) * HALF], start=True, stop=True)
                    last.then_inc(sum_ready, 1)


def in_proj(nc, layer, x_src, x_dst, norm_g, mod_rows, w_in, out_t, ident, combine=None, gates=None, conv=None, blank=None, ada=None):
    with Phase(nc, f"in{layer}") as ph:
        u_hi = ph.sb("u_hi", [P, KT, T], F32R)
        u_lo = ph.sb("u_lo", [P, KT, T], F32R)
        w_raw = ph.sb("w_raw", [P, RING, KT, P])
        w_hi = ph.sb("w_hi", [P, RING, KT, P], F32R)
        w_lo = ph.sb("w_lo", [P, RING, KT, P], F32R)
        work = ph.sb("work", [P, (12 if combine else 9) * D])
        junk = ph.sb("junk", [P, D])
        view = lambda at, n: work[:, at * D:(at + n) * D]
        xin = view(0, 2).rearrange("p (s d) -> p s d", s=RING)
        row_a = view(2, 2).rearrange("p (s d) -> p s d", s=RING)
        row_b = view(4, 2).rearrange("p (s d) -> p s d", s=RING)
        xr = view(8, 2).rearrange("p (s d) -> p s d", s=RING) if combine else xin
        u = view(10, 2).rearrange("p (s d) -> p s d", s=RING) if combine else row_a
        ng_b = view(11, 1) if combine else view(3, 1)
        scale_b, shift_b = view(6, 1), view(7, 1)
        stage = view(0, 4).rearrange("p (s t) -> p s t", s=RING)
        gate_rows = view(4, 2)
        c_rows = view(4, 2)
        z_rows = work[:, 6 * D:6 * D + 2 + T]
        ssq = ph.sb("ssq", [P, RING])
        rstd = ph.sb("rstd", [P, RING])
        mhalf = ph.sb("mhalf", [P, 1])
        idx = ph.sb("idx", [P, RING, 2], I32)
        wts = ph.sb("wts", [P, RING, 2])
        psum_t = ph.ps("psum_t", [P, RING, D])
        psum_o = ph.ps("psum_o", [P, NBLK, HALF])
        mod_in = ph.sem("mod_in")
        mod_ready = ph.sem("mod_ready")
        x_in = [ph.sem(f"x_in{s}") for s in range(RING)]
        ssq_ready = ph.sem("ssq_ready")
        var_ready = ph.sem("var_ready")
        rstd_ready = ph.sem("rstd_ready")
        passed = ph.sem("passed")
        um_ready = ph.sem("um_ready")
        u_ready = ph.sem("u_ready")
        tr_done = ph.sem("tr_done")
        hi_done = ph.sem("hi_done")
        lo_done = ph.sem("lo_done")
        const_ready = ph.sem("const_ready")
        wr_in = [ph.sem(f"wr_in{s}") for s in range(RING)]
        w_hi_ready = ph.sem("w_hi_ready")
        w_lo_ready = ph.sem("w_lo_ready")
        blk_done = ph.sem("blk_done")
        ev_act = ph.sem("ev_act")
        out_done = [ph.sem(f"out_done{s}") for s in range(RING)]
        if combine:
            ys, pos, pair_w = combine
            rows_in = [ph.sem(f"rows_in{s}") for s in range(RING)]
            idx_ready = ph.sem("idx_ready")
            wts_ready = ph.sem("wts_ready")
            ra_added = ph.sem("ra_added")
            x2_ready = ph.sem("x2_ready")
            x_out = [ph.sem(f"x_out{s}") for s in range(RING)]
        if blank is not None:
            zero = ph.sb("zero", [P, D])
            zero_ready = ph.sem("zero_ready")
            blank_out = ph.sem("blank_out")
        if gates:
            b_gates, gates_t = gates
            gw_raw = ph.sb("gw_raw", [P, KT, 8])
            gw_hi = ph.sb("gw_hi", [P, KT, 8], F32R)
            gw_lo = ph.sb("gw_lo", [P, KT, 8], F32R)
            gbias = ph.sb("gbias", [8, 1])
            gw_in = ph.sem("gw_in")
            gw_ready = ph.sem("gw_ready")
            gates_ev = ph.sem("gates_ev")
            gates_out = ph.sem("gates_out")
        if ada:
            w_ada, b_ada, cond, ones = ada
            ada_w = (view(6, 1), view(7, 1))
            ada_acc = view(8, 1)
            ada_row = ph.sb("ada_row", [1, D])
            ada_in = [ph.sem(f"ada_in{s}") for s in range(RING)]
            bias_in = ph.sem("bias_in")
            mac = ph.sem("mac")
            sum_ready = ph.sem("sum_ready")
            row_ready = ph.sem("row_ready")
            row_out = ph.sem("row_out")
        if conv:
            conv_w, conv_b = conv
            taps = ph.sb("taps", [P, KT, 4])
            tap = ph.sb("tap", [P, RING, 4])
            taps_in = ph.sem("taps_in")
            tap_ready = ph.sem("tap_ready")
            z_ready = ph.sem("z_ready")
            zc_ready = ph.sem("zc_ready")
            y_ready = ph.sem("y_ready")
        m_scale, m_shift = 1, 0
        CH = 6 if conv else 2
        if conv:
            kind_at = (D, 2 * D, 0)
            chunk_col = lambda i, q: kind_at[q % 3] + P * (q // 3) + i * (2 * P)
        else:
            chunk_col = lambda i, q: i * (CH * P) + q * P
        BODIES = NCHUNK // CH
        LOOPED = MOD_ROWS - ADA_FIRST if ada else BODIES - 1
        UM, HI, LO = (-1, -2, -3) if combine else (0, -1, -1)

        with ph.block() as block:
            @block.sync
            def _(sp):
                def load_x(n, s):
                    sp.dma_start(xin[:, s, :], x_src[bass.ds(n * P, P), :]).then_inc(x_in[s], 16)

                def load_w(col, s):
                    src = w_in[:, bass.ds(col, P)].rearrange("(k p) n -> p k n", p=P)
                    sp.dma_start(w_raw[:, s, :, :], src).then_inc(wr_in[s], 16)

                load_x(0, 0)
                sp.dma_start(scale_b, rowcast(mod_rows[MOD_L * layer + m_scale:MOD_L * layer + m_scale + 1, :])).then_inc(mod_in, 16)
                sp.dma_start(ng_b, rowcast(norm_g[layer:layer + 1, :])).then_inc(mod_in, 16)
                sp.dma_start(shift_b, rowcast(mod_rows[MOD_L * layer + m_shift:MOD_L * layer + m_shift + 1, :])).then_inc(mod_in, 16)
                load_x(1, 1)
                if gates:
                    with nc.allow_non_contiguous_dma(reason="eight gate columns"):
                        sp.dma_start(gw_raw[:, :, :], w_in[:, NCOL:NCOL + 8].rearrange("(k p) n -> p k n", p=P)).then_inc(gw_in, 16)
                        sp.dma_start(gbias[0:8, 0:1], b_gates[0, :].rearrange("(n a) -> n a", a=1)).then_inc(gw_in, 16)
                if conv:
                    with nc.allow_non_contiguous_dma(reason="a few KB of taps laid over the partitions"):
                        for j in range(3):
                            sp.dma_start(taps[:, :, j], cols(conv_w[0, j, :])).then_inc(taps_in, 16)
                        sp.dma_start(taps[:, :, 3], cols(conv_b[0, :])).then_inc(taps_in, 16)
                for s in range(RING):
                    load_w(chunk_col(0, s), s)

                def step(i, s):
                    if combine:
                        if live(i, s):
                            sp.wait_ge(x2_ready, upto(i, s))
                            if live(i, s, RING):
                                load_x(i * RING + (s + RING), s)
                            sp.dma_start(x_dst[bass.ds((i * RING + s) * P, P), :], xr[:, s, :]).then_inc(x_out[s], 16)
                    elif live(i, s, RING):
                        sp.wait_ge(um_ready, upto(i, s))
                        load_x(i * RING + (s + RING), s)

                skewed(sp, step, behind=0)

                def store(i, q):
                    if conv:
                        if q % 3 == 2:
                            j, s = q // 3, (q // 3) % RING
                            sp.wait_ge(y_ready, i * (2 * NBLK) + NBLK * (j + 2))
                            sp.dma_start(out_t[bass.ds(i * (2 * P) + j * P, P), :], stage[:, s, :]).then_inc(out_done[s], 16)
                    else:
                        sp.wait_ge(ev_act, i * (CH * NBLK) + NBLK * (q + 2))
                        sp.dma_start(out_t[bass.ds(i * (CH * P) + q * P, P), :], stage[:, q % RING, :]).then_inc(out_done[q % RING], 16)

                def body(i, more):
                    for q in range(CH):
                        if more or q + 2 < CH:
                            sp.wait_ge(w_lo_ready, i * CH + (q + 1))
                            load_w(chunk_col(i, q + 2), q % RING)
                        store(i, q)

                with sp.Fori(0, LOOPED) as i:
                    body(i, True)
                    if ada:
                        sp.wait_ge(row_ready, i + 2)
                        sp.dma_start(mod_rows[bass.ds(i + ADA_FIRST, 1), :], ada_row[0:1, :]).then_inc(row_out, 16)
                for i in range(LOOPED, BODIES):
                    body(i, i < BODIES - 1)
                if ada:
                    sp.wait_ge(row_out, 16 * (LOOPED + 1))
                if gates:
                    sp.wait_ge(gates_ev, NBLK)
                    sp.dma_start(gates_t[:, :], gate_rows[0:8, :]).then_inc(gates_out, 16)
                    sp.wait_ge(gates_out, 16)
                n_out = (KT if conv else NCHUNK) // RING
                for s in range(RING):
                    sp.wait_ge(out_done[s], 16 * (n_out + 1))

            @block.gpsimd
            def _(pool):
                pool.memset(mhalf[:, :], -0.5).then_inc(const_ready, 1)
                pool.wait_ge(const_ready, 1)

                def gather(n, s, count):
                    pool.tensor_copy(idx[:, s, :], pos[:, :, bass.ds(n, 1)].rearrange("p j a -> p (j a)")).then_inc(idx_ready, 1)
                    pool.wait_ge(idx_ready, count)
                    stand(pool, passed)
                    for j, dst in enumerate((row_a, row_b)):
                        pool.indirect_dma_start(dst[:, s, :], None, ys, bass.IndirectOffsetOnAxis(ap=idx[:, s, j:j + 1], axis=0)).then_inc(rows_in[s], 16)

                def step(i, s):
                    if combine and live(i, s, RING):
                        pool.wait_ge(x2_ready, upto(i, s))
                        gather(i * RING + (s + RING), s, upto(i, s, RING))
                    if live(i, s):
                        pool.wait_ge(ssq_ready, upto(i, s, 1))
                        stand(pool, passed)
                        pool.tensor_scalar(rstd[:, s:s + 1], ssq[:, s:s + 1], 1.0 / D, EPS, ALU.mult, ALU.add).then_inc(var_ready, 1)
                        pool.wait_ge(var_ready, upto(i, s))
                        pool.tensor_tensor(rstd[:, s:s + 1], rstd[:, s:s + 1], mhalf[:, 0:1], ALU.pow).then_inc(rstd_ready, 1)
                    if live(i, s, UM):
                        pool.wait_ge(um_ready, upto(i, s, UM))
                        pool.tensor_tensor(u[:, slot(s, UM), :], u[:, slot(s, UM), :], shift_b, ALU.add).then_inc(u_ready, 1)

                if combine:
                    gather(0, 0, 1)
                    gather(1, 1, 2)
                pool.wait_ge(mod_ready, 1)
                if blank is not None:
                    pool.memset(zero[:, :], 0.0).then_inc(zero_ready, 1)
                skewed(pool, step)
                if ada:
                    def load_group(layer, g, j):
                        pool.wait_ge(row_out, j * 16 + 16)
                        stand(pool, passed)
                        pool.dma_start(ada_row[0:1, :], b_ada[layer:layer + 1, bass.ds(g * D, D)]).then_inc(bias_in, 16)
                        for k in range(KT):
                            pool.wait_ge(mac, j * KT + (k + 1))
                            stand(pool, passed)
                            pool.dma_start(ada_w[k % RING], w_ada[layer, k * P:(k + 1) * P, bass.ds(g * D, D)]).then_inc(ada_in[k % RING], 16)

                    pool.wait_ge(um_ready, NT)
                    pool.wait_ge(u_ready, NT)
                    with pool.Fori(ADA_FIRST, MOD_L) as g:
                        load_group(0, g, g - ADA_FIRST)
                    with pool.Fori(0, MOD_L) as g:
                        load_group(1, g, g + (MOD_L - ADA_FIRST))
                if blank is not None:
                    pool.wait_ge(zero_ready, 1)
                    with pool.Fori(0, MAX_TILES) as a:
                        pool.dma_start(blank[bass.ds(a * P, P), :], zero[:, :]).then_inc(blank_out, 16)
                    pool.wait_ge(blank_out, 16 * MAX_TILES)

            @block.scalar
            def _(act):
                act.sem_inc(hi_done, RING)
                act.sem_inc(ev_act, NBLK)
                act.sem_inc(ssq_ready, 1)
                if ada:
                    act.sem_inc(row_out, 16)
                for s in range(RING):
                    act.sem_inc(out_done[s], 16)

                def split_w(blocks, loaded, s):
                    act.wait_ge(wr_in[s], loaded)
                    if blocks is not None:
                        act.wait_ge(blk_done, blocks)
                    act.activation(w_hi[:, s, :, :], w_raw[:, s, :, :], ACT.Copy).then_inc(w_hi_ready, 1)

                def step(i, s):
                    if live(i, s):
                        if combine:
                            act.wait_ge(x2_ready, upto(i, s))
                        else:
                            act.wait_ge(x_in[s], 16 * uses(i, s))
                        act.wait_ge(ssq_ready, upto(i, s))
                        act.activation(junk[:, :], xr[:, s, :], ACT.Square, accum_out=ssq[:, s:s + 1]).then_inc(ssq_ready, 1)
                    if live(i, s, HI):
                        act.wait_ge(tr_done, upto(i, s, HI))
                        act.activation(u_hi[:, :, bass.ds((i * RING + (s + HI)) * P, P)],
                                       psum_t[:, slot(s, HI), :].rearrange("p (k t) -> p k t", k=KT), ACT.Copy).then_inc(hi_done, 1)

                def first_weights():
                    for s in range(RING):
                        split_w(None, 16, s)
                    if gates:
                        act.wait_ge(gw_in, 32)
                        act.activation(gw_hi[:, :, :], gw_raw[:, :, :], ACT.Copy).then_inc(gw_ready, 1)

                skewed(act, step, between=first_weights)

                def body(i, q, more):
                    if conv:
                        if q % 3 == 0:
                            j = q // 3
                            for b in range(NBLK):
                                act.wait_ge(y_ready, i * (2 * NBLK) + NBLK * j + b + 1)
                                act.wait_ge(blk_done, i * (CH * NBLK) + NBLK * q + b + 1)
                                act.activation(c_rows[:, b * HALF:(b + 1) * HALF], psum_o[:, b, :], ACT.Copy).then_inc(ev_act, 1)
                    else:
                        act.wait_ge(out_done[q % RING], 16 * i + 16)
                        for b in range(NBLK):
                            act.wait_ge(blk_done, i * (CH * NBLK) + NBLK * q + b + 1)
                            act.activation(stage[:, q % RING, b * HALF:(b + 1) * HALF], psum_o[:, b, :], ACT.Copy).then_inc(ev_act, 1)
                    if more:
                        split_w(i * (CH * NBLK) + NBLK * (q + 1), i * (16 * CH // RING) + 16 * (q // RING + 2), q % RING)

                with act.Fori(0, LOOPED) as i:
                    for q in range(CH):
                        body(i, q, True)
                for i in range(LOOPED, BODIES):
                    for q in range(CH):
                        body(i, q, i < BODIES - 1 or q + 2 < CH)
                if gates:
                    for b in range(NBLK):
                        act.wait_ge(blk_done, NCHUNK * NBLK + b + 1)
                        act.activation(gate_rows[0:8, b * HALF:(b + 1) * HALF], psum_o[0:8, b, :], ACT.Identity, bias=gbias[0:8, 0:1]).then_inc(gates_ev, 1)

            @block.vector
            def _(dve):
                dve.sem_inc(lo_done, RING)
                dve.wait_ge(mod_in, 48)
                dve.scalar_tensor_tensor(out=scale_b, in0=scale_b, scalar=1.0, in1=ng_b,
                                         op0=ALU.add, op1=ALU.mult).then_inc(mod_ready, 1)
                dve.wait_ge(mod_ready, 1)
                if conv:
                    dve.sem_inc(y_ready, NBLK)

                def weights(i, s, n):
                    dve.tensor_copy(wts[:, slot(s, n), :], pair_w[:, :, bass.ds(i * RING + (s + n), 1)].rearrange("p j a -> p (j a)")).then_inc(wts_ready, 1)

                def split_w(n1, s):
                    dve.wait_ge(w_hi_ready, n1)
                    dve.tensor_tensor(w_lo[:, s, :, :], w_raw[:, s, :, :], w_hi[:, s, :, :].bitcast(F32), ALU.subtract).then_inc(w_lo_ready, 1)

                def low(i, s):
                    if live(i, s, LO):
                        dve.wait_ge(hi_done, upto(i, s, LO + RING))
                        dst = bass.ds((i * RING + (s + LO)) * P, P)
                        dve.tensor_tensor(u_lo[:, :, dst], psum_t[:, slot(s, LO), :].rearrange("p (k t) -> p k t", k=KT),
                                          u_hi[:, :, dst].bitcast(F32), ALU.subtract).then_inc(lo_done, 1)

                def step(i, s):
                    if combine and live(i, s):
                        dve.wait_ge(x_in[s], 16 * uses(i, s))
                        dve.wait_ge(rows_in[s], 32 * uses(i, s))
                        dve.wait_ge(wts_ready, upto(i, s))
                        dve.scalar_tensor_tensor(out=row_a[:, s, :], in0=row_a[:, s, :], scalar=wts[:, s, 0:1], in1=xin[:, s, :],
                                                 op0=ALU.mult, op1=ALU.add).then_inc(ra_added, 1)
                        if live(i, s, 1):
                            if live(i, s, -1):
                                dve.wait_ge(x2_ready, upto(i, s, -1))
                            weights(i, s, 1)
                        dve.wait_ge(ra_added, upto(i, s))
                        if live(i, s, -RING):
                            dve.wait_ge(x_out[s], 16 * uses(i, s, -RING))
                        dve.scalar_tensor_tensor(out=xr[:, s, :], in0=row_b[:, s, :], scalar=wts[:, s, 1:2], in1=row_a[:, s, :],
                                                 op0=ALU.mult, op1=ALU.add).then_inc(x2_ready, 1)
                    if combine:
                        low(i, s)
                    if live(i, s, UM):
                        n = slot(s, UM)
                        dve.wait_ge(rstd_ready, upto(i, s, UM))
                        if combine:
                            dve.wait_ge(x2_ready, upto(i, s, UM))
                        else:
                            dve.wait_ge(x_in[n], 16 * uses(i, s, UM))
                        dve.scalar_tensor_tensor(out=u[:, n, :], in0=xr[:, n, :], scalar=rstd[:, n:n + 1], in1=scale_b,
                                                 op0=ALU.mult, op1=ALU.mult).then_inc(um_ready, 1)
                    if not combine:
                        low(i, s)

                if combine:
                    weights(0, 0, 0)

                def first_weights():
                    for s in range(RING):
                        split_w(s + 1, s)
                    if gates:
                        dve.wait_ge(gw_ready, 1)
                        dve.tensor_tensor(gw_lo[:, :, :], gw_raw[:, :, :], gw_hi[:, :, :].bitcast(F32), ALU.subtract).then_inc(gw_ready, 1)

                skewed(dve, step, between=first_weights)
                if conv:
                    dve.wait_ge(taps_in, 64)
                    dve.memset(z_rows[:, 0:2], 0.0).then_inc(z_ready, 1)
                    for s in range(RING):
                        dve.wait_ge(x_out[s], 16 * (NT // RING))

                def body(i, q, more):
                    if conv:
                        j, kind = q // 3, q % 3
                        n0 = i * (2 * NBLK) + NBLK * j
                        if kind == 0:
                            dve.tensor_copy(tap[:, j, :], taps[:, bass.ds(i * 2 + j, 1), :].rearrange("p a j -> p (a j)")).then_inc(tap_ready, 1)
                        if kind == 1:
                            for b in range(NBLK):
                                cs, at = c_rows[:, b * HALF:(b + 1) * HALF], b * HALF
                                dve.wait_ge(ev_act, n0 + (NBLK + b + 1))
                                dve.wait_ge(blk_done, i * (CH * NBLK) + NBLK * q + b + 1)
                                dve.tensor_tensor(z_rows[:, 2 + at:2 + at + HALF], cs, psum_o[:, b, :], ALU.mult).then_inc(z_ready, 1)
                            for b in range(NBLK):
                                cs, at = c_rows[:, b * HALF:(b + 1) * HALF], b * HALF
                                if b == 0:
                                    dve.wait_ge(tap_ready, i * 2 + (j + 1))
                                    dve.wait_ge(z_ready, n0 + (NBLK + 1))
                                dve.tensor_scalar(cs, z_rows[:, 2 + at:2 + at + HALF], tap[:, j, 2:3], tap[:, j, 3:4],
                                                  ALU.mult, ALU.add).then_inc(zc_ready, 1)
                                for m, o in ((1, 1), (0, 0)):
                                    dve.wait_ge(zc_ready, i * (2 * NBLK * 3) + 3 * (NBLK * j + b) + 2 - m)
                                    dve.scalar_tensor_tensor(out=cs, in0=z_rows[:, o + at:o + at + HALF], scalar=tap[:, j, m:m + 1],
                                                             in1=cs, op0=ALU.mult, op1=ALU.add).then_inc(zc_ready, 1)
                        if kind == 2:
                            dve.wait_ge(out_done[j], 16 * i + 16)
                            dve.wait_ge(zc_ready, i * (2 * NBLK * 3) + 3 * NBLK * (j + 1))
                            for b in range(NBLK):
                                dve.wait_ge(blk_done, i * (CH * NBLK) + NBLK * q + b + 1)
                                dve.tensor_tensor(stage[:, j, b * HALF:(b + 1) * HALF], c_rows[:, b * HALF:(b + 1) * HALF], psum_o[:, b, :],
                                                  ALU.mult).then_inc(y_ready, 1)
                    if more:
                        split_w(i * CH + (q + 3), q % RING)

                def add_rows(j, k):
                    dve.wait_ge(ada_in[k % RING], j * (16 * KT // RING) + 16 * (k // RING + 1))
                    if k == 0:
                        dve.tensor_scalar(ada_acc, ada_w[0], cond[:, 0:1], None, ALU.mult).then_inc(mac, 1)
                    else:
                        dve.wait_ge(mac, j * KT + (k + 2))
                        dve.scalar_tensor_tensor(out=ada_acc, in0=ada_w[k % RING], scalar=cond[:, k:k + 1], in1=ada_acc,
                                                 op0=ALU.mult, op1=ALU.add).then_inc(mac, 1)

                if ada:
                    dve.sem_inc(mac, RING)
                    dve.sem_inc(row_ready, 1)
                with dve.Fori(0, LOOPED) as i:
                    for q in range(CH):
                        if ada:
                            for k in range(q * KT // CH, (q + 1) * KT // CH):
                                add_rows(i, k)
                        body(i, q, True)
                    if ada:
                        dve.wait_ge(sum_ready, i + 1)
                        dve.wait_ge(bias_in, i * 16 + 16)
                        dve.tensor_tensor(ada_row[0:1, :], psum_t[0:1, 0, :], ada_row[0:1, :], ALU.add).then_inc(row_ready, 1)
                for i in range(LOOPED, BODIES):
                    for q in range(CH):
                        body(i, q, i < BODIES - 1 or q + 2 < CH)

            @block.tensor
            def _(pe):
                def transpose_u(i):
                    for s in range(RING):
                        n1 = i * RING + (s + 1)
                        pe.wait_ge(u_ready, n1)
                        pe.wait_ge(hi_done, n1)
                        pe.wait_ge(lo_done, n1)
                        for k in range(KT):
                            last = pe.transpose(psum_t[:, s, k * P:(k + 1) * P], u[:, s, k * P:(k + 1) * P], ident[:, :])
                        last.then_inc(tr_done, 1)

                def block_of(b, rows, wh, wl):
                    ts = slice(b * HALF, (b + 1) * HALF)
                    for k in range(KT):
                        last = split_mm(pe, psum_o[0:rows, b, :], (wh[:, k, :], wl[:, k, :]),
                                        (u_hi[:, k, ts], u_lo[:, k, ts]), k == 0, k == KT - 1)
                    last.then_inc(blk_done, 1)
                    return last

                def body(i, q, first=0):
                    pe.wait_ge(w_lo_ready, i * CH + (q + 1))
                    for b in range(first, NBLK):
                        if conv:
                            n0 = i * (2 * NBLK) + NBLK * (q // 3) + b + 1
                            if q % 3 == 0:
                                pe.wait_ge(y_ready, n0)
                            elif q % 3 == 1:
                                pe.wait_ge(ev_act, n0 + NBLK)
                            else:
                                pe.wait_ge(z_ready, n0 + 1)
                        else:
                            pe.wait_ge(ev_act, i * (CH * NBLK) + NBLK * q + b + 1)
                        block_of(b, P, w_hi[:, q % RING], w_lo[:, q % RING])

                def modulation(i):
                    if ada:
                        pe.wait_ge(mac, i * KT + (KT + RING))
                        pe.wait_ge(row_ready, i + 1)
                        for h in range(2):
                            hs = slice(h * HALF, (h + 1) * HALF)
                            last = pe.matmul(psum_t[0:1, 0, hs], ones[:, 0:1], ada_acc[:, hs], start=True, stop=True)
                        last.then_inc(sum_ready, 1)

                pairs = NT // RING // NBLK
                for b in range(NBLK - 1):
                    with pe.Fori((b + 1) * pairs if b else 0, (b + 2) * pairs) as i:
                        transpose_u(i)
                    pe.wait_ge(hi_done, (b + 1) * RING * pairs + RING)
                    pe.wait_ge(lo_done, (b + 1) * RING * pairs + RING)
                    if b == 0:
                        pe.wait_ge(w_lo_ready, 1)
                    block_of(b, P, w_hi[:, 0], w_lo[:, 0])
                pe.wait_ge(hi_done, NT + RING)
                pe.wait_ge(lo_done, NT + RING)
                body(0, 0, NBLK - 1)
                for q in range(1, CH):
                    body(0, q)
                modulation(0)
                with pe.Fori(1, LOOPED) as i:
                    for q in range(CH):
                        body(i, q)
                    modulation(i)
                with pe.Fori(LOOPED, BODIES) as i:
                    for q in range(CH):
                        body(i, q)
                if gates:
                    pe.wait_ge(gw_ready, 2)
                    for b in range(NBLK):
                        pe.wait_ge(ev_act, NCHUNK * NBLK + b + 1)
                        block_of(b, 8, gw_hi, gw_lo)


def mlstm(nc, proj_t, gates_t, gate_d, norm_g, h_t, ident):
    HC = HEADS * NT
    V1 = DV + 1
    SCALE = float(DQK) ** -0.5
    with Phase(nc, "rec") as ph:
        gi = ph.sb("gi", [HC, P])
        gf = ph.sb("gf", [HC, P])
        tmp = ph.sb("tmp", [HC, P])
        lf = ph.sb("lf", [HC, P])
        b = ph.sb("b", [HC, P])
        g = ph.sb("g", [HC, P])
        zeros = ph.sb("zeros", [HC, P])
        ones = ph.sb("ones", [HC, P])
        m_run = ph.sb("m_run", [HC, P])
        ends = ph.sb("ends", [HC, 2])
        m_start = ph.sb("m_start", [HC, 1])
        neg_last = ph.sb("neg_last", [HC, 1])
        neg_m = ph.sb("neg_m", [HC, 2, P])
        wk = ph.sb("wk", [HC, P])
        enm = ph.sb("enm", [HC, P])
        chain = ph.sb("chain", [HEADS, NT, 2])
        m_seq = ph.sb("m_seq", [HEADS, NT + 1])
        tok = ph.sb("tok", [P, 3, HC])
        decay = ph.sb("decay", [P, HC])
        causal = ph.sb("causal", [P, P])
        causal4 = ph.sb("causal4", [P, HEADS, P])
        ng = ph.sb("ng", [P, KT])
        mhalf = ph.sb("mhalf", [P, HEADS])
        pt = ph.sb("pt", [P, RING, 3 * KT, P])
        bc = ph.sb("bc", [P, RING, HEADS, 2, P])
        kw = ph.sb("kw", [P, RING, HEADS, DQK])
        val = ph.sb("val", [P, RING, HEADS, V1])
        qw = ph.sb("qw", [P, RING, HEADS, P])
        arg = ph.sb("arg", [P, HEADS, P])
        sd = ph.sb("sd", [P, RING, HEADS, P])
        cst = ph.sb("cst", [P, HEADS, V1])
        sgate = ph.sb("sgate", [P, RING, KT, P])
        numer = ph.sb("numer", [P, RING, HEADS, V1])
        junk = ph.sb("junk", [P, DV])
        den = ph.sb("den", [P, HEADS])
        ssq = ph.sb("ssq", [P, RING, HEADS])
        fac = ph.sb("fac", [P, HEADS])
        hout = ph.sb("hout", [P, RING, KT, P])
        tokc = ph.sb("tokc", [P, RING, 3, HEADS])
        decc = ph.sb("decc", [P, RING, HEADS])
        ps_k = ph.ps("ps_k", [P, HEADS, P])
        ps_v = ph.ps("ps_v", [P, KT, P])
        ps_s = ph.ps("ps_s", [P, HEADS, P])
        ps_n = ph.ps("ps_n", [P, RING, HALF])
        ps_c = ph.ps("ps_c", [P, RING, HALF])
        g_in = ph.sem("g_in")
        pre = ph.sem("pre")
        pre_act = ph.sem("pre_act")
        ends_out = ph.sem("ends_out")
        chain_in = ph.sem("chain_in")
        seq_out = ph.sem("seq_out")
        start_in = ph.sem("start_in")
        rows_out = ph.sem("rows_out")
        decay_in = ph.sem("decay_in")
        tok_tr = ph.sem("tok_tr")
        passed = ph.sem("passed")
        tok_ready = ph.sem("tok_ready")
        consts = ph.sem("consts")
        ng_in = ph.sem("ng_in")
        pt_in = [ph.sem(f"pt_in{s}") for s in range(RING)]
        bc_in = [ph.sem(f"bc_in{s}") for s in range(RING)]
        k_tr = ph.sem("k_tr")
        v_tr = ph.sem("v_tr")
        tanh_ready = ph.sem("tanh_ready")
        s_done = ph.sem("s_done")
        kw_ready = ph.sem("kw_ready")
        val_ready = ph.sem("val_ready")
        qw_ready = ph.sem("qw_ready")
        cols_ready = ph.sem("cols_ready")
        arg_ready = ph.sem("arg_ready")
        masked = ph.sem("masked")
        exp_ready = ph.sem("exp_ready")
        sd_ready = ph.sem("sd_ready")
        num_done = ph.sem("num_done")
        cup_done = ph.sem("cup_done")
        c_ready = ph.sem("c_ready")
        num_ev = ph.sem("num_ev")
        den_ready = ph.sem("den_ready")
        norm_step = ph.sem("norm_step")
        fsq = ph.sem("fsq")
        fss = ph.sem("fss")
        fac_ready = ph.sem("fac_ready")
        hn_ready = ph.sem("hn_ready")
        h_tr = ph.sem("h_tr")
        h_ready = ph.sem("h_ready")
        sig_ready = ph.sem("sig_ready")
        gate_ready = ph.sem("gate_ready")
        h_out = [ph.sem(f"h_out{s}") for s in range(RING)]
        ends_d, seq_d, rows_d, decay_d = gate_d
        NPRE = 3

        with ph.block() as block:
            @block.sync
            def _(sp):
                src = lambda r: gates_t[r:r + HEADS, :].rearrange("h (c t) -> (h c) t", t=P)
                sp.dma_start(gi[:, :], src(0)).then_inc(g_in, 16)
                sp.dma_start(gf[:, :], src(HEADS)).then_inc(g_in, 16)
                with nc.allow_non_contiguous_dma(reason="4 KB vector laid over the partitions"):
                    sp.dma_start(ng[:, :], cols(norm_g[0, :])).then_inc(ng_in, 16)

                def load(c, s):
                    sp.dma_start(pt[:, s, :, :], proj_t[:, bass.ds(c * P, P)].rearrange("(r p) t -> p r t", p=P)).then_inc(pt_in[s], 16)

                def load_bc(c, s):
                    src = rows_d.rearrange("(h c) a -> c h a", h=HEADS)[bass.ds(c, 1), :, :].to_broadcast([P, HEADS, 2 * P])
                    sp.dma_start(bc[:, s, :, :, :].rearrange("p h a t -> p h (a t)"), src).then_inc(bc_in[s], 16)

                sp.wait_ge(pre, 8)
                sp.dma_start(ends_d[:, :], ends[:, :]).then_inc(ends_out, 16)
                sp.wait_ge(ends_out, 16)
                sp.dma_start(chain[:, :, :], ends_d.rearrange("(h c) a -> h c a", h=HEADS)).then_inc(chain_in, 16)
                sp.wait_ge(pre, 10)
                sp.dma_start(seq_d.rearrange("(h c) a -> h (c a)", h=HEADS), m_seq[:, 0:NT]).then_inc(seq_out, 16)
                sp.wait_ge(seq_out, 16)
                sp.dma_start(m_start[:, :], seq_d).then_inc(start_in, 16)
                load(0, 0)
                sp.wait_ge(pre, 14)
                sp.wait_ge(pre_act, 3)
                sp.dma_start(rows_d, neg_m[:, :, :].rearrange("p a t -> p (a t)")).then_inc(rows_out, 16)
                sp.dma_start(decay_d, neg_m[:, 1, P - 1:P]).then_inc(rows_out, 16)
                sp.wait_ge(rows_out, 32)
                sp.dma_start(decay[:, :], decay_d.rearrange("c a -> a c").to_broadcast([P, HC])).then_inc(decay_in, 16)
                load_bc(0, 0)
                load_bc(1, 1)
                load(1, 1)

                def step(i, s):
                    if live(i, s, RING):
                        sp.wait_ge(tanh_ready, upto(i, s))
                        sp.wait_ge(sd_ready, upto(i, s))
                        sp.wait_ge(kw_ready, upto(i, s))
                        sp.wait_ge(v_tr, upto(i, s))
                        load_bc(i * RING + (s + RING), s)
                        load(i * RING + (s + RING), s)
                    if live(i, s, -1):
                        q = slot(s, -1)
                        sp.wait_ge(h_ready, upto(i, s, -1 + RING))
                        sp.dma_start(h_t[:, bass.ds((i * RING + (s - 1)) * P, P)].rearrange("(k p) t -> p k t", p=P), hout[:, q, :, :]).then_inc(h_out[q], 16)

                skewed(sp, step, head=1, behind=1)
                for s in range(RING):
                    sp.wait_ge(h_out[s], 16 * (NT // RING + 1))

            @block.gpsimd
            def _(pool):
                pool.memset(zeros[:, :], 0.0).then_inc(consts, 1)
                pool.memset(ones[:, :], 1.0).then_inc(consts, 1)
                pool.memset(mhalf[:, :], -0.5).then_inc(consts, 1)
                pool.memset(causal4[:, :, :], 0.0).then_inc(consts, 1)
                pool.memset(val[:, :, :, DV:V1], 1.0).then_inc(consts, 1)
                pool.memset(cst[:, :, :], 0.0).then_inc(consts, 1)
                pool.wait_ge(consts, 6)
                pool.affine_select(out=causal4[:, :, :], in_=causal4[:, :, :], compare_op=ALU.is_ge, fill=-BIG, base=0,
                                   pattern=[[0, HEADS], [1, P]], channel_multiplier=-1).then_inc(consts, 1)
                pool.wait_ge(consts, 7)
                pool.wait_ge(ng_in, 16)

                def step(i, s):
                    if live(i, s, 1):
                        pool.wait_ge(arg_ready, upto(i, s, 1))
                        pool.tensor_tensor(arg[:, :, :], arg[:, :, :], causal4[:, :, :], ALU.add).then_inc(masked, 1)
                    if live(i, s):
                        pool.wait_ge(sig_ready, upto(i, s))
                        pool.tensor_tensor(sgate[:, s, :, :], sgate[:, s, :, :], ng[:, :].unsqueeze(2).to_broadcast([P, KT, P]), ALU.mult).then_inc(gate_ready, 1)
                        pool.wait_ge(norm_step, i * (RING * 3) + (3 * s + 2))
                        pool.tensor_tensor(fac[:, :], fac[:, :], mhalf[:, :], ALU.pow).then_inc(fac_ready, 1)

                pool.wait_ge(arg_ready, 1)
                pool.tensor_tensor(arg[:, :, :], arg[:, :, :], causal4[:, :, :], ALU.add).then_inc(masked, 1)
                skewed(pool, step, head=1, behind=0)

            @block.scalar
            def _(act):
                for s in range(RING):
                    act.sem_inc(h_out[s], 16)
                act.sem_inc(num_ev, 2 * RING)
                act.wait_ge(pre, 1)
                act.activation(tmp[:, :], tmp[:, :], ACT.Exp, scale=-1.0).then_inc(pre_act, 1)
                act.wait_ge(pre, 2)
                act.activation(tmp[:, :], tmp[:, :], ACT.Ln).then_inc(pre_act, 1)
                act.wait_ge(pre, 14)
                act.activation(neg_m[:, 1, :], neg_m[:, 0, :], ACT.Exp, bias=m_start[:, 0:1]).then_inc(pre_act, 1)
                act.activation(wk[:, :], g[:, :], ACT.Exp, bias=neg_last[:, 0:1]).then_inc(pre_act, 1)
                act.activation(enm[:, :], tmp[:, :], ACT.Exp, scale=-1.0).then_inc(pre_act, 1)

                def gate(i, s):
                    act.wait_ge(pt_in[s], 16 * uses(i, s))
                    act.wait_ge(h_ready, upto(i, s))
                    act.activation(sgate[:, s, :, :], pt[:, s, 2 * KT:3 * KT, :], ACT.Tanh, scale=0.5).then_inc(tanh_ready, 1)

                def prepare(i, s, n):
                    q = slot(s, n)
                    act.wait_ge(v_tr, upto(i, s, n))
                    act.activation(val[:, q, :, 0:DV], ps_v[:, :, :].rearrange("p (h a) d -> p h (a d)", h=HEADS), ACT.Copy).then_inc(val_ready, 1)
                    act.wait_ge(masked, upto(i, s, n))
                    act.activation(arg[:, :, :], arg[:, :, :], ACT.Exp).then_inc(exp_ready, 1)

                def evacuate(i, s):
                    act.wait_ge(h_tr, upto(i, s))
                    for h in range(HEADS):
                        act.wait_ge(num_done, (i * RING + s) * HEADS + (h + 1))
                        act.wait_ge(num_ev, (i * RING + s) * (2 * HEADS) + (2 * h + 3))
                        act.activation(junk[:, :], ps_n[:, h % RING, 0:DV], ACT.Square, accum_out=ssq[:, s, h:h + 1]).then_inc(num_ev, 1)
                        act.activation(numer[:, s, h, :], ps_n[:, h % RING, 0:V1], ACT.Copy).then_inc(num_ev, 1)
                    act.wait_ge(cup_done, upto(i, s) * HEADS)
                    stand(act, passed)

                def step(i, s):
                    if live(i, s):
                        gate(i, s)
                    if live(i, s, 1):
                        prepare(i, s, 1)
                    if live(i, s):
                        evacuate(i, s)

                act.wait_ge(consts, 7)
                prepare(0, 0, 0)
                skewed(act, step, head=1, behind=0)

            @block.vector
            def _(dve):
                dve.wait_ge(g_in, 32)
                dve.wait_ge(consts, 7)
                dve.scalar_tensor_tensor(out=tmp[:, :], in0=gf[:, :], scalar=-1.0, in1=gf[:, :], op0=ALU.mult, op1=ALU.max).then_inc(pre, 1)
                dve.wait_ge(pre_act, 1)
                dve.tensor_scalar(tmp[:, :], tmp[:, :], 1.0, None, ALU.add).then_inc(pre, 1)
                dve.wait_ge(pre_act, 2)
                dve.scalar_tensor_tensor(out=lf[:, :], in0=gf[:, :], scalar=0.0, in1=tmp[:, :], op0=ALU.min, op1=ALU.subtract).then_inc(pre, 1)
                dve.wait_ge(pre, 3)
                dve.tensor_tensor_scan(b[:, :], ones[:, :], lf[:, :], 0.0, ALU.mult, ALU.add).then_inc(pre, 1)
                dve.wait_ge(pre, 4)
                dve.tensor_tensor(g[:, :], gi[:, :], b[:, :], ALU.subtract).then_inc(pre, 1)
                dve.tensor_copy(ends[:, 1:2], b[:, P - 1:P]).then_inc(pre, 1)
                dve.wait_ge(pre, 5)
                dve.tensor_tensor_scan(m_run[:, :], zeros[:, :], g[:, :], -BIG, ALU.add, ALU.max).then_inc(pre, 1)
                dve.wait_ge(pre, 7)
                dve.tensor_copy(ends[:, 0:1], m_run[:, P - 1:P]).then_inc(pre, 1)
                dve.memset(m_seq[:, 0:1], 0.0).then_inc(pre, 1)
                dve.wait_ge(chain_in, 16)
                dve.tensor_tensor_scan(m_seq[:, 1:NT + 1], chain[:, :, 0], chain[:, :, 1], 0.0, ALU.max, ALU.add).then_inc(pre, 1)
                dve.wait_ge(start_in, 16)
                dve.tensor_scalar(m_run[:, :], m_run[:, :], m_start[:, 0:1], None, ALU.max).then_inc(pre, 1)
                dve.wait_ge(pre, 11)
                dve.tensor_scalar(neg_m[:, 0, :], m_run[:, :], -1.0, None, ALU.mult).then_inc(pre, 1)
                dve.tensor_scalar(neg_last[:, :], m_run[:, P - 1:P], -1.0, None, ALU.mult).then_inc(pre, 1)
                dve.tensor_tensor(tmp[:, :], b[:, :], m_run[:, :], ALU.add).then_inc(pre, 1)
                dve.wait_ge(tok_tr, 1)
                dve.tensor_copy(tok[:, :, :], ps_s[:, 0:NPRE, 0:HC]).then_inc(tok_ready, 1)
                dve.wait_ge(tok_ready, 1)
                dve.wait_ge(decay_in, 16)
                dve.sem_inc(c_ready, HEADS)
                dve.sem_inc(h_ready, RING)

                def prepare(i, s, n):
                    q, c1 = slot(s, n), upto(i, s, n)
                    dve.tensor_copy(tokc[:, q, :, :], tok[:, :, :].rearrange("p a (h c) -> p a h c", h=HEADS)[:, :, :, bass.ds(i * RING + (s + n), 1)]
                                    .rearrange("p a h c -> p a (h c)")).then_inc(cols_ready, 1)
                    dve.tensor_copy(decc[:, q, :], decay[:, :].rearrange("p (h c) -> p h c", h=HEADS)[:, :, bass.ds(i * RING + (s + n), 1)]
                                    .rearrange("p h c -> p (h c)")).then_inc(cols_ready, 1)
                    dve.wait_ge(cols_ready, c1 * 2)
                    dve.wait_ge(bc_in[q], 16 * uses(i, s, n))
                    dve.tensor_tensor(arg[:, :, :], bc[:, q, :, 0, :], tokc[:, q, 0, :].unsqueeze(2).to_broadcast([P, HEADS, P]), ALU.add).then_inc(arg_ready, 1)
                    dve.wait_ge(pt_in[q], 16 * uses(i, s, n))
                    dve.scalar_tensor_tensor(out=qw[:, q, :, :], in0=pt[:, q, 0:HEADS, :], scalar=SCALE, in1=bc[:, q, :, 1, :],
                                             op0=ALU.mult, op1=ALU.mult).then_inc(qw_ready, 1)
                    dve.wait_ge(k_tr, c1)
                    dve.tensor_tensor(kw[:, q, :, :], ps_k[:, :, :], tokc[:, q, 1, :].unsqueeze(2).to_broadcast([P, HEADS, P]), ALU.mult).then_inc(kw_ready, 1)
                    dve.wait_ge(exp_ready, c1)
                    dve.wait_ge(s_done, c1)
                    dve.scalar_tensor_tensor(out=sd[:, q, :, :], in0=ps_s[:, :, :], scalar=SCALE, in1=arg[:, :, :], op0=ALU.mult, op1=ALU.mult).then_inc(sd_ready, 1)

                def update(i, s):
                    dve.wait_ge(tanh_ready, upto(i, s))
                    dve.tensor_scalar(sgate[:, s, :, :], sgate[:, s, :, :], 0.5, 0.5, ALU.mult, ALU.add).then_inc(sig_ready, 1)
                    for h in range(HEADS):
                        dve.wait_ge(cup_done, (i * RING + s) * HEADS + (h + 1))
                        dve.scalar_tensor_tensor(out=cst[:, h, :], in0=cst[:, h, :], scalar=decc[:, s, h:h + 1], in1=ps_c[:, h % RING, 0:V1],
                                                 op0=ALU.mult, op1=ALU.add).then_inc(c_ready, 1)

                def denominators(i, s):
                    c1, n3 = upto(i, s), (i * RING + s) * 3
                    dve.wait_ge(num_ev, c1 * (2 * HEADS) + 2 * RING)
                    dens = numer[:, s, :, DV:V1].rearrange("p h a -> p (h a)")
                    dve.scalar_tensor_tensor(out=den[:, :], in0=dens, scalar=-1.0, in1=tokc[:, s, 2, :], op0=ALU.mult, op1=ALU.max).then_inc(den_ready, 1)
                    dve.wait_ge(den_ready, (i * RING + s) * 2 + 1)
                    dve.tensor_tensor(den[:, :], den[:, :], dens, ALU.max).then_inc(den_ready, 1)
                    dve.wait_ge(den_ready, c1 * 2)
                    dve.reciprocal(den[:, :], den[:, :]).then_inc(norm_step, 1)
                    dve.wait_ge(norm_step, n3 + 1)
                    dve.tensor_tensor(fac[:, :], den[:, :], den[:, :], ALU.mult).then_inc(fsq, 1)
                    dve.wait_ge(fsq, c1)
                    dve.tensor_tensor(fac[:, :], fac[:, :], ssq[:, s, :], ALU.mult).then_inc(fss, 1)
                    dve.wait_ge(fss, c1)
                    dve.tensor_scalar(fac[:, :], fac[:, :], 1.0 / DV, EPS, ALU.mult, ALU.add).then_inc(norm_step, 1)

                def gated_output(i, s, n):
                    q = slot(s, n)
                    dve.wait_ge(h_tr, upto(i, s, n + RING))
                    dve.wait_ge(gate_ready, upto(i, s, n))
                    dve.wait_ge(h_out[q], 16 * uses(i, s, n))
                    dve.tensor_tensor(hout[:, q, :, :], ps_v[:, :, :], sgate[:, q, :, :], ALU.mult).then_inc(h_ready, 1)

                def normalise(i, s):
                    dve.wait_ge(fac_ready, upto(i, s))
                    dve.tensor_tensor(fac[:, :], fac[:, :], den[:, :], ALU.mult).then_inc(norm_step, 1)
                    dve.wait_ge(norm_step, upto(i, s) * 3)
                    dve.tensor_tensor(numer[:, s, :, 0:DV], numer[:, s, :, 0:DV], fac[:, :].unsqueeze(2).to_broadcast([P, HEADS, DV]), ALU.mult).then_inc(hn_ready, 1)

                def step(i, s):
                    if live(i, s, 1):
                        prepare(i, s, 1)
                    if live(i, s):
                        update(i, s)
                        denominators(i, s)
                    if live(i, s, -1):
                        gated_output(i, s, -1)
                    if live(i, s):
                        normalise(i, s)

                prepare(0, 0, 0)
                skewed(dve, step, head=1, behind=1)

            @block.tensor
            def _(pe):
                pe.sem_inc(h_tr, RING)
                pe.wait_ge(pre, 14)
                pe.wait_ge(pre_act, 5)
                for a, src in enumerate((g, wk, enm)):
                    last = pe.transpose(ps_s[:, a, 0:HC], src[:, :], ident[0:HC, 0:HC])
                last.then_inc(tok_tr, 1)

                def prepare(i, s, n, first=False):
                    q = slot(s, n)
                    pe.wait_ge(pt_in[q], 16 * uses(i, s, n))
                    if not first:
                        pe.wait_ge(kw_ready, upto(i, s, n - 1))
                        pe.wait_ge(sd_ready, upto(i, s, n - 1))
                    for h in range(HEADS):
                        last = pe.transpose(ps_k[:, h, :], pt[:, q, HEADS + h, :], ident[:, :])
                    last.then_inc(k_tr, 1)
                    for h in range(HEADS):
                        last = pe.matmul(ps_s[:, h, :], pt[:, q, HEADS + h, :], pt[:, q, h, :], start=True, stop=True)
                    last.then_inc(s_done, 1)
                    if not first:
                        pe.wait_ge(h_ready, upto(i, s, n - 1))
                        pe.wait_ge(val_ready, upto(i, s, n - 1))
                    for r in range(KT):
                        last = pe.transpose(ps_v[:, r, :], pt[:, q, KT + r, :], ident[:, :])
                    last.then_inc(v_tr, 1)

                def products(i, s):
                    n, n4 = upto(i, s), (i * RING + s) * HEADS
                    pe.wait_ge(qw_ready, n)
                    pe.wait_ge(kw_ready, n)
                    pe.wait_ge(val_ready, n)
                    pe.wait_ge(sd_ready, n)
                    for h in range(HEADS):
                        pe.wait_ge(c_ready, n4 + (h + 1))
                        pe.wait_ge(num_ev, n4 * 2 + (2 * h + 2))
                        pe.matmul(ps_n[:, h % RING, 0:V1], qw[:, s, h, :], cst[:, h, :], start=True, stop=False)
                        pe.matmul(ps_n[:, h % RING, 0:V1], sd[:, s, h, :], val[:, s, h, :], start=False, stop=True).then_inc(num_done, 1)
                        pe.wait_ge(c_ready, n4 + (h + 1 + RING))
                        pe.matmul(ps_c[:, h % RING, 0:V1], kw[:, s, h, :], val[:, s, h, :], start=True, stop=True).then_inc(cup_done, 1)

                def transpose_out(i, s, n):
                    pe.wait_ge(hn_ready, upto(i, s, n))
                    pe.wait_ge(val_ready, upto(i, s, 1) if live(i, s, 1) else NT)
                    for r in range(KT):
                        last = pe.transpose(ps_v[:, r, :], numer[:, slot(s, n), r // 2, (r % 2) * P:(r % 2 + 1) * P], ident[:, :])
                    last.then_inc(h_tr, 1)

                def step(i, s):
                    if live(i, s, 1):
                        prepare(i, s, 1)
                    if live(i, s):
                        products(i, s)
                    if live(i, s, -1):
                        if not live(i, s, 1):
                            pe.wait_ge(h_ready, upto(i, s, 0))
                        transpose_out(i, s, -1)

                pe.wait_ge(tok_ready, 1)
                prepare(0, 0, 0, True)
                skewed(pe, step, head=1, behind=1)


def out_proj(nc, layer, h_t, w_out, x_src, x_dst, u_dst, norm_g, mod_rows, w_router, logits, ident):
    WS = 4
    with Phase(nc, f"out{layer}") as ph:
        w_raw = ph.sb("w_raw", [P, WS, D])
        w_hi = ph.sb("w_hi", [P, KT, D], F32R)
        w_lo = ph.sb("w_lo", [P, KT, D], F32R)
        wr_raw = ph.sb("wr_raw", [P, KT, E])
        wr_hi = ph.sb("wr_hi", [P, KT, E], F32R)
        wr_lo = ph.sb("wr_lo", [P, KT, E], F32R)
        h_raw = ph.sb("h_raw", [P, RING, KT, P])
        h_hi = ph.sb("h_hi", [P, RING, KT, P], F32R)
        h_lo = ph.sb("h_lo", [P, RING, KT, P], F32R)
        xin = ph.sb("xin", [P, RING, D])
        xo = ph.sb("xo", [P, RING, D])
        u = ph.sb("u", [P, RING, D])
        u_hi = ph.sb("u_hi", [P, KT, P], F32R)
        u_lo = ph.sb("u_lo", [P, KT, P], F32R)
        gate_b = ph.sb("gate_b", [P, D])
        scale_b = ph.sb("scale_b", [P, D])
        shift_b = ph.sb("shift_b", [P, D])
        ng_b = ph.sb("ng_b", [P, D])
        ssq = ph.sb("ssq", [P, RING])
        rstd = ph.sb("rstd", [P, RING])
        mhalf = ph.sb("mhalf", [P, 1])
        psum_o = ph.ps("psum_o", [P, RING, D])
        psum_t = ph.ps("psum_t", [P, D])
        psum_r = ph.ps("psum_r", [P, RING, E])
        mod_in = ph.sem("mod_in")
        mod_ready = ph.sem("mod_ready")
        w_in = [ph.sem(f"w_in{s}") for s in range(WS)]
        wr_in = ph.sem("wr_in")
        w_hi_ready = ph.sem("w_hi_ready")
        w_lo_ready = ph.sem("w_lo_ready")
        h_in = [ph.sem(f"h_in{s}") for s in range(RING)]
        h_hi_ready = ph.sem("h_hi_ready")
        h_lo_ready = ph.sem("h_lo_ready")
        x_in = [ph.sem(f"x_in{s}") for s in range(RING)]
        mm_done = ph.sem("mm_done")
        gated = ph.sem("gated")
        xo_ready = ph.sem("xo_ready")
        x_out = [ph.sem(f"x_out{s}") for s in range(RING)]
        ssq_ready = ph.sem("ssq_ready")
        var_ready = ph.sem("var_ready")
        rstd_ready = ph.sem("rstd_ready")
        passed = ph.sem("passed")
        um_ready = ph.sem("um_ready")
        u_ready = ph.sem("u_ready")
        u_out = [ph.sem(f"u_out{s}") for s in range(RING)]
        tr_done = ph.sem("tr_done")
        u_hi_ready = ph.sem("u_hi_ready")
        u_lo_ready = ph.sem("u_lo_ready")
        r_done = ph.sem("r_done")
        logits_ready = ph.sem("logits_ready")
        const_ready = ph.sem("const_ready")
        LAST = NT // RING - 1
        upto = lambda i, s, n=0: i * RING + (s + n + 1)

        with ph.block() as block:
            @block.sync
            def _(sp):
                def load_h(n, s):
                    sp.dma_start(h_raw[:, s, :, :], h_t[:, bass.ds(n * P, P)].rearrange("(k p) t -> p k t", p=P)).then_inc(h_in[s], 16)

                def load_x(n, s):
                    sp.dma_start(xin[:, s, :], x_src[bass.ds(n * P, P), :]).then_inc(x_in[s], 16)

                load_h(0, 0)
                for k in range(KT):
                    if k >= WS:
                        sp.wait_ge(w_lo_ready, k - WS + 1)
                    sp.dma_start(w_raw[:, k % WS, :], w_out[k * P:(k + 1) * P, :]).then_inc(w_in[k % WS], 16)
                    if k == 0:
                        load_h(1, 1)
                load_x(0, 0)
                for g, dst in ((2, gate_b), (3, shift_b), (4, scale_b)):
                    sp.dma_start(dst[:, :], rowcast(mod_rows[MOD_L * layer + g:MOD_L * layer + g + 1, :])).then_inc(mod_in, 16)
                sp.dma_start(ng_b[:, :], rowcast(norm_g[layer:layer + 1, :])).then_inc(mod_in, 16)
                load_x(1, 1)
                with nc.allow_non_contiguous_dma(reason="64 KB router"):
                    sp.dma_start(wr_raw[:, :, :], w_router.rearrange("(k p) e -> p k e", p=P)).then_inc(wr_in, 16)
                for s in range(RING):
                    sp.wait_ge(h_lo_ready, s + 1)
                    load_h(RING + s, s)

                def step(i, s, more_x, more_h):
                    n = upto(i, s)
                    sp.wait_ge(xo_ready, n)
                    if more_x:
                        load_x(i * RING + (RING + s), s)
                    sp.dma_start(x_dst[bass.ds(i * (RING * P) + s * P, P), :], xo[:, s, :]).then_inc(x_out[s], 16)
                    if more_h:
                        sp.wait_ge(h_lo_ready, upto(i, s, RING))
                        load_h(i * RING + (2 * RING + s), s)
                    sp.wait_ge(u_ready, n)
                    sp.dma_start(u_dst[bass.ds(i * (RING * P) + s * P, P), :], u[:, s, :]).then_inc(u_out[s], 16)

                with sp.Fori(0, LAST - 1) as i:
                    for s in range(RING):
                        step(i, s, True, True)
                for i in (LAST - 1, LAST):
                    for s in range(RING):
                        step(i, s, i < LAST, False)
                for s in range(RING):
                    sp.wait_ge(x_out[s], 16 * (LAST + 2))
                    sp.wait_ge(u_out[s], 16 * (LAST + 2))

            @block.gpsimd
            def _(pool):
                pool.memset(mhalf[:, :], -0.5).then_inc(const_ready, 1)
                pool.wait_ge(const_ready, 1)
                pool.wait_ge(mod_ready, 1)
                with pool.Fori(0, NT // RING) as i:
                    for s in range(RING):
                        n = upto(i, s)
                        pool.wait_ge(ssq_ready, n)
                        stand(pool, passed)
                        pool.tensor_scalar(rstd[:, s:s + 1], ssq[:, s:s + 1], 1.0 / D, EPS, ALU.mult, ALU.add).then_inc(var_ready, 1)
                        pool.wait_ge(var_ready, n)
                        pool.tensor_tensor(rstd[:, s:s + 1], rstd[:, s:s + 1], mhalf[:, 0:1], ALU.pow).then_inc(rstd_ready, 1)
                        pool.wait_ge(um_ready, n)
                        pool.tensor_tensor(u[:, s, :], u[:, s, :], shift_b[:, :], ALU.add).then_inc(u_ready, 1)

            @block.scalar
            def _(act):
                for s in range(RING):
                    act.sem_inc(x_out[s], 16)
                    act.sem_inc(u_out[s], 16)
                act.sem_inc(logits_ready, RING)

                def split_h(products, loaded, s):
                    act.wait_ge(h_in[s], loaded)
                    if products is not None:
                        act.wait_ge(mm_done, products)
                    act.activation(h_hi[:, s, :, :], h_raw[:, s, :, :], ACT.Copy).then_inc(h_hi_ready, 1)

                split_h(None, 16, 0)
                for k in range(KT):
                    act.wait_ge(w_in[k % WS], 16 * (k // WS + 1))
                    act.activation(w_hi[:, k, :], w_raw[:, k % WS, :], ACT.Copy).then_inc(w_hi_ready, 1)
                    if k == 0:
                        split_h(None, 16, 1)
                act.wait_ge(wr_in, 16)
                act.activation(wr_hi[:, :, :], wr_raw[:, :, :], ACT.Copy).then_inc(w_hi_ready, 1)

                def logits_of(i, s, n):
                    act.wait_ge(r_done, upto(i, s, n))
                    act.activation(logits[:, bass.ds(i * RING + (s + n), 1), :].rearrange("p a e -> p (a e)"),
                                   psum_r[:, s, :], ACT.Copy).then_inc(logits_ready, 1)

                def split_u(i, s, n):
                    act.wait_ge(tr_done, upto(i, s, n))
                    act.activation(u_hi[:, :, :], psum_t[:, :].rearrange("p (k t) -> p k t", k=KT), ACT.Copy).then_inc(u_hi_ready, 1)

                def square(i, s):
                    act.wait_ge(xo_ready, upto(i, s))
                    act.wait_ge(u_out[s], 16 * i + 16)
                    act.activation(u[:, s, :], xo[:, s, :], ACT.Square, accum_out=ssq[:, s:s + 1]).then_inc(ssq_ready, 1)

                def step(i, s, more=True):
                    logits_of(i, s, -RING)
                    split_u(i, s, -1)
                    square(i, s)
                    if more:
                        split_h(upto(i, s), 16 * i + 32, s)

                square(0, 0)
                split_h(1, 32, 0)
                split_u(0, 1, -1)
                square(0, 1)
                split_h(2, 32, 1)
                with act.Fori(1, LAST) as i:
                    for s in range(RING):
                        step(i, s)
                for s in range(RING):
                    step(LAST, s, False)
                logits_of(LAST + 1, 0, -RING)
                split_u(LAST + 1, 0, -1)
                logits_of(LAST + 1, 1, -RING)

            @block.vector
            def _(dve):
                def split_h(n1, s):
                    dve.wait_ge(h_hi_ready, n1)
                    dve.tensor_tensor(h_lo[:, s, :, :], h_raw[:, s, :, :], h_hi[:, s, :, :].bitcast(F32), ALU.subtract).then_inc(h_lo_ready, 1)

                split_h(1, 0)
                for k in range(KT):
                    dve.wait_ge(w_hi_ready, k + 1)
                    dve.tensor_tensor(w_lo[:, k, :], w_raw[:, k % WS, :], w_hi[:, k, :].bitcast(F32), ALU.subtract).then_inc(w_lo_ready, 1)
                    if k == 0:
                        split_h(2, 1)
                dve.wait_ge(mod_in, 64)
                dve.scalar_tensor_tensor(out=scale_b[:, :], in0=scale_b[:, :], scalar=1.0, in1=ng_b[:, :],
                                         op0=ALU.add, op1=ALU.mult).then_inc(mod_ready, 1)
                dve.wait_ge(mod_ready, 1)
                dve.wait_ge(w_hi_ready, KT + 1)
                dve.tensor_tensor(wr_lo[:, :, :], wr_raw[:, :, :], wr_hi[:, :, :].bitcast(F32), ALU.subtract).then_inc(w_lo_ready, 1)

                def residual(i, s):
                    n = upto(i, s)
                    dve.wait_ge(mm_done, n)
                    dve.wait_ge(x_out[s], 16 * i + 16)
                    dve.tensor_tensor(xo[:, s, :], psum_o[:, s, :], gate_b[:, :], ALU.mult).then_inc(gated, 1)
                    dve.wait_ge(gated, n)
                    dve.wait_ge(x_in[s], 16 * i + 16)
                    dve.tensor_tensor(xo[:, s, :], xo[:, s, :], xin[:, s, :], ALU.add).then_inc(xo_ready, 1)

                def split_u(i, s, n):
                    dve.wait_ge(u_hi_ready, upto(i, s, n))
                    dve.tensor_tensor(u_lo[:, :, :], psum_t[:, :].rearrange("p (k t) -> p k t", k=KT), u_hi[:, :, :].bitcast(F32), ALU.subtract).then_inc(u_lo_ready, 1)

                def normalise(i, s):
                    dve.wait_ge(rstd_ready, upto(i, s))
                    dve.scalar_tensor_tensor(out=u[:, s, :], in0=xo[:, s, :], scalar=rstd[:, s:s + 1], in1=scale_b[:, :],
                                             op0=ALU.mult, op1=ALU.mult).then_inc(um_ready, 1)

                residual(0, 0)
                split_h(RING + 1, 0)
                normalise(0, 0)
                residual(0, 1)
                split_u(0, 1, -1)
                split_h(RING + 2, 1)
                normalise(0, 1)

                def step(i, s, more=True):
                    residual(i, s)
                    split_u(i, s, -1)
                    if more:
                        split_h(upto(i, s, RING), s)
                    normalise(i, s)

                with dve.Fori(1, LAST) as i:
                    for s in range(RING):
                        step(i, s)
                for s in range(RING):
                    step(LAST, s, False)
                split_u(LAST + 1, 0, -1)

            @block.tensor
            def _(pe):
                def project(i, s, h, first=False):
                    if h == 0:
                        pe.wait_ge(h_lo_ready, upto(i, s))
                        if not first:
                            pe.wait_ge(gated, upto(i, s, -RING))
                    hs = slice(h * HALF, (h + 1) * HALF)
                    for k in range(KT):
                        if first and s == 0 and h == 0:
                            pe.wait_ge(w_lo_ready, k + 1)
                        last = split_mm(pe, psum_o[:, s, hs], (h_hi[:, s, k, :], h_lo[:, s, k, :]),
                                        (w_hi[:, k, hs], w_lo[:, k, hs]), k == 0, k == KT - 1)
                    if h == 1:
                        last.then_inc(mm_done, 1)

                def transpose_u(i, s, n, slot):
                    pe.wait_ge(u_ready, upto(i, s, n))
                    pe.wait_ge(u_lo_ready, upto(i, s, n - 1))
                    for k in range(KT):
                        last = pe.transpose(psum_t[:, k * P:(k + 1) * P], u[:, slot, k * P:(k + 1) * P], ident[:, :])
                    last.then_inc(tr_done, 1)

                def logit(i, s, n):
                    pe.wait_ge(u_lo_ready, upto(i, s, n))
                    pe.wait_ge(logits_ready, upto(i, s, n))
                    for k in range(KT):
                        last = split_mm(pe, psum_r[:, s, :], (u_hi[:, k, :], u_lo[:, k, :]), (wr_hi[:, k, :], wr_lo[:, k, :]), k == 0, k == KT - 1)
                    last.then_inc(r_done, 1)

                project(0, 0, 0, True)
                project(0, 0, 1, True)
                project(0, 1, 0, True)
                project(0, 1, 1, True)
                pe.wait_ge(w_lo_ready, KT + 1)
                pe.wait_ge(u_ready, 1)
                for k in range(KT):
                    last = pe.transpose(psum_t[:, k * P:(k + 1) * P], u[:, 0, k * P:(k + 1) * P], ident[:, :])
                last.then_inc(tr_done, 1)
                with pe.Fori(1, NT // RING) as i:
                    for s in range(RING):
                        project(i, s, 0)
                        logit(i, s, -RING)
                        project(i, s, 1)
                        transpose_u(i, s, -1, 1 - s)
                logit(LAST + 1, 0, -RING)
                transpose_u(LAST + 1, 0, -1, 1)
                logit(LAST + 1, 1, -RING)


def routing(nc, layer, logits, b_router, pos, pair_w, starts, tok_idx):
    with Phase(nc, f"rt{layer}") as ph:
        brb = ph.sb("brb", [P, E])
        iot = ph.sb("iot", [P, 256], I32)
        tid_i = ph.sb("tid_i", [P, NT], I32)
        tid = ph.sb("tid", [P, NT])
        io128 = ph.sb("io128", [P, P])
        rev = ph.sb("rev", [P, E])
        thr = ph.sb("thr", [P, E])
        reset = ph.sb("reset", [P, E, NT])
        ones = ph.sb("ones", [P, P])
        before = ph.sb("before", [P, P])
        probs = ph.sb("probs", [P, NT, E])
        sel = ph.sb("sel", [P, NT, E])
        work = ph.sb("work", [P, NT, E])
        sums = ph.sb("sums", [P, NT * GROUPS, 2])
        maxs = ph.sb("maxs", [P, NT * GROUPS, 2])
        gs = ph.sb("gs", [P, NT, GROUPS])
        ing = ph.sb("ing", [P, NT, GROUPS])
        col = ph.sb("col", [P, NT])
        rec = ph.sb("rec", [P, NT])
        oh = ph.sb("oh", [P, 2, NT, E])
        mask = ph.sb("mask", [P, NT, E])
        tot = ph.sb("tot", [P, E, NT])
        incl = ph.sb("incl", [P, E, NT])
        gt = ph.sb("gt", [P, E, NT])
        tiles = ph.sb("tiles", [P, E])
        ends = ph.sb("ends", [P, E + 1])
        base = ph.sb("base", [P, E])
        posf = ph.sb("posf", [P, 2, NT])
        slot = ph.sb("slot", [P, NT, E])
        ai = ph.sb("ai", [P, 2, NT], I32)
        af = ph.sb("af", [P, 2, NT])
        bf = ph.sb("bf", [P, 2, NT])
        ob = ph.sb("ob", [P, 2 * NT, P])
        oa = ph.sb("oa", [P, 2 * NT, MAX_TILES])
        ps_rank = ph.ps("ps_rank", [P, NT, E])
        ps_tot = ph.ps("ps_tot", [P, NT, E])
        ps_tab = ph.ps("ps_tab", [P, MAX_TILES])
        br_in = ph.sem("br_in")
        iota_ready = ph.sem("iota_ready")
        step = ph.sem("step")
        centred = ph.sem("centred")
        exp_ready = ph.sem("exp_ready")
        mask_ready = ph.sem("mask_ready")
        counted = ph.sem("counted")
        hot_ready = ph.sem("hot_ready")
        tab_done = ph.sem("tab_done")

        with ph.block() as block:
            @block.sync
            def _(sp):
                sp.dma_start(brb[:, :], b_router.rearrange("(a e) -> a e", a=1).to_broadcast([P, E])).then_inc(br_in, 16)

            @block.gpsimd
            def _(pool):
                pool.iota(iot[:, :], pattern=[[1, 256]], base=0, channel_multiplier=0).then_inc(iota_ready, 1)
                pool.iota(tid_i[:, :], pattern=[[P, NT]], base=0, channel_multiplier=1).then_inc(iota_ready, 1)
                pool.memset(ones[:, :], 1.0).then_inc(iota_ready, 1)
                pool.memset(reset[:, :, :], 1.0).then_inc(iota_ready, 1)
                pool.wait_ge(iota_ready, 4)
                pool.affine_select(out=before[:, :], in_=ones[:, :], compare_op=ALU.is_gt, fill=0.0, base=0,
                                   pattern=[[1, P]], channel_multiplier=-1).then_inc(iota_ready, 1)
                pool.memset(reset[:, :, 0:1], 0.0).then_inc(iota_ready, 1)

            @block.scalar
            def _(act):
                act.wait_ge(centred, 1)
                act.activation(work[:, :, :], work[:, :, :], ACT.Exp).then_inc(exp_ready, 1)

            @block.vector
            def _(dve):
                count = [0]

                def link(ins):
                    count[0] += 1
                    ins.then_inc(step, 1)
                    dve.wait_ge(step, count[0])

                def over_e(x):
                    return x.unsqueeze(2).to_broadcast([P, NT, E])

                dve.wait_ge(iota_ready, 6)
                dve.wait_ge(br_in, 16)
                link(dve.tensor_copy(tid[:, :], tid_i[:, :]))
                link(dve.tensor_copy(io128[:, :], iot[:, 0:P]))
                link(dve.tensor_scalar(rev[:, :], io128[:, 0:E], -1.0, float(E), ALU.mult, ALU.add))
                link(dve.tensor_scalar(thr[:, :], io128[:, 0:E], float(P), None, ALU.mult))
                link(dve.tensor_reduce(col[:, :], logits[:, :, :], AX.X, ALU.max))
                dve.tensor_tensor(work[:, :, :], logits[:, :, :], over_e(col[:, :]), ALU.subtract).then_inc(centred, 1)
                dve.wait_ge(exp_ready, 1)
                link(dve.tensor_reduce(col[:, :], work[:, :, :], AX.X, ALU.add))
                link(dve.reciprocal(rec[:, :], col[:, :]))
                link(dve.tensor_tensor(probs[:, :, :], work[:, :, :], over_e(rec[:, :]), ALU.mult))
                link(dve.tensor_tensor(sel[:, :, :], probs[:, :, :], brb[:, :].unsqueeze(1).to_broadcast([P, NT, E]), ALU.add))
                pair = sel[:, :, :].rearrange("p t (g a b) -> p (t g a) b", g=GROUPS, a=2)
                link(dve.tensor_tensor(sums[:, :, :].rearrange("p g a -> p (g a)"), pair[:, :, 0], pair[:, :, 1], ALU.add))
                link(dve.tensor_tensor(maxs[:, :, :].rearrange("p g a -> p (g a)"), pair[:, :, 0], pair[:, :, 1], ALU.max))
                flat = gs[:, :, :].rearrange("p t g -> p (t g)")
                link(dve.tensor_tensor(flat, maxs[:, :, 0], maxs[:, :, 1], ALU.add))
                link(dve.tensor_tensor(flat, flat, sums[:, :, 0], ALU.max))
                link(dve.tensor_tensor(flat, flat, sums[:, :, 1], ALU.max))

                def first_max(out, x, n):
                    wide = lambda c: c.unsqueeze(2).to_broadcast([P, NT, n])
                    link(dve.tensor_reduce(col[:, :], x, AX.X, ALU.max))
                    link(dve.tensor_tensor(out, x, wide(col[:, :]), ALU.is_equal))
                    link(dve.tensor_tensor(out, out, rev[:, 0:n].unsqueeze(1).to_broadcast([P, NT, n]), ALU.mult))
                    link(dve.tensor_reduce(col[:, :], out, AX.X, ALU.max))
                    link(dve.tensor_tensor(out, out, wide(col[:, :]), ALU.is_equal))

                first_max(ing[:, :, :], gs[:, :, :], GROUPS)
                link(dve.tensor_scalar(ing[:, :, :], ing[:, :, :], 1.0, BIG, ALU.subtract, ALU.mult))
                link(dve.tensor_tensor(sel[:, :, :].rearrange("p t (g a) -> p (t g) a", g=GROUPS), sel[:, :, :].rearrange("p t (g a) -> p (t g) a", g=GROUPS),
                                       ing[:, :, :].rearrange("p t g -> p (t g)").unsqueeze(2).to_broadcast([P, NT * GROUPS, PER_G]), ALU.add))
                first_max(oh[:, 0, :, :], sel[:, :, :], E)
                link(dve.scalar_tensor_tensor(out=sel[:, :, :], in0=oh[:, 0, :, :], scalar=-4.0 * BIG, in1=sel[:, :, :], op0=ALU.mult, op1=ALU.add))
                first_max(oh[:, 1, :, :], sel[:, :, :], E)
                dve.tensor_tensor(mask[:, :, :], oh[:, 0, :, :], oh[:, 1, :, :], ALU.add).then_inc(mask_ready, 1)
                for j in range(2):
                    link(dve.tensor_tensor(work[:, :, :], probs[:, :, :], oh[:, j, :, :], ALU.mult))
                    link(dve.tensor_reduce(pair_w[:, j, :], work[:, :, :], AX.X, ALU.add))
                link(dve.tensor_tensor(col[:, :], pair_w[:, 0, :], pair_w[:, 1, :], ALU.add))
                link(dve.reciprocal(rec[:, :], col[:, :]))
                for j in range(2):
                    link(dve.tensor_tensor(pair_w[:, j, :], pair_w[:, j, :], rec[:, :], ALU.mult))
                dve.wait_ge(counted, 1)
                link(dve.tensor_copy(tot[:, :, :], ps_tot[:, :, :].rearrange("p t e -> p e t")))
                et = lambda x: x[:, :, :].rearrange("p e t -> p (e t)")
                link(dve.tensor_tensor_scan(et(incl), et(reset), et(tot), 0.0, ALU.mult, ALU.add))
                link(dve.tensor_tensor(tot[:, :, :], incl[:, :, :], tot[:, :, :], ALU.subtract))
                link(dve.tensor_tensor(gt[:, :, :], incl[:, :, NT - 1:NT].to_broadcast([P, E, NT]), thr[:, :].unsqueeze(1).to_broadcast([P, E, NT]), ALU.is_gt))
                link(dve.tensor_reduce(tiles[:, :], gt[:, :, :], AX.X, ALU.add))
                link(dve.tensor_scalar(tiles[:, :], tiles[:, :], 1.0, None, ALU.max))
                link(dve.memset(ends[:, 0:1], 0.0))
                link(dve.tensor_tensor_scan(ends[:, 1:E + 1], ones[:, 0:E], tiles[:, :], 0.0, ALU.mult, ALU.add))
                link(dve.tensor_copy(starts[0:1, :], ends[0:1, :]))
                link(dve.tensor_scalar(base[:, :], ends[:, 0:E], float(P), None, ALU.mult))
                link(dve.tensor_tensor(slot[:, :, :], ps_rank[:, :, :], tot[:, :, :].rearrange("p e t -> p t e"), ALU.add))
                link(dve.tensor_tensor(slot[:, :, :], slot[:, :, :], base[:, :].unsqueeze(1).to_broadcast([P, NT, E]), ALU.add))
                for j in range(2):
                    link(dve.tensor_tensor(work[:, :, :], slot[:, :, :], oh[:, j, :, :], ALU.mult))
                    link(dve.tensor_reduce(posf[:, j, :], work[:, :, :], AX.X, ALU.add))
                link(dve.tensor_copy(ai[:, :, :], posf[:, :, :]))
                link(dve.tensor_scalar(ai[:, :, :], ai[:, :, :], 7, None, ALU.arith_shift_right))
                link(dve.tensor_copy(af[:, :, :], ai[:, :, :]))
                link(dve.scalar_tensor_tensor(out=bf[:, :, :], in0=af[:, :, :], scalar=-float(P), in1=posf[:, :, :], op0=ALU.mult, op1=ALU.add))
                link(dve.tensor_scalar(pos[:, :, :], posf[:, :, :], float(P), None, ALU.add))
                pairs = lambda x: x[:, :, :].rearrange("p j t -> p (j t)").unsqueeze(2)
                link(dve.tensor_tensor(ob[:, :, :], io128[:, :].unsqueeze(1).to_broadcast([P, 2 * NT, P]), pairs(bf).to_broadcast([P, 2 * NT, P]), ALU.is_equal))
                link(dve.tensor_tensor(oa[:, :, :], io128[:, 0:MAX_TILES].unsqueeze(1).to_broadcast([P, 2 * NT, MAX_TILES]),
                                       pairs(af).to_broadcast([P, 2 * NT, MAX_TILES]), ALU.is_equal))
                for j in range(2):
                    link(dve.tensor_tensor(oa[:, j * NT:(j + 1) * NT, :], oa[:, j * NT:(j + 1) * NT, :], tid[:, :].unsqueeze(2).to_broadcast([P, NT, MAX_TILES]), ALU.mult))
                dve.sem_inc(hot_ready, 1)
                dve.wait_ge(tab_done, 1)
                dve.tensor_copy(tok_idx[:, :], ps_tab[:, :])

            @block.tensor
            def _(pe):
                pe.wait_ge(iota_ready, 6)
                pe.wait_ge(mask_ready, 1)
                flat = mask[:, :, :].rearrange("p t e -> p (t e)")
                pe.matmul(ps_rank[:, :, :].rearrange("p t e -> p (t e)"), before[:, :], flat, start=True, stop=True)
                pe.matmul(ps_tot[:, :, :].rearrange("p t e -> p (t e)"), ones[:, :], flat, start=True, stop=True).then_inc(counted, 1)
                pe.wait_ge(hot_ready, 1)
                for m in range(2 * NT):
                    last = pe.matmul(ps_tab[:, :], ob[:, m, :], oa[:, m, :], start=(m == 0), stop=(m == 2 * NT - 1))
                last.then_inc(tab_done, 1)


def experts(nc, layer, u_src, w_gate, w_up, w_down, gate_row, starts, tok_idx, ys, ident):
    WG = 4
    WD = 4
    NCH = 2 * WG + WD
    RAW = NCH
    AH = DE // 2
    with Phase(nc, f"ex{layer}") as ph:
        w_raw = ph.sb("w_raw", [P, RAW, D])
        w_hi = ph.sb("w_hi", [P, NCH, D], F32R)
        w_lo = ph.sb("w_lo", [P, NCH, D], F32R)
        idx = ph.sb("idx", [P, 1], I32)
        rows = ph.sb("rows", [P, D])
        u_hi = ph.sb("u_hi", [P, KT, P], F32R)
        u_lo = ph.sb("u_lo", [P, KT, P], F32R)
        sig = ph.sb("sig", [P, DE])
        a = ph.sb("a", [P, DE])
        a_hi = ph.sb("a_hi", [P, FT, P], F32R)
        a_lo = ph.sb("a_lo", [P, FT, P], F32R)
        out = ph.sb("out", [P, D])
        gate_b = ph.sb("gate_b", [P, D])
        ps_u = ph.ps("ps_u", [P, D])
        ps_g = ph.ps("ps_g", [P, DE])
        ps_up = ph.ps("ps_up", [P, 2, HALF])
        ps_a1 = ph.ps("ps_a1", [P, HALF])
        ps_a = (ps_g, ps_a1)
        ps_o = ph.ps("ps_o", [P, D])
        raw_in = [ph.sem(f"raw_in{s}") for s in range(RAW)]
        whi_ready = ph.sem("whi_ready")
        wlo_ready = ph.sem("wlo_ready")
        idx_ready = ph.sem("idx_ready")
        rows_in = ph.sem("rows_in")
        passed = ph.sem("passed")
        tr_done = ph.sem("tr_done")
        uhi_ready = ph.sem("uhi_ready")
        ulo_ready = ph.sem("ulo_ready")
        gate_done = ph.sem("gate_done")
        up_done = ph.sem("up_done")
        sig_ready = ph.sem("sig_ready")
        gated = ph.sem("gated")
        a_ready = ph.sem("a_ready")
        at_done = ph.sem("at_done")
        ahi_ready = ph.sem("ahi_ready")
        alo_ready = ph.sem("alo_ready")
        down_done = ph.sem("down_done")
        out_ready = ph.sem("out_ready")
        out_gated = ph.sem("out_gated")
        out_free = ph.sem("out_free")
        gate_in = ph.sem("gate_in")
        out_done = ph.sem("out_done")

        def bounds(eng, e):
            return (eng.value_load(starts[0:1, bass.ds(e, 1)], min_val=0, max_val=MAX_TILES - 2),
                    eng.value_load(starts[0:1, bass.ds(e + 1, 1)], min_val=1, max_val=MAX_TILES - 1))

        def walk(eng, before, tile):
            with eng.Fori(0, E) as e:
                first, end = bounds(eng, e)
                before(e)
                tile(e, first, True)
                with eng.If(first + 1 < end):
                    with eng.Fori(first + 1, end) as t:
                        tile(e, t, False)

        with ph.block() as block:
            @block.sync
            def _(sp):
                def load(e, c, first):
                    if c < 2 * WG:
                        w = w_gate if c < WG else w_up
                        k = 2 * (c % WG)
                        src = w[layer, bass.ds(e, 1), k * P:(k + 2) * P, :].rearrange("a (k p) n -> p (a k) n", p=P)
                        dst = w_raw[:, c % RAW, :].rearrange("p (k n) -> p k n", k=2)
                    else:
                        f = c - 2 * WG
                        src = w_down[layer, bass.ds(e, 1), f * P:(f + 1) * P, :].rearrange("a p n -> p (a n)")
                        dst = w_raw[:, c % RAW, :]
                    if not first:
                        sp.wait_ge(wlo_ready, e * NCH + (c - RAW + 1))
                    sp.dma_start(dst, src).then_inc(raw_in[c % RAW], 16)

                for c in range(NCH):
                    load(0, c, c < RAW)
                    if c == 1:
                        sp.wait_ge(tr_done, 1)
                        sp.dma_start(gate_b[:, :], rowcast(gate_row)).then_inc(gate_in, 16)
                with sp.Fori(1, E) as e:
                    for c in range(NCH):
                        load(e, c, False)

            @block.gpsimd
            def _(pool):
                pool.memset(out[:, :], 0.0).then_inc(idx_ready, 1)

                def fetch(t):
                    pool.tensor_copy(idx[:, :], tok_idx[:, bass.ds(t, 1)]).then_inc(idx_ready, 1)
                    pool.wait_ge(idx_ready, t + 2)
                    stand(pool, passed)
                    pool.indirect_dma_start(rows[:, :], None, u_src, bass.IndirectOffsetOnAxis(ap=idx[:, 0:1], axis=0)).then_inc(rows_in, 16)

                def store(t):
                    pool.wait_ge(out_ready, t + 1)
                    stand(pool, passed)
                    pool.tensor_tensor(out[:, :], out[:, :], gate_b[:, :], ALU.mult).then_inc(out_gated, 1)
                    pool.wait_ge(out_gated, t + 1)
                    stand(pool, passed)
                    pool.dma_start(ys[bass.ds(t * P, P), :], out[:, :]).then_inc(out_done, 16)

                def fetched(t):
                    pool.wait_ge(rows_in, t * 16 + 16)
                    pool.wait_ge(tr_done, t + 1)
                    stand(pool, passed)

                def tile(e, t, first):
                    fetch(t + 1)
                    store(t)
                    fetched(t + 1)
                    pool.wait_ge(out_done, t * 16 + 16)
                    pool.sem_inc(out_free, 1)

                pool.sem_inc(out_free, 1)
                fetch(0)
                fetched(0)
                pool.wait_ge(gate_in, 16)
                walk(pool, lambda e: None, tile)
                end = pool.value_load(starts[0:1, E:E + 1], min_val=1, max_val=MAX_TILES - 1)
                store(end)
                pool.wait_ge(out_done, end * 16 + 16)
                stand(pool, passed)

            @block.scalar
            def _(act):

                def split_w(e, c):
                    act.wait_ge(raw_in[c % RAW], e * (16 * NCH // RAW) + 16 * (c // RAW + 1))
                    act.activation(w_hi[:, c, :], w_raw[:, c % RAW, :], ACT.Copy).then_inc(whi_ready, 1)

                def split_u(t):
                    act.wait_ge(tr_done, t + 1)
                    act.activation(u_hi[:, :, :].rearrange("p k t -> p (k t)"), ps_u[:, :], ACT.Copy).then_inc(uhi_ready, 1)

                def take(t):
                    act.wait_ge(down_done, t + 1)
                    act.wait_ge(out_free, t + 1)
                    act.activation(out[:, :], ps_o[:, :], ACT.Copy).then_inc(out_ready, 1)

                def tile(e, t, first):
                    take(t)
                    act.wait_ge(gate_done, t + 1)
                    act.activation(sig[:, :], ps_g[:, :], ACT.Sigmoid).then_inc(sig_ready, 1)
                    if first:
                        for c in range(2 * WG, NCH):
                            split_w(e, c)
                    for h in range(2):
                        act.wait_ge(at_done, t * 2 + (h + 1))
                        act.activation(a_hi[:, 2 * h:2 * h + 2, :].rearrange("p f t -> p (f t)"), ps_a[h][:, 0:AH], ACT.Copy).then_inc(ahi_ready, 1)
                    split_u(t + 1)

                def before(e):
                    for c in range(2 * WG):
                        split_w(e, c)

                split_u(0)
                walk(act, before, tile)
                end = act.value_load(starts[0:1, E:E + 1], min_val=1, max_val=MAX_TILES - 1)
                take(end)

            @block.vector
            def _(dve):
                def split_w(e, c):
                    dve.wait_ge(whi_ready, e * NCH + (c + 1))
                    dve.tensor_tensor(w_lo[:, c, :], w_raw[:, c % RAW, :], w_hi[:, c, :].bitcast(F32), ALU.subtract).then_inc(wlo_ready, 1)

                def split_u(t):
                    dve.wait_ge(uhi_ready, t + 1)
                    dve.tensor_tensor(u_lo[:, :, :].rearrange("p k t -> p (k t)"), ps_u[:, :], u_hi[:, :, :].rearrange("p k t -> p (k t)").bitcast(F32),
                                      ALU.subtract).then_inc(ulo_ready, 1)

                def tile(e, t, first):
                    dve.wait_ge(sig_ready, t + 1)
                    dve.tensor_tensor(sig[:, :], sig[:, :], ps_g[:, :], ALU.mult).then_inc(gated, 1)
                    dve.wait_ge(gated, t + 1)

                    def multiply(h):
                        hs = slice(AH * h, AH * (h + 1))
                        dve.wait_ge(up_done, t * 2 + (h + 1))
                        dve.tensor_tensor(a[:, hs], sig[:, hs], ps_up[:, h, 0:AH], ALU.mult).then_inc(a_ready, 1)

                    def split_a(h):
                        dve.wait_ge(ahi_ready, t * 2 + (h + 1))
                        dve.tensor_tensor(a_lo[:, 2 * h:2 * h + 2, :].rearrange("p f t -> p (f t)"), ps_a[h][:, 0:AH],
                                          a_hi[:, 2 * h:2 * h + 2, :].rearrange("p f t -> p (f t)").bitcast(F32), ALU.subtract).then_inc(alo_ready, 1)

                    multiply(0)
                    if first:
                        split_w(e, 2 * WG)
                        split_w(e, 2 * WG + 1)
                    multiply(1)
                    split_a(0)
                    if first:
                        split_w(e, 2 * WG + 2)
                    split_a(1)
                    if first:
                        split_w(e, 2 * WG + 3)
                    split_u(t + 1)

                def before(e):
                    for c in range(2 * WG):
                        split_w(e, c)

                split_u(0)
                walk(dve, before, tile)

            @block.tensor
            def _(pe):
                def transpose_rows(t):
                    pe.wait_ge(rows_in, t * 16 + 16)
                    for k in range(KT):
                        last = pe.transpose(ps_u[:, k * P:(k + 1) * P], rows[:, k * P:(k + 1) * P], ident[:, :])
                    last.then_inc(tr_done, 1)

                def up_or_gate(e, which, dst, at, n):
                    for k in range(KT):
                        c = which * WG + k // 2
                        if k % 2 == 0 and at == 0:
                            pe.wait_ge(wlo_ready, e * NCH + (c + 1))
                        ws = slice((k % 2) * DE + at, (k % 2) * DE + at + n)
                        last = split_mm(pe, dst[:, 0:n], (u_hi[:, k, :], u_lo[:, k, :]), (w_hi[:, c, ws], w_lo[:, c, ws]), k == 0, k == KT - 1)
                    return last

                def transpose_a(t, h):
                    pe.wait_ge(a_ready, t * 2 + (h + 1))
                    for f in range(2 * h, 2 * h + 2):
                        last = pe.transpose(ps_a[h][:, (f % 2) * P:(f % 2 + 1) * P], a[:, f * P:(f + 1) * P], ident[:, :])
                    last.then_inc(at_done, 1)

                def down(e, t, h):
                    pe.wait_ge(alo_ready, t * 2 + (h + 1))
                    for o in range(2):
                        os = slice(o * HALF, (o + 1) * HALF)
                        for f in range(2 * h, 2 * h + 2):
                            c = 2 * WG + f
                            if o == 0:
                                pe.wait_ge(wlo_ready, e * NCH + (c + 1))
                            last = split_mm(pe, ps_o[:, os], (a_hi[:, f, :], a_lo[:, f, :]), (w_hi[:, c, os], w_lo[:, c, os]), f == 0, f == FT - 1)
                    return last

                def tile(e, t):
                    pe.wait_ge(ulo_ready, t + 1)
                    up_or_gate(e, 0, ps_g, 0, DE).then_inc(gate_done, 1)
                    for h in range(2):
                        up_or_gate(e, 1, ps_up[:, h, :], h * AH, AH).then_inc(up_done, 1)
                    transpose_a(t, 0)
                    transpose_rows(t + 1)
                    transpose_a(t, 1)
                    pe.wait_ge(out_ready, t + 1)
                    down(e, t, 0)
                    down(e, t, 1).then_inc(down_done, 1)

                pe.wait_ge(idx_ready, 1)
                for h in range(2):
                    last = pe.matmul(ps_o[:, h * HALF:(h + 1) * HALF], ident[:, :], out[:, h * HALF:(h + 1) * HALF], start=True, stop=True)
                last.then_inc(down_done, 1)
                transpose_rows(0)
                walk(pe, lambda e: None, lambda e, t, first: tile(e, t))


def final(nc, x_src, ys, pos, pair_w, final_g, out):
    with Phase(nc, "fin") as ph:
        xin = ph.sb("xin", [P, RING, D])
        xr = ph.sb("xr", [P, RING, D])
        row_a = ph.sb("row_a", [P, RING, D])
        row_b = ph.sb("row_b", [P, RING, D])
        yo = ph.sb("yo", [P, RING, D])
        fg_b = ph.sb("fg_b", [P, D])
        ssq = ph.sb("ssq", [P, RING])
        rstd = ph.sb("rstd", [P, RING])
        mhalf = ph.sb("mhalf", [P, 1])
        junk = ph.sb("junk", [P, D])
        idx = ph.sb("idx", [P, RING, 2], I32)
        wts = ph.sb("wts", [P, RING, 2])
        vec_in = ph.sem("vec_in")
        const_ready = ph.sem("const_ready")
        x_in = [ph.sem(f"x_in{s}") for s in range(RING)]
        rows_in = [ph.sem(f"rows_in{s}") for s in range(RING)]
        idx_ready = ph.sem("idx_ready")
        wts_ready = ph.sem("wts_ready")
        ra_added = ph.sem("ra_added")
        x2_ready = ph.sem("x2_ready")
        ssq_ready = ph.sem("ssq_ready")
        var_ready = ph.sem("var_ready")
        rstd_ready = ph.sem("rstd_ready")
        passed = ph.sem("passed")
        y_ready = ph.sem("y_ready")
        y_out = [ph.sem(f"y_out{s}") for s in range(RING)]
        UM = -1

        with ph.block() as block:
            @block.sync
            def _(sp):
                def load(n, s):
                    sp.dma_start(xin[:, s, :], x_src[bass.ds(n * P, P), :]).then_inc(x_in[s], 16)

                def step(i, s):
                    if live(i, s, RING):
                        sp.wait_ge(ra_added, upto(i, s))
                        load(i * RING + (s + RING), s)
                    if live(i, s, UM):
                        q = slot(s, UM)
                        sp.wait_ge(y_ready, upto(i, s, UM))
                        sp.dma_start(out[0, bass.ds((i * RING + (s + UM)) * P, P), :], yo[:, q, :]).then_inc(y_out[q], 16)

                for s in range(RING):
                    load(s, s)
                sp.dma_start(fg_b[:, :], final_g.rearrange("(a d) -> a d", a=1).to_broadcast([P, D])).then_inc(vec_in, 16)
                skewed(sp, step)
                for s in range(RING):
                    sp.wait_ge(y_out[s], 16 * (NT // RING + 1))

            @block.gpsimd
            def _(pool):
                pool.memset(mhalf[:, :], -0.5).then_inc(const_ready, 1)
                pool.wait_ge(const_ready, 1)

                def gather(n, s, count):
                    pool.tensor_copy(idx[:, s, :], pos[:, :, bass.ds(n, 1)].rearrange("p j a -> p (j a)")).then_inc(idx_ready, 1)
                    pool.wait_ge(idx_ready, count)
                    stand(pool, passed)
                    for j, dst in enumerate((row_a, row_b)):
                        pool.indirect_dma_start(dst[:, s, :], None, ys, bass.IndirectOffsetOnAxis(ap=idx[:, s, j:j + 1], axis=0)).then_inc(rows_in[s], 16)

                def step(i, s):
                    if live(i, s, RING):
                        pool.wait_ge(x2_ready, upto(i, s))
                        gather(i * RING + (s + RING), s, upto(i, s, RING))
                    if live(i, s):
                        pool.wait_ge(ssq_ready, upto(i, s, 1))
                        stand(pool, passed)
                        pool.tensor_scalar(rstd[:, s:s + 1], ssq[:, s:s + 1], 1.0 / D, EPS, ALU.mult, ALU.add).then_inc(var_ready, 1)
                        pool.wait_ge(var_ready, upto(i, s))
                        pool.tensor_tensor(rstd[:, s:s + 1], rstd[:, s:s + 1], mhalf[:, 0:1], ALU.pow).then_inc(rstd_ready, 1)

                for s in range(RING):
                    gather(s, s, s + 1)
                skewed(pool, step)

            @block.scalar
            def _(act):
                for s in range(RING):
                    act.sem_inc(y_out[s], 16)
                act.sem_inc(ssq_ready, 1)

                def step(i, s):
                    if live(i, s):
                        act.wait_ge(x2_ready, upto(i, s))
                        act.wait_ge(ssq_ready, upto(i, s))
                        act.activation(junk[:, :], xr[:, s, :], ACT.Square, accum_out=ssq[:, s:s + 1]).then_inc(ssq_ready, 1)

                skewed(act, step)

            @block.vector
            def _(dve):
                def weights(i, s, n):
                    dve.tensor_copy(wts[:, slot(s, n), :], pair_w[:, :, bass.ds(i * RING + (s + n), 1)].rearrange("p j a -> p (j a)")).then_inc(wts_ready, 1)

                def step(i, s):
                    if live(i, s):
                        dve.wait_ge(x_in[s], 16 * uses(i, s))
                        dve.wait_ge(rows_in[s], 32 * uses(i, s))
                        dve.wait_ge(wts_ready, upto(i, s))
                        dve.scalar_tensor_tensor(out=row_a[:, s, :], in0=row_a[:, s, :], scalar=wts[:, s, 0:1], in1=xin[:, s, :],
                                                 op0=ALU.mult, op1=ALU.add).then_inc(ra_added, 1)
                        if live(i, s, 1):
                            if live(i, s, -1):
                                dve.wait_ge(x2_ready, upto(i, s, -1))
                            weights(i, s, 1)
                        dve.wait_ge(ra_added, upto(i, s))
                        dve.scalar_tensor_tensor(out=xr[:, s, :], in0=row_b[:, s, :], scalar=wts[:, s, 1:2], in1=row_a[:, s, :],
                                                 op0=ALU.mult, op1=ALU.add).then_inc(x2_ready, 1)
                    if live(i, s, UM):
                        q = slot(s, UM)
                        dve.wait_ge(rstd_ready, upto(i, s, UM))
                        dve.wait_ge(x2_ready, upto(i, s, UM))
                        dve.wait_ge(y_out[q], 16 * uses(i, s, UM))
                        dve.scalar_tensor_tensor(out=yo[:, q, :], in0=xr[:, q, :], scalar=rstd[:, q:q + 1], in1=fg_b[:, :],
                                                 op0=ALU.mult, op1=ALU.mult).then_inc(y_ready, 1)

                weights(0, 0, 0)
                dve.wait_ge(vec_in, 16)
                skewed(dve, step)


def trunk(nc, x, c, norm1_g, norm2_g, w_ada, b_ada, m_w_in, m_b_gates, m_norm_g, m_w_out,
          c_w_in, c_conv_w, c_conv_b, c_w_out, w_router, b_router, e_w_gate, e_w_up, e_w_down, final_g, out):
    dram = lambda name, shape: nc.dram_tensor(name, shape, F32, kind="Internal").ap()
    mod_rows = dram("mod_rows", (MOD_ROWS, D))
    x1 = dram("x1", (T, D))
    x2 = dram("x2", (T, D))
    u2 = dram("u2", (T, D))
    ys = dram("ys", (MAX_TILES * P, D))
    proj_t = dram("proj_t", (NCOL, T))
    gates_t = dram("gates_t", (2 * HEADS, T))
    h_t = dram("h_t", (D, T))
    gate_d = (dram("ends_d", (HEADS * NT, 2)), dram("seq_d", (HEADS * NT, 1)), dram("rows_d", (HEADS * NT, 2 * P)), dram("decay_d", (HEADS * NT, 1)))

    with ExitStack() as ctx:
        sb = lambda name, shape, dt=F32: ctx.enter_context(nc.sbuf_tensor(name, shape, dt))
        ident = sb("ident", [P, P])
        logits = sb("logits", [P, NT, E])
        pos = sb("pos", [P, 2, NT], I32)
        pair_w = sb("pair_w", [P, 2, NT])
        starts = sb("starts", [1, E + 1], I32)
        tok_idx = sb("tok_idx", [P, MAX_TILES], I32)

        cond = sb("cond", [P, KT])
        ones = sb("ones", [P, 1])

        adaln(nc, c, w_ada, b_ada, mod_rows, cond, ones, ident)
        for layer in range(2):
            if layer == 0:
                in_proj(nc, 0, x[0, :, :], None, norm1_g, mod_rows, m_w_in[0, :, :], proj_t, ident, gates=(m_b_gates, gates_t), blank=ys,
                        ada=(w_ada, b_ada, cond, ones))
                mlstm(nc, proj_t, gates_t, gate_d, m_norm_g, h_t, ident)
                out_proj(nc, 0, h_t, m_w_out[0, :, :], x[0, :, :], x1, u2, norm2_g, mod_rows, w_router, logits, ident)
            else:
                in_proj(nc, 1, x1, x2, norm1_g, mod_rows, c_w_in[0, :, :], h_t, ident,
                        combine=(ys, pos, pair_w), conv=(c_conv_w, c_conv_b))
                out_proj(nc, 1, h_t, c_w_out[0, :, :], x2, x1, u2, norm2_g, mod_rows, w_router, logits, ident)
            routing(nc, layer, logits, b_router, pos, pair_w, starts, tok_idx)
            gate_row = MOD_L * (layer + 1) - 1
            experts(nc, layer, u2, e_w_gate, e_w_up, e_w_down, mod_rows[gate_row:gate_row + 1, :], starts, tok_idx, ys, ident)
        final(nc, x1, ys, pos, pair_w, final_g, out)


_INS = ["x", "c", "norm1_g", "norm2_g", "w_ada", "b_ada", "m_w_in", "m_b_gates", "m_norm_g", "m_w_out",
        "c_w_in", "c_conv_w", "c_conv_b", "c_w_out", "w_router", "b_router", "e_w_gate", "e_w_up", "e_w_down", "final_g"]


def kernel(**inputs):
    import numpy as _np
    import concourse.bacc as _bacc
    from concourse.bass_utils import run_bass_kernel_spmd as _run

    nc = _bacc.Bacc("TRN2", target_bir_lowering=False, num_devices=1)
    arrays, args = {}, []
    for name in _INS:
        a = _np.ascontiguousarray(inputs[name])
        arrays[f"in_{name}_dram"] = a
        args.append(nc.dram_tensor(f"in_{name}_dram", a.shape, mybir.dt.from_np(a.dtype), kind="ExternalInput").ap())
    args.append(nc.dram_tensor("out_0_dram", (1, T, D), F32, kind="ExternalOutput").ap())
    trunk(nc, *args)
    r = _run(nc, [arrays], core_ids=[0])
    return r.results[0]["out_0_dram"]
```
